# Optimizing a Trainium2 kernel written in Bass

```python
import math
import jax, jax.numpy as jnp
from jax import lax
import numpy as np

D_MODEL = 2048
BATCH = 1
SEQ = 256
DEPTH = 1

HEAD_DIM = 128
D_MIX = D_MODEL
GLA_HEADS = D_MIX // 2 // HEAD_DIM
GLA_DK = HEAD_DIM // 2
GLA_DV = HEAD_DIM
GLA_RANK = 16
GLA_TAU = 16.0
GLA_CHUNK = 64
FOX_HEADS = D_MIX // 4 // HEAD_DIM
FOX_BLOCK = 128
MEM_HEADS = 4
MEM_TOKENS = 256
N_OUT_HEADS = GLA_HEADS + FOX_HEADS + MEM_HEADS
D_FF = 4 * D_MODEL
EPS = 1e-6


def _in_widths():
    return (
        GLA_HEADS * GLA_DK,
        GLA_HEADS * GLA_DK,
        GLA_HEADS * GLA_DV,
        GLA_HEADS * GLA_DV,
        GLA_RANK,
        FOX_HEADS * HEAD_DIM,
        FOX_HEADS * HEAD_DIM,
        FOX_HEADS * HEAD_DIM,
        FOX_HEADS * HEAD_DIM,
        FOX_HEADS,
        MEM_HEADS * HEAD_DIM,
        MEM_HEADS * HEAD_DIM,
    )

def _split_points():
    pts, acc = [], 0
    for w in _in_widths()[:-1]:
        acc += w
        pts.append(acc)
    return pts

def rms_norm(x, g):
    xf = x.astype(jnp.float32)
    y = xf * lax.rsqrt(jnp.mean(xf * xf, axis=-1, keepdims=True) + EPS)
    return (y * g.astype(jnp.float32)).astype(x.dtype)

def _heads(t, h):
    return t.reshape(t.shape[0], t.shape[1], h, -1).transpose(0, 2, 1, 3)

def gla_chunked(q, k, v, log_a):
    B, H, S, DK = q.shape
    DV = v.shape[-1]
    C = GLA_CHUNK
    n = S // C

    def to_chunks(t):
        return t.reshape(B, H, n, C, t.shape[-1]).transpose(2, 0, 1, 3, 4)

    qc = to_chunks(q * (DK ** -0.5))
    kc, vc, gc = to_chunks(k), to_chunks(v), to_chunks(log_a)
    causal = jnp.tril(jnp.ones((C, C), dtype=bool))[:, :, None]

    def step(state, xs):
        qi, ki, vi, gi = xs
        b = jnp.cumsum(gi.astype(jnp.float32), axis=2)
        inter = jnp.einsum('bhck,bhkv->bhcv', qi * jnp.exp(b), state)
        rel = b[:, :, :, None, :] - b[:, :, None, :, :]
        decay = jnp.exp(jnp.where(causal, rel, -jnp.inf))
        scores = jnp.einsum('bhik,bhijk,bhjk->bhij', qi.astype(jnp.float32), decay,
                            ki.astype(jnp.float32))
        intra = jnp.einsum('bhij,bhjv->bhiv', scores, vi.astype(jnp.float32))
        b_last = b[:, :, -1:, :]
        new_state = (jnp.exp(b_last[:, :, 0, :])[..., None] * state
                     + jnp.einsum('bhck,bhcv->bhkv', ki * jnp.exp(b_last - b),
                                  vi.astype(jnp.float32)))
        return new_state, inter + intra

    state0 = jnp.zeros((B, H, DK, DV), jnp.float32)
    _, out = lax.scan(step, state0, (qc, kc, vc, gc))
    return out.transpose(1, 2, 0, 3, 4).reshape(B, H, S, DV)

def forgetting_attention(q, k, v, log_f):
    B, H, S, D = q.shape
    scale = D ** -0.5
    c = jnp.cumsum(log_f.astype(jnp.float32), axis=-1)
    outs = []
    for i in range(S // FOX_BLOCK):
        q0, q1 = i * FOX_BLOCK, (i + 1) * FOX_BLOCK
        qb, kb, vb = q[:, :, q0:q1], k[:, :, :q1], v[:, :, :q1]
        logits = (jnp.einsum('bhqd,bhkd->bhqk', qb, kb).astype(jnp.float32) * scale
                  + c[:, :, q0:q1, None] - c[:, :, None, :q1])
        mask = (q0 + jnp.arange(FOX_BLOCK))[:, None] >= jnp.arange(q1)[None, :]
        p = jax.nn.softmax(jnp.where(mask, logits, -jnp.inf), axis=-1)
        outs.append(jnp.einsum('bhqk,bhkd->bhqd', p.astype(v.dtype), vb))
    return jnp.concatenate(outs, axis=2)

def first_inputs(seed: int = 0) -> dict:
    key = jax.random.key(seed)
    ks = jax.random.split(key, 20)
    n = jax.random.normal
    d_in = sum(_in_widths())
    return {
        "x": n(ks[0], (BATCH, SEQ, D_MODEL), jnp.float32),
        "mem": n(ks[1], (BATCH, MEM_TOKENS, D_MODEL), jnp.float32),
        "attn_norm_g": 1.0 + 0.02 * n(ks[2], (D_MODEL,), jnp.float32),
        "w_in": n(ks[3], (D_MODEL, d_in), jnp.float32) * D_MODEL ** -0.5,
        "gla_a_w2": n(ks[4], (GLA_RANK, GLA_HEADS * GLA_DK), jnp.float32) * GLA_RANK ** -0.5,
        "gla_a_b": 0.5 * n(ks[5], (GLA_HEADS * GLA_DK,), jnp.float32),
        "fox_f_b": 3.0 + 0.5 * n(ks[6], (FOX_HEADS,), jnp.float32),
        "fox_q_norm_g": 1.0 + 0.02 * n(ks[7], (HEAD_DIM,), jnp.float32),
        "fox_k_norm_g": 1.0 + 0.02 * n(ks[8], (HEAD_DIM,), jnp.float32),
        "mem_norm_g": 1.0 + 0.02 * n(ks[9], (D_MODEL,), jnp.float32),
        "w_mem_kv": n(ks[10], (D_MODEL, 2 * MEM_HEADS * HEAD_DIM), jnp.float32) * D_MODEL ** -0.5,
        "mem_q_norm_g": 1.0 + 0.02 * n(ks[11], (HEAD_DIM,), jnp.float32),
        "mem_k_norm_g": 1.0 + 0.02 * n(ks[12], (HEAD_DIM,), jnp.float32),
        "out_norm_g": 1.0 + 0.02 * n(ks[13], (N_OUT_HEADS * HEAD_DIM,), jnp.float32),
        "w_out": n(ks[14], (N_OUT_HEADS * HEAD_DIM, D_MODEL), jnp.float32) * (N_OUT_HEADS * HEAD_DIM) ** -0.5,
        "mlp_norm_g": 1.0 + 0.02 * n(ks[15], (D_MODEL,), jnp.float32),
        "w_up": n(ks[16], (D_MODEL, D_FF), jnp.float32) * D_MODEL ** -0.5,
        "w_down": n(ks[17], (D_FF, D_MODEL), jnp.float32) * D_FF ** -0.5,
    }

def first_block(x, mem, attn_norm_g, w_in, gla_a_w2, gla_a_b, fox_f_b, fox_q_norm_g,
              fox_k_norm_g, mem_norm_g, w_mem_kv, mem_q_norm_g, mem_k_norm_g,
              out_norm_g, w_out, mlp_norm_g, w_up, w_down):
    B, S, _ = x.shape
    h = x
    for _layer in range(DEPTH):
        xn = rms_norm(h, attn_norm_g)
        proj = xn @ w_in
        (gq, gk, gv, gg, ga, fq, fk, fv, fg, ff, mq, mg) = jnp.split(proj, _split_points(), axis=-1)

        log_a = jax.nn.log_sigmoid((ga @ gla_a_w2 + gla_a_b).astype(jnp.float32)) / GLA_TAU
        gla_o = gla_chunked(_heads(gq, GLA_HEADS), _heads(gk, GLA_HEADS),
                            _heads(gv, GLA_HEADS), _heads(log_a, GLA_HEADS))
        gla_o = gla_o.astype(x.dtype).transpose(0, 2, 1, 3)

        fq_h = rms_norm(_heads(fq, FOX_HEADS), fox_q_norm_g)
        fk_h = rms_norm(_heads(fk, FOX_HEADS), fox_k_norm_g)
        log_f = jax.nn.log_sigmoid((ff + fox_f_b).astype(jnp.float32)).transpose(0, 2, 1)
        fox_o = forgetting_attention(fq_h, fk_h, _heads(fv, FOX_HEADS), log_f)
        fox_o = fox_o.astype(x.dtype).transpose(0, 2, 1, 3)

        mn = rms_norm(mem, mem_norm_g)
        mk, mv = jnp.split(mn @ w_mem_kv, 2, axis=-1)
        mk = rms_norm(mk.reshape(B, mem.shape[1], MEM_HEADS, HEAD_DIM), mem_k_norm_g)
        mv = mv.reshape(B, mem.shape[1], MEM_HEADS, HEAD_DIM)
        mq_h = rms_norm(mq.reshape(B, S, MEM_HEADS, HEAD_DIM), mem_q_norm_g)
        m_logits = jnp.einsum('bshd,bmhd->bhsm', mq_h, mk).astype(jnp.float32) * HEAD_DIM ** -0.5
        m_p = jax.nn.softmax(m_logits, axis=-1)
        mem_o = jnp.einsum('bhsm,bmhd->bshd', m_p.astype(mv.dtype), mv)

        o = jnp.concatenate([gla_o, fox_o, mem_o], axis=2)
        o = rms_norm(o, out_norm_g.reshape(N_OUT_HEADS, HEAD_DIM)).reshape(B, S, -1)
        gate = jnp.concatenate([jax.nn.silu(gg), jax.nn.sigmoid(fg), jax.nn.sigmoid(mg)], axis=-1)
        h = h + (o * gate) @ w_out

        u = jax.nn.relu(rms_norm(h, mlp_norm_g) @ w_up)
        h = h + (u * u) @ w_down
    return h


N_MEM = 256
NSA_HEADS = 16
NSA_GROUPS = 4
NSA_HPG = NSA_HEADS // NSA_GROUPS
HEAD_DIM_2 = 64
NSA_WIDTH = NSA_HEADS * HEAD_DIM_2
KV_WIDTH = NSA_GROUPS * HEAD_DIM_2
CMP_LEN = 32
CMP_STRIDE = 16
CMP_HID = 2 * HEAD_DIM_2
SEL_BLK = 64
SEL_TOPN = 16
WIN = 512
Q_BLK = 128
FORCE_SCORE = 1e4
POOL_WINDOWS = (2, 4, 8, 16)
POOL_GROUPS = 4
POOL_WIDTH = D_MODEL // 2
POOL_GW = POOL_WIDTH // POOL_GROUPS
REL_BUCKETS = 32
REL_MAX_DIST = 2048
X_HEADS = 4
X_HEAD_DIM = 128
X_WIDTH = X_HEADS * X_HEAD_DIM
D_FF_2 = -(-8 * D_MODEL // (3 * 256)) * 256
IN_WIDTH = NSA_WIDTH + 6 * KV_WIDTH + 3 * NSA_HEADS + POOL_WIDTH + 2 * D_MODEL


def rms_norm_2(x, g, eps=1e-6):
    xf = x.astype(jnp.float32)
    y = xf * lax.rsqrt(jnp.mean(xf * xf, axis=-1, keepdims=True) + eps)
    return (y * g.astype(jnp.float32)).astype(x.dtype)

def rel_bucket(dist):
    n = jnp.maximum(dist, 0)
    exact = REL_BUCKETS // 2
    nf = jnp.maximum(n, 1).astype(jnp.float32)
    large = exact + (jnp.log(nf / exact) / math.log(REL_MAX_DIST / exact)
                     * (REL_BUCKETS - exact)).astype(jnp.int32)
    return jnp.where(n < exact, n, jnp.minimum(large, REL_BUCKETS - 1))

def masked_softmax(s, mask):
    s = jnp.where(mask, s.astype(jnp.float32), -1e30)
    m = jnp.max(s, axis=-1, keepdims=True)
    e = jnp.where(mask, jnp.exp(s - m), 0.0)
    return e / jnp.maximum(jnp.sum(e, axis=-1, keepdims=True), 1.0)

def compress_kv(raw, pe, w1, w2):
    b, s = raw.shape[0], raw.shape[1]
    n_cmp = (s - CMP_LEN) // CMP_STRIDE + 1
    idx = jnp.arange(n_cmp)[:, None] * CMP_STRIDE + jnp.arange(CMP_LEN)[None, :]
    blk = raw[:, idx] + pe[:, None, :]
    flat = jnp.transpose(blk, (0, 1, 3, 2, 4)).reshape(b, n_cmp, NSA_GROUPS, CMP_LEN * HEAD_DIM_2)
    return jax.nn.gelu(flat @ w1) @ w2

def cmp_to_sel_overlap(n_cmp, n_sel):
    i = jnp.arange(n_cmp)[:, None]
    j = jnp.arange(n_sel)[None, :]
    lo = jnp.maximum(i * CMP_STRIDE, j * SEL_BLK)
    hi = jnp.minimum(i * CMP_STRIDE + CMP_LEN, (j + 1) * SEL_BLK)
    return jnp.maximum(hi - lo, 0).astype(jnp.float32) / CMP_LEN

def nsa_attention(q, k_cmp_raw, v_cmp_raw, k_sel, v_sel, k_win, v_win, gate_logits,
                  cmp_pe, cmp_w1, cmp_w2, rel_bias):
    b, s = q.shape[0], q.shape[1]
    scale = HEAD_DIM_2 ** -0.5
    kc = compress_kv(k_cmp_raw, cmp_pe[0], cmp_w1[0], cmp_w2[0])
    vc = compress_kv(v_cmp_raw, cmp_pe[1], cmp_w1[1], cmp_w2[1])
    n_cmp = kc.shape[1]
    n_sel = s // SEL_BLK
    topn = min(SEL_TOPN, n_sel)
    overlap = cmp_to_sel_overlap(n_cmp, n_sel)
    cmp_end = jnp.arange(n_cmp) * CMP_STRIDE + CMP_LEN - 1
    kb = k_sel.reshape(b, n_sel, SEL_BLK, NSA_GROUPS, HEAD_DIM_2).transpose(0, 3, 1, 2, 4)
    vb = v_sel.reshape(b, n_sel, SEL_BLK, NSA_GROUPS, HEAD_DIM_2).transpose(0, 3, 1, 2, 4)
    kw_pad = jnp.pad(k_win, ((0, 0), (WIN, 0), (0, 0), (0, 0)))
    vw_pad = jnp.pad(v_win, ((0, 0), (WIN, 0), (0, 0), (0, 0)))
    gates = jax.nn.sigmoid(gate_logits.astype(jnp.float32)).astype(q.dtype).reshape(b, s, NSA_HEADS, 3)
    tab_g = rel_bias.reshape(NSA_GROUPS, NSA_HPG, REL_BUCKETS)
    gather_blocks = jax.vmap(jax.vmap(lambda blocks, idx: blocks[idx]))
    group_bias = jax.vmap(jax.vmap(lambda tab, bk: tab[:, bk]), in_axes=(None, 0))

    def head_bias(dist):
        return tab_g[:, :, rel_bucket(dist)]

    def block(qi):
        q0 = qi * Q_BLK
        t = q0 + jnp.arange(Q_BLK)
        qg = lax.dynamic_slice_in_dim(q, q0, Q_BLK, 1).reshape(b, Q_BLK, NSA_GROUPS, NSA_HPG, HEAD_DIM_2)
        gq = lax.dynamic_slice_in_dim(gates, q0, Q_BLK, 1)
        d_c = t[:, None] - cmp_end[None, :]
        s_c = jnp.einsum('bqghd,bngd->bghqn', qg, kc).astype(jnp.float32) * scale + head_bias(d_c)
        p_c = masked_softmax(s_c, d_c >= 0)
        o_c = jnp.einsum('bghqn,bngd->bqghd', p_c.astype(vc.dtype), vc)
        imp = jnp.einsum('bghqn,nj->bgqj', p_c, overlap)
        cur = t // SEL_BLK
        j = jnp.arange(n_sel)[None, :]
        forced = (j == 0) | (j == cur[:, None]) | (j == cur[:, None] - 1)
        imp = jnp.where(forced, FORCE_SCORE, imp)
        imp = jnp.where(j > cur[:, None], -1.0, imp)
        top_val, top_idx = lax.top_k(imp, topn)
        ks = gather_blocks(kb, top_idx)
        vs = gather_blocks(vb, top_idx)
        pos = top_idx[..., None] * SEL_BLK + jnp.arange(SEL_BLK)
        d_s = t[:, None, None] - pos
        mask_s = (top_val >= 0)[..., None] & (d_s >= 0)
        bias_s = group_bias(tab_g, rel_bucket(d_s))
        s_s = jnp.einsum('bqghd,bgqnkd->bghqnk', qg, ks).astype(jnp.float32) * scale + bias_s
        m_len = topn * SEL_BLK
        p_s = masked_softmax(s_s.reshape(b, NSA_GROUPS, NSA_HPG, Q_BLK, m_len),
                             mask_s.reshape(b, NSA_GROUPS, 1, Q_BLK, m_len))
        o_s = jnp.einsum('bghqm,bgqmd->bqghd', p_s.astype(vs.dtype),
                         vs.reshape(b, NSA_GROUPS, Q_BLK, m_len, HEAD_DIM_2))
        kw = lax.dynamic_slice_in_dim(kw_pad, q0, WIN + Q_BLK, 1)
        vw = lax.dynamic_slice_in_dim(vw_pad, q0, WIN + Q_BLK, 1)
        s_pos = q0 - WIN + jnp.arange(WIN + Q_BLK)
        d_w = t[:, None] - s_pos[None, :]
        mask_w = (d_w >= 0) & (d_w < WIN) & (s_pos[None, :] >= 0)
        s_w = jnp.einsum('bqghd,bkgd->bghqk', qg, kw).astype(jnp.float32) * scale + head_bias(d_w)
        p_w = masked_softmax(s_w, mask_w)
        o_w = jnp.einsum('bghqk,bkgd->bqghd', p_w.astype(vw.dtype), vw)
        o = jnp.stack([o_c, o_s, o_w], axis=-1).reshape(b, Q_BLK, NSA_HEADS, HEAD_DIM_2, 3)
        return jnp.einsum('bqhdc,bqhc->bqhd', o, gq)

    out = lax.map(block, jnp.arange(s // Q_BLK))
    return jnp.transpose(out, (1, 0, 2, 3, 4)).reshape(b, s, NSA_WIDTH)

def pool_mixer(u, w_pool, pool_scale):
    b, s, _ = u.shape
    uf = u.astype(jnp.float32)
    cnt_base = jnp.arange(s) + 1
    outs = []
    for gi, w in enumerate(POOL_WINDOWS):
        ug = uf[..., gi * POOL_GW:(gi + 1) * POOL_GW]
        c = jnp.concatenate([jnp.zeros((b, 1, POOL_GW), jnp.float32), jnp.cumsum(ug, axis=1)], axis=1)
        hi = c[:, 1:]
        lo = jnp.pad(c[:, :s + 1 - w], ((0, 0), (w - 1, 0), (0, 0)))
        cnt = jnp.minimum(cnt_base, w).astype(jnp.float32)[None, :, None]
        outs.append((hi - lo) / cnt - ug)
    y = jnp.stack(outs, axis=2).astype(u.dtype)
    y = jnp.einsum('bsgc,gcd->bsgd', y, w_pool)
    return y.reshape(b, s, POOL_WIDTH) * pool_scale

def memory_cross_attention(h, mem_n, wq, wkv, wo):
    b, s, _ = h.shape
    q = (h @ wq).reshape(b, s, X_HEADS, X_HEAD_DIM)
    k, v = jnp.split(mem_n @ wkv, 2, axis=-1)
    k = k.reshape(b, -1, X_HEADS, X_HEAD_DIM)
    v = v.reshape(b, -1, X_HEADS, X_HEAD_DIM)
    sc = jnp.einsum('bshd,bmhd->bhsm', q, k).astype(jnp.float32) * (X_HEAD_DIM ** -0.5)
    p = jax.nn.softmax(sc, axis=-1).astype(v.dtype)
    o = jnp.einsum('bhsm,bmhd->bshd', p, v).reshape(b, s, X_WIDTH)
    return o @ wo

def second_inputs(seed: int = 0) -> dict:
    key = jax.random.key(seed)
    ks = jax.random.split(key, 32)
    f32 = jnp.float32

    def w(k, shape, fan_in):
        return jax.random.normal(k, shape, f32) * (fan_in ** -0.5)

    def gain(k, shape):
        return 1.0 + 0.05 * jax.random.normal(k, shape, f32)

    L = DEPTH
    return {
        "x": jax.random.normal(ks[0], (BATCH, SEQ, D_MODEL), f32),
        "mem": jax.random.normal(ks[1], (BATCH, N_MEM, D_MODEL), f32),
        "rel_bias": 0.5 * jax.random.normal(ks[2], (NSA_HEADS, REL_BUCKETS), f32),
        "ln_mix_pre": gain(ks[3], (L, D_MODEL)),
        "ln_mix_post": gain(ks[4], (L, D_MODEL)),
        "ln_x_pre": gain(ks[5], (L, D_MODEL)),
        "ln_x_post": gain(ks[6], (L, D_MODEL)),
        "ln_mem": gain(ks[7], (L, D_MODEL)),
        "ln_ffn_pre": gain(ks[8], (L, D_MODEL)),
        "ln_ffn_post": gain(ks[9], (L, D_MODEL)),
        "w_in": w(ks[10], (L, D_MODEL, IN_WIDTH), D_MODEL),
        "cmp_pe": 0.1 * jax.random.normal(ks[11], (L, 2, CMP_LEN, HEAD_DIM_2), f32),
        "cmp_w1": w(ks[12], (L, 2, CMP_LEN * HEAD_DIM_2, CMP_HID), CMP_LEN * HEAD_DIM_2),
        "cmp_w2": w(ks[13], (L, 2, CMP_HID, HEAD_DIM_2), CMP_HID),
        "w_pool": w(ks[14], (L, POOL_GROUPS, POOL_GW, POOL_GW), POOL_GW),
        "pool_scale": gain(ks[15], (L, POOL_WIDTH)),
        "w_br_attn": w(ks[16], (L, NSA_WIDTH, D_MODEL), NSA_WIDTH),
        "w_br_pool": w(ks[17], (L, POOL_WIDTH, D_MODEL), POOL_WIDTH),
        "w_mix_out": w(ks[18], (L, D_MODEL, D_MODEL), D_MODEL),
        "w_xq": w(ks[19], (L, D_MODEL, X_WIDTH), D_MODEL),
        "w_xkv": w(ks[20], (L, D_MODEL, 2 * X_WIDTH), D_MODEL),
        "w_xo": w(ks[21], (L, X_WIDTH, D_MODEL), X_WIDTH),
        "w_gate": w(ks[22], (L, D_MODEL, D_FF_2), D_MODEL),
        "w_up": w(ks[23], (L, D_MODEL, D_FF_2), D_MODEL),
        "w_down": w(ks[24], (L, D_FF_2, D_MODEL), D_FF_2),
    }

def second_block(x, mem, rel_bias, ln_mix_pre, ln_mix_post, ln_x_pre, ln_x_post, ln_mem,
              ln_ffn_pre, ln_ffn_post, w_in, cmp_pe, cmp_w1, cmp_w2, w_pool, pool_scale,
              w_br_attn, w_br_pool, w_mix_out, w_xq, w_xkv, w_xo, w_gate, w_up, w_down):
    b, s, _ = x.shape
    splits = [NSA_WIDTH,
              NSA_WIDTH + 6 * KV_WIDTH,
              NSA_WIDTH + 6 * KV_WIDTH + 3 * NSA_HEADS,
              NSA_WIDTH + 6 * KV_WIDTH + 3 * NSA_HEADS + POOL_WIDTH]
    for l in range(DEPTH):
        h = rms_norm_2(x, ln_mix_pre[l])
        z = h @ w_in[l]
        q, kv, nsa_gl, u, merge_logits = jnp.split(z, splits, axis=-1)
        q = q.reshape(b, s, NSA_HEADS, HEAD_DIM_2)
        kv = kv.reshape(b, s, 6, NSA_GROUPS, HEAD_DIM_2)
        a = nsa_attention(q, kv[:, :, 0], kv[:, :, 1], kv[:, :, 2], kv[:, :, 3],
                          kv[:, :, 4], kv[:, :, 5], nsa_gl,
                          cmp_pe[l], cmp_w1[l], cmp_w2[l], rel_bias)
        p = pool_mixer(u, w_pool[l], pool_scale[l])
        g_a, g_p = jnp.split(jax.nn.sigmoid(merge_logits.astype(jnp.float32)).astype(x.dtype), 2, axis=-1)
        y = (g_a * (a @ w_br_attn[l]) + g_p * (p @ w_br_pool[l])) @ w_mix_out[l]
        x = x + rms_norm_2(y, ln_mix_post[l])
        h = rms_norm_2(x, ln_x_pre[l])
        mem_n = rms_norm_2(mem, ln_mem[l])
        y = memory_cross_attention(h, mem_n, w_xq[l], w_xkv[l], w_xo[l])
        x = x + rms_norm_2(y, ln_x_post[l])
        h = rms_norm_2(x, ln_ffn_pre[l])
        y = (jax.nn.silu(h @ w_gate[l]) * (h @ w_up[l])) @ w_down[l]
        x = x + rms_norm_2(y, ln_ffn_post[l])
    return x


def setup_inputs(seed=0):
    out = dict(first_inputs(seed))
    for name, value in second_inputs(seed + 1).items():
        if name != "x":
            out[name + "_2"] = value
    return out


def reference(
    x, mem, attn_norm_g, w_in, gla_a_w2, gla_a_b, fox_f_b, fox_q_norm_g, fox_k_norm_g,
    mem_norm_g, w_mem_kv, mem_q_norm_g, mem_k_norm_g, out_norm_g, w_out, mlp_norm_g, w_up,
    w_down, mem_2, rel_bias_2, ln_mix_pre_2, ln_mix_post_2, ln_x_pre_2, ln_x_post_2, ln_mem_2,
    ln_ffn_pre_2, ln_ffn_post_2, w_in_2, cmp_pe_2, cmp_w1_2, cmp_w2_2, w_pool_2, pool_scale_2,
    w_br_attn_2, w_br_pool_2, w_mix_out_2, w_xq_2, w_xkv_2, w_xo_2, w_gate_2, w_up_2, w_down_2,
):
    x = first_block(
        x, mem, attn_norm_g, w_in, gla_a_w2, gla_a_b, fox_f_b, fox_q_norm_g, fox_k_norm_g,
        mem_norm_g, w_mem_kv, mem_q_norm_g, mem_k_norm_g, out_norm_g, w_out, mlp_norm_g, w_up,
        w_down,
    )
    return second_block(
        x, mem_2, rel_bias_2, ln_mix_pre_2, ln_mix_post_2, ln_x_pre_2, ln_x_post_2, ln_mem_2,
        ln_ffn_pre_2, ln_ffn_post_2, w_in_2, cmp_pe_2, cmp_w1_2, cmp_w2_2, w_pool_2,
        pool_scale_2, w_br_attn_2, w_br_pool_2, w_mix_out_2, w_xq_2, w_xkv_2, w_xo_2, w_gate_2,
        w_up_2, w_down_2,
    )


_drawn_inputs = setup_inputs


def setup_inputs(seed=0):
    import zlib

    import numpy as np

    out = dict(_drawn_inputs(seed))
    spreads = {}
    factors = {'fox_q_norm_g': 8.0,
     'fox_k_norm_g': 8.0,
     'mem_norm_g': 6.809,
     'mem_q_norm_g': 8.0,
     'mem_k_norm_g': 8.0,
     'out_norm_g': 4.692,
     'mlp_norm_g': 2.924,
     'ln_ffn_post_2': 12.813,
     'cmp_pe_2': 16.68,
     'rel_bias_2': 7.553,
     'ln_mix_pre_2': 8.0,
     'ln_mix_post_2': 8.0,
     'ln_x_pre_2': 8.0,
     'ln_x_post_2': 8.0,
     'ln_mem_2': 8.0,
     'ln_ffn_pre_2': 3.119,
     'pool_scale_2': 8.0}
    for name, (base, spread) in spreads.items():
        noise = np.random.default_rng([zlib.crc32(name.encode()), seed]).standard_normal(out[name].shape)
        drawn = base * np.exp(spread * noise) if base else spread * noise
        out[name] = __import__('jax').numpy.asarray(drawn.astype(out[name].dtype))
    for name, factor in factors.items():
        out[name] = (out[name] * factor).astype(out[name].dtype)
    return out
```

```python
from contextlib import ExitStack

import numpy as np

import concourse.bass as bass
from concourse import mybir

F32 = mybir.dt.float32
F32R = mybir.dt.float32r
U32 = mybir.dt.uint32
ACT = mybir.ActivationFunctionType
ALU = mybir.AluOpType
AX = mybir.AxisListType.X

P = 128
S = 256
SB = S // P
D = 2048
KB = D // P
NT = 512
CK = 4
SLOTS = 4
EPS = 1e-6
NEG = -1e30

GLA_H, GLA_DK, GLA_DV, GLA_RANK, GLA_TAU = 8, 64, 128, 16, 16.0
HD = 128
GQ, GK, GV, GG = 0, 512, 1024, 2048
GA = 3072
FQ = GA + GLA_RANK
FK, FV, FG = FQ + 512, FQ + 1024, FQ + 1536
FF = FQ + 2048
MQ = FF + 4
MG = MQ + 512
IN1 = MG + 512
T1 = IN1 // NT
TAIL1 = IN1 - T1 * NT
D_FF = 4 * D
LEVELS = [1, 2, 4, 8, 16, 32, 64]

NSA_H, NSA_G, HD2 = 16, 4, 64
NQ, NKV, NGL = 0, 1024, 2560
NU = NGL + 3 * NSA_H
NM = NU + 1024
IN2 = NM + 2 * D
T2 = IN2 // NT
TAIL2 = IN2 - T2 * NT
CMP_LEN, CMP_STRIDE = 32, 16
N_CMP = (S - CMP_LEN) // CMP_STRIDE + 1
WINDOWS = (2, 4, 8, 16)
REL_BUCKETS, REL_MAX = 32, 2048
D_FF2 = 5632

G_ATTN, G_MEM, G_MLP, G_MIX, G_X, G_MEM2, G_FFN, G_OUT = (16 * n for n in range(8))
B_GLA, G_FQ, G_FK, G_MQ, G_MK, G_POOL = 0, 4, 5, 6, 7, 8


def shape_constants():
    j, i = np.arange(P)[:, None], np.arange(P)[None, :]
    ident = (j == i).astype(np.float32)
    masks = [((j // (2 * w) == i // (2 * w)) & (j % (2 * w) < w) & (i % (2 * w) >= w)).astype(np.float32)
             for w in LEVELS] + [ident]
    q = np.arange(S).reshape(SB, P).T[:, :, None]
    causal = np.where(q >= np.arange(S), 0.0, NEG).astype(np.float32).reshape(P, -1)
    sel = np.zeros((P, 4, S), np.float32)
    for h in range(4):
        sel[h, h] = 1.0
    blocks = (np.arange(P)[:, None] // 16 == np.arange(8)).astype(np.float32)
    base = np.concatenate([ident, blocks, *masks, causal, sel.reshape(P, -1)], 1)
    s0, s1 = np.arange(S)[:, None], np.arange(S)[None, :]
    bands = np.stack([((s1 - s0 >= 0) & (s1 - s0 < w)) / np.minimum(s1 + 1, w) - (s0 == s1) for w in WINDOWS])
    bands = bands.astype(np.float32).reshape(4, SB, P, S).transpose(2, 1, 0, 3).reshape(P, -1)
    y = np.arange(512)
    n = np.maximum(255 - y, 0)
    exact = REL_BUCKETS // 2
    large = exact + (np.log(np.maximum(n, 1).astype(np.float32) / np.float32(exact)) / np.float32(np.log(REL_MAX / exact))
                     * np.float32(REL_BUCKETS - exact)).astype(np.int32)
    bucket = np.where(n < exact, n, np.minimum(large, REL_BUCKETS - 1))
    hot = np.zeros((P, 512 + P), np.float32)
    hot[:REL_BUCKETS, :512] = np.arange(REL_BUCKETS)[:, None] == bucket
    hot[REL_BUCKETS, :512] = np.where(y > 255, NEG, 0.0)
    hot[:, 512:] = ident[::-1]
    return base, np.ascontiguousarray(bands), hot


C_ID, C_BLK = 0, P
C_MASK = C_BLK + 8
C_CAUSAL = C_MASK + 8 * P
C_SEL = C_CAUSAL + SB * S
C_ALL = C_SEL + 4 * S


def hybrid_blocks_kernel(nc, a, c_base, c_bands, c_hot, out):
    es = ExitStack()
    with es:
        place = [1152]

        def sb(name, shape, dt=F32, at=None):
            size = 4 * int(np.prod(shape[1:]))
            if at is None:
                at = place[0]
                place[0] += (size + 31) // 32 * 32
            t = nc.alloc_sbuf_tensor_at(name, shape, dt, offset=at)
            spots[name] = at
            return t

        spots = {}

        def sem(name):
            return es.enter_context(nc.semaphore(name))

        raw = sb("raw", [P, SLOTS, CK, NT])
        whi = sb("whi", [P, 4, 2, NT], F32R)
        wlo = sb("wlo", [P, 4, 2, NT], F32R)
        xhi = sb("xhi", [P, KB, S], F32R)
        xlo = sb("xlo", [P, KB, S], F32R)
        h = sb("h", [P, SB, D])
        mix = sb("mix", [P, SB, D])
        proj_at = place[0]
        proj1 = sb("proj1", [P, SB, IN1], at=proj_at)
        proj2 = sb("proj2", [P, SB, IN2])
        xkv = sb("xkv", [P, SB, 1024])
        base_at = place[0]
        base = sb("base", [P, C_ALL])
        mkv = sb("mkv", [P, SB, 1024])
        gains = sb("gains", [P, P])
        gain_t = sb("gain_t", [P, P])
        gains2 = sb("gains2", [16, P])
        gain2_t = sb("gain2_t", [P, 16])
        mix_gain = sb("mix_gain", [P, 16])
        small = sb("small", [P, 256])
        stage_t = sb("stage_t", [P, 2, NT])
        ybuf = sb("ybuf", [P, SB, D], at=proj_at)
        mem_rows = sb("mem_rows", [P, 2, SB, D], at=proj_at)
        xn = sb("xn", [P, SB, D], at=proj_at + 32768)
        junk = sb("junk", [P, D], at=proj_at + 49152)
        post_gain = sb("post_gain", [P, D], at=proj_at + 16384)
        u_row = sb("u_row", [P, SB, NT], at=proj_at + 24576)
        uhi = sb("uhi", [P, 4, S], F32R, at=proj_at + 28672)
        ulo = sb("ulo", [P, 4, S], F32R, at=proj_at + 53248)
        g_row = sb("g_row", [P, SB, NT], at=proj_at + 57344)
        wa = spots["xhi"]
        qn = sb("qn", [P, SB, 512], at=wa)
        kn = sb("kn", [P, SB, 512], at=wa + 4096)
        qt = sb("qt", [P, 4, S], at=wa + 8192)
        kt = sb("kt", [P, 4, S], at=wa + 12288)
        pr = sb("pr", [P, 8, S], at=wa + 16384)
        pt = sb("pt", [P, 8, 2, P], at=wa + 24576)
        gqt = sb("gqt", [P, 4, S], at=wa)
        gkt = sb("gkt", [P, 4, S], at=wa + 4096)
        gbt = sb("gbt", [P, 4, S], at=wa + 8192)
        gl = sb("gl", [P, 4, S], at=wa + 12288)
        ge = sb("ge", [P, 2, 4, S], at=wa + 16384)
        att = sb("att", [P, 2, 8, P], at=wa + 24576)
        wb = spots["whi"]
        gqe = sb("gqe", [P, 2, 4, S], at=wb)
        gke = sb("gke", [P, 2, 4, S], at=wb + 8192)
        att10 = sb("att10", [P, 8, P], at=wb + 16384)
        gat = sb("gat", [GLA_RANK, S], at=wb + 20480)
        gw2 = sb("gw2", [GLA_RANK, 512], at=wb + 21504)
        g_ones = sb("g_ones", [P, S], at=wb + 23552)
        fct = sb("fct", [4, 4, S], at=wb + 24576)
        fbias = sb("fbias", [4, 1], at=wb + 28672)
        nqt = sb("nqt", [P, 8, S], at=wa)
        nkt = sb("nkt", [P, 2, NSA_G, S], at=wa + 8192)
        kdup = sb("kdup", [P, SB, 2, NSA_G, 2, HD2], at=wa + 16384)
        kvr = sb("kvr", [P, SB, NSA_G, 2, HD2], at=wa + 24576)
        bias = sb("bias", [P, NSA_H, S], at=base_at + 4 * C_MASK)
        hot = sb("hot", [P, 512 + P], at=wb)
        relt = sb("relt", [P, 16], at=wb + 2560)
        toep = sb("toep", [16, 512], at=wb + 2688)
        flip = sb("flip", [P, NSA_H, S], at=wb + 4736)
        rawt = sb("rawt", [P, NSA_G, S], at=wb)
        pet = sb("pet", [P, CMP_LEN], at=wb + 4096)
        cw2 = sb("cw2", [P, 3, HD2], at=wb + 4224)
        hid = sb("hid", [P, 2, NSA_G, 16], at=wb + 4992)
        hidr = sb("hidr", [P, 2, 8, 16], at=wb + 5504)
        kct = sb("kct", [P, NSA_G * 16], at=wb + 6528)
        vbd = sb("vbd", [P, 2, 8, HD2], at=wb + 6784)
        pc = sb("pc", [P, SB, NSA_H, 16], at=wb + 10880)
        pct = sb("pct", [P, SB, 2, P], at=wb + 12928)
        yt = sb("yt", [P, 8, S], at=wb + 14976)
        gates = sb("gates", [P, SB, 3 * NSA_H], at=wb + 23168)
        tmp = sb("tmp", [P, 8 * HD2 * 2], at=wb + 23552)
        qx = sb("qx", [P, SB, 512], at=proj_at + 57344 - 4096)
        assert place[0] <= nc.sbuf_usable_end, place[0]
        assert base_at + 4 * C_MASK + 16384 <= spots["gains"]

        ident = base[:, C_ID:C_ID + P]
        blkmask = base[:, C_BLK:C_BLK + 8]

        ps_a = es.enter_context(nc.psum_tensor("ps_a", [P, 4 * NT], F32))
        ps_b = es.enter_context(nc.psum_tensor("ps_b", [P, 4 * NT], F32))

        def bank(n):
            t = ps_a if n < 4 else ps_b
            return t[:, (n % 4) * NT:(n % 4 + 1) * NT]

        toep_dram = nc.dram_tensor("toep_scratch", [16, 512], F32, kind="Internal").ap()

        w_loaded = [sem(f"w_loaded{i}") for i in range(SLOTS)]
        sp_loaded = [sem(f"sp_loaded{i}") for i in range(4)]
        hi_done, lo_done, pe_half, evicted = sem("hi_done"), sem("lo_done"), sem("pe_half"), sem("evicted")
        ld = {n: sem(f"ld_{n}") for n in ("mem", "mem2", "x", "gains", "gains2", "base", "gw2", "hot", "rel",
                                          "toep", "flip", "cmp", "gain")}
        gain_ps, gain_sb = sem("gain_ps"), sem("gain_sb")
        n_sq, n_var, n_std, n_rows = sem("norm_sq"), sem("norm_var"), sem("norm_std"), sem("norm_rows")
        t_ps, t_y, t_hi, t_lo = sem("t_ps"), sem("t_y"), sem("t_hi"), sem("t_lo")
        dve_order, act_order, pool_order = sem("dve_order"), sem("act_order"), sem("pool_order")
        post_sq, post_var, post_std, post_done = sem("post_sq"), sem("post_var"), sem("post_std"), sem("post_done")
        a_var, a_std, a_rows, a_tps, a_tsb = (sem(n) for n in ("att_var", "att_std", "att_rows", "att_tps", "att_tsb"))
        a_log, a_sub, a_exp, a_pps, a_psb, a_o, a_out = (
            sem(n) for n in ("att_logits", "att_sub", "att_exp", "att_pps", "att_psb", "att_o", "att_out"))
        gla = {n: sem("gla_" + n) for n in ("gaps", "gat", "zps", "z", "abs", "exp", "ln", "b", "d", "e", "qk",
                                            "tps", "tsb", "s", "att", "o", "out")}
        fx = {n: sem("fox_" + n) for n in ("tps", "z", "abs", "exp", "ln", "c")}
        gate_done, o_var, o_std, o_rows = sem("gate_done"), sem("o_var"), sem("o_std"), sem("o_rows")
        u_row_done, u_tps, u_hi, u_lo, d_add = sem("u_row"), sem("u_tps"), sem("u_hi"), sem("u_lo"), sem("down_added")
        ns = {n: sem("nsa_" + n) for n in ("rel", "rows", "tp", "tpsb", "flip", "bias", "t1", "t1s", "t2", "t2s", "t3", "t3s",
                                           "hid", "gelu", "hidr", "kv", "kvs", "log", "sub", "exp", "p", "pps", "psb",
                                           "oc", "acc", "gate", "yps", "ysb", "pool", "pooled")}
        merge_gate, y1_done = sem("merge_gate"), sem("y1_done")
        silu_done = sem("silu_done")
        stored = sem("stored")

        seg = {}
        at_c, at_q, at_t = 0, 0, 0
        q_after = []
        special0 = None
        for name, tiles, chunks in (("memkv", 2, 4), ("xkv", 2, 4), ("in1", T1, 4), ("tail1", 1, 1), ("wout", 4, 4),
                                    ("mlp", 16, 8), ("in2", T2, 4), ("tail2", 1, 1), ("special", 4, 1), ("br", 8, 2),
                                    ("mixo", 4, 4), ("xq", 1, 4), ("xo", 4, 1), ("ffn", 11, 12)):
            seg[name] = (at_c, at_q, at_t)
            n = tiles * chunks
            if name == "special":
                special0 = at_c
            q_after += [at_q + (0 if name == "special" else 2 * (k + 1)) for k in range(n)]
            at_c += n
            if name != "special":
                at_q += 2 * n
            if name not in ("mlp", "ffn", "special"):
                at_t += tiles
        seg["end"] = (at_c, at_q, at_t)

        def loads_before(c):
            return c // SLOTS - (1 if c >= special0 + 4 else 0)

        block = es.enter_context(nc.Block())

        w1 = {"memkv": a["w_mem_kv"], "xkv": a["w_xkv_2"][0], "in1": a["w_in"], "wout": a["w_out"],
              "in2": a["w_in_2"][0], "mixo": a["w_mix_out_2"][0], "xq": a["w_xq_2"][0], "xo": a["w_xo_2"][0]}

        @block.sync
        def _(sp):
            def load(c, src, dst=None, i=None, chunks=0):
                more = 0 if i is None else i
                if special0 + 4 <= c < special0 + 8:
                    s = c - 4 - special0
                    if s < 2:
                        sp.wait_ge(ns["hid"], 1)
                    elif s == 2:
                        sp.wait_ge(ns["yps"], 1)
                    else:
                        sp.wait_ge(ns["pool"], 1)
                elif c >= SLOTS:
                    sp.wait_ge(lo_done, q_after[c - SLOTS] + more * (2 * chunks))
                d = raw[:, c % SLOTS] if dst is None else dst
                sp.dma_start(d, src).then_inc(w_loaded[c % SLOTS], 16)

            def rows(w, r0, n, c0, cols=NT):
                return w[r0:r0 + n, c0:c0 + cols].rearrange("(k p) n -> p k n", p=P)

            def linear(name, first, last, kchunks=4):
                c0 = seg[name][0]
                for t in range(first, last):
                    for k in range(kchunks):
                        load(c0 + t * kchunks + k, rows(w1[name], k * CK * P, CK * P, t * NT))

            def looped(name, pairs):
                c0 = seg[name][0]
                linear(name, 0, 2)
                with sp.Fori(1, pairs) as i:
                    for j in range(8):
                        load(c0 + j, w1[name][(j % 4) * CK * P:(j % 4 + 1) * CK * P,
                                              bass.ds(i * (2 * NT) + (j // 4) * NT, NT)].rearrange("(k p) n -> p k n", p=P),
                             i=i, chunks=8)

            def tail(name, w, cols, n):
                c = seg[name][0]
                load(c, w[:, cols:cols + n].rearrange("(k p) n -> p k n", p=P),
                     raw[:, c % SLOTS].rearrange("p k n -> p (k n)")[:, 0:KB * n].rearrange("p (k n) -> p k n", n=n))

            linear("memkv", 0, 2)
            linear("xkv", 0, 2)
            looped("in1", T1 // 2)
            tail("tail1", a["w_in"], T1 * NT, TAIL1)
            linear("wout", 0, 4)

            c0 = seg["mlp"][0]

            def mlp_up(c, g, i=None):
                for k in range(4):
                    cols = slice(g * NT, (g + 1) * NT) if i is None else bass.ds(i * NT + g * NT, NT)
                    load(c + k, a["w_up"][k * CK * P:(k + 1) * CK * P, cols].rearrange("(k p) n -> p k n", p=P), i=i, chunks=8)

            def mlp_down(c, g, w, i=None, chunks=8):
                for t in range(4):
                    r = slice(g * NT, (g + 1) * NT) if i is None else bass.ds(i * NT + g * NT, NT)
                    load(c + t, w[r, t * NT:(t + 1) * NT].rearrange("(k p) n -> p k n", p=P), i=i, chunks=chunks)

            ng = D_FF // NT
            mlp_up(c0, 0)
            mlp_up(c0 + 4, 1)
            with sp.Fori(0, ng - 2) as i:
                mlp_down(c0 + 8, 0, a["w_down"], i)
                mlp_up(c0 + 12, 2, i)
            mlp_down(c0 + 8 * ng - 8, ng - 2, a["w_down"])
            mlp_down(c0 + 8 * ng - 4, ng - 1, a["w_down"])

            looped("in2", T2 // 2)
            linear("in2", T2 - 1, T2)
            tail("tail2", a["w_in_2"][0], T2 * NT, TAIL2)
            for s in range(4):
                c = special0 + s
                sp.wait_ge(lo_done, q_after[c - SLOTS])
                slot = raw[:, c % SLOTS]
                flat = slot.rearrange("p k n -> p (k n)")
                if s < 2:
                    for kv in range(2):
                        sp.dma_start(flat[kv * HD2:(kv + 1) * HD2, :].rearrange("p (l n) -> p l n", n=P),
                                     a["cmp_w1_2"][0, kv, s * 1024:(s + 1) * 1024, :].rearrange("(l d) n -> d l n", d=HD2)
                                     ).then_inc(sp_loaded[s], 16)
                elif s == 2:
                    sp.dma_start(flat, c_bands).then_inc(sp_loaded[s], 16)
                else:
                    sp.dma_start(flat.rearrange("p (g k n) -> p (g k) n", g=4, k=2),
                                 a["w_pool_2"][0].rearrange("g (k p) n -> p (g k) n", p=P)).then_inc(sp_loaded[s], 16)
            c0 = seg["br"][0]
            for t in range(4):
                for k in range(2):
                    load(c0 + 4 * t + k, rows(a["w_br_attn_2"][0], k * 512, 512, t * NT))
                for k in range(2):
                    load(c0 + 4 * t + 2 + k, rows(a["w_br_pool_2"][0], k * 512, 512, t * NT))
            linear("mixo", 0, 4)
            linear("xq", 0, 1)
            linear("xo", 0, 4, 1)

            c0 = seg["ffn"][0]

            def ffn_in(c, g, i=None):
                for n, w in enumerate((a["w_gate_2"][0], a["w_up_2"][0])):
                    for k in range(4):
                        cols = slice(g * NT, (g + 1) * NT) if i is None else bass.ds(i * NT + g * NT, NT)
                        load(c + 4 * n + k, w[k * CK * P:(k + 1) * CK * P, cols].rearrange("(k p) n -> p k n", p=P),
                             i=i, chunks=12)

            ng = D_FF2 // NT
            wd = a["w_down_2"][0]
            ffn_in(c0, 0)
            ffn_in(c0 + 8, 1)
            with sp.Fori(0, ng - 2) as i:
                mlp_down(c0 + 16, 0, wd, i, 12)
                ffn_in(c0 + 20, 2, i)
            mlp_down(c0 + 12 * ng - 8, ng - 2, wd)
            mlp_down(c0 + 12 * ng - 4, ng - 1, wd)

            for b in range(SB):
                sp.wait_ge(post_done, 2 * SB + b + 1)
                sp.dma_start(out[0, b * P:(b + 1) * P, :], h[:, b]).then_inc(stored, 16)
            sp.wait_ge(stored, 16 * SB)

        s_sq, s_var, s_std, s_rstd = (small[:, 2 * n:2 * n + 2] for n in range(4))
        s_psq, s_pvar, s_pstd, s_prstd = (small[:, 8 + 2 * n:10 + 2 * n] for n in range(4))
        s_ass, s_astd, s_arstd = small[:, 16:32], small[:, 32:48], small[:, 48:64]
        s_max, s_sum, s_co = small[:, 64:72], small[:, 72:80], small[:, 80:88]
        s_oss, s_ostd, s_orstd = small[:, 96:128], small[:, 128:160], small[:, 160:192]
        s_cmax, s_csum, s_cinv = small[:, 96:128], small[:, 128:160], small[:, 160:192]

        norms = [(lambda: mem_rows[:, 0], G_MEM), (lambda: mem_rows[:, 1], G_MEM2), (lambda: h[:], G_ATTN),
                 (lambda: h[:], G_MLP), (lambda: h[:], G_MIX), (lambda: h[:], G_X), (lambda: h[:], G_FFN)]
        norm_loaded = [ld["mem"], ld["mem2"], ld["x"]]
        QUADS = {}
        at = 0
        for name, kb in (("n0", 16), ("n1", 16), ("n2", 16), ("o", 16), ("n3", 16), ("n4", 16), ("ap", 16), ("y1", 16),
                         ("n5", 16), ("xo", 4), ("n6", 16)):
            QUADS[name] = (at, SB * kb // 4)
            at += SB * kb // 4
        XT_FREE = {"n1": "xkv", "n2": "in1", "o": "wout", "n3": "mlp", "n4": "in2", "ap": "br", "y1": "mixo",
                   "n5": "xq", "xo": "xo", "n6": "ffn"}

        def quad_dst(name, k):
            per = QUADS[name][1] // SB
            b, k4 = k // per, k % per
            return b, 4 * k4

        @block.scalar
        def _(act):
            order = [0]

            def link(ins):
                order[0] += 1
                ins.then_inc(act_order, 1)
                act.wait_ge(act_order, order[0])

            def copy(o, i):
                return nc.scalar.copy(o, i)

            act.dma_start(mem_rows[:, 0], a["mem"][0].rearrange("(b p) d -> p b d", p=P)).then_inc(ld["mem"], 16)
            act.dma_start(base[:], c_base).then_inc(ld["base"], 16)
            for n, g in enumerate(("attn_norm_g", "mem_norm_g", "mlp_norm_g", "ln_mix_pre_2", "ln_x_pre_2", "ln_mem_2",
                                   "ln_ffn_pre_2", "out_norm_g")):
                g = a[g] if len(a[g].shape) == 1 else a[g][0]
                act.dma_start(gains[16 * n:16 * n + 16, :], g.rearrange("(r c) -> r c", c=P)).then_inc(ld["gains"], 16)
            act.dma_start(mem_rows[:, 1], a["mem_2"][0].rearrange("(b p) d -> p b d", p=P)).then_inc(ld["mem2"], 16)
            act.dma_start(h[:], a["x"][0].rearrange("(b p) d -> p b d", p=P)).then_inc(ld["x"], 16)
            act.dma_start(gains2[0:4, :], a["gla_a_b"].rearrange("(r c) -> r c", c=P)).then_inc(ld["gains2"], 16)
            for n, g in enumerate(("fox_q_norm_g", "fox_k_norm_g", "mem_q_norm_g", "mem_k_norm_g")):
                act.dma_start(gains2[4 + n:5 + n, :], a[g].rearrange("(r c) -> r c", c=P)).then_inc(ld["gains2"], 16)
            act.dma_start(gains2[8:16, :], a["pool_scale_2"][0].rearrange("(r c) -> r c", c=P)).then_inc(ld["gains2"], 16)

            def hi(q, slot, i=None, halves=0, chunk=None, kn_=None):
                c = chunk
                more = 0 if i is None else i
                act.wait_ge(w_loaded[c % SLOTS], 16 * (loads_before(c) + 1) + more * (16 * halves // 8))
                if q >= 4:
                    act.wait_ge(pe_half, q - 3 + more * halves)
                j = q % 2
                if kn_ is None:
                    return copy(whi[:, q % 4], raw[:, c % SLOTS, 2 * j:2 * j + 2]).then_inc(hi_done, 1)
                n = kn_ * KB // 2
                return copy(whi[:, q % 4].rearrange("p k n -> p (k n)")[:, 0:n],
                            raw[:, c % SLOTS].rearrange("p k n -> p (k n)")[:, j * n:(j + 1) * n]).then_inc(hi_done, 1)

            def evict(t, q_end, dst, cols=NT):
                act.wait_ge(pe_half, q_end)
                for b in range(SB):
                    ins = copy(dst(b), bank(2 * (t % 2) + b)[:, 0:cols])
                ins.then_inc(evicted, 1)

            def linear(name, first, last, dst, kchunks=4, evicting=True):
                c0, q0, t0 = seg[name]
                n = 2 * kchunks
                pend = []
                for k in range(first * n, last * n):
                    hi(q0 + k, 0, chunk=c0 + k // 2)
                    if evicting:
                        if (k + 1) % n == 0:
                            pend.append((k + 3, k // n))
                        if pend and pend[0][0] <= k:
                            _, t = pend.pop(0)
                            evict(t0 + t, q0 + (t + 1) * n, lambda b: dst(t, b))
                for _, t in pend:
                    evict(t0 + t, q0 + (t + 1) * n, lambda b: dst(t, b))

            def looped(name, pairs):
                c0, q0, _ = seg[name]
                for k in range(16):
                    hi(q0 + k, 0, chunk=c0 + k // 2)
                with act.Fori(1, pairs) as i:
                    for k in range(16):
                        hi(q0 + k, 0, i=i, halves=16, chunk=c0 + k // 2)

            def tail(name, n):
                c0, q0, t0 = seg[name]
                for k in range(2):
                    hi(q0 + k, 0, chunk=c0, kn_=n)

            def square_sums(n):
                if n < 3:
                    act.wait_ge(norm_loaded[n], 16)
                elif n == 3:
                    act.wait_ge(evicted, seg["mlp"][2])
                elif n == 4:
                    act.wait_ge(d_add, 64)
                else:
                    act.wait_ge(post_done, SB * (n - 4))
                if n:
                    act.wait_ge(n_rows, n)
                src = norms[n][0]()
                for b in range(SB):
                    ins = nc.scalar.activation(junk[:], src[:, b], ACT.Square, accum_out=s_sq[:, b:b + 1])
                    if b == 0:
                        link(ins)
                ins.then_inc(n_sq, 1)
                act.wait_ge(n_var, n + 1)
                nc.scalar.activation(s_std, s_var, ACT.Sqrt).then_inc(n_std, 1)

            def to_hi(name, free=None):
                q0, n = QUADS[name]
                if free is not None:
                    act.wait_ge(pe_half, free)
                for k in range(n):
                    b, kb = quad_dst(name, k)
                    act.wait_ge(t_y, q0 + k + 1)
                    copy(xhi[:, kb:kb + 4, b * P:(b + 1) * P],
                         stage_t[:, (q0 + k) % 2].rearrange("p (k n) -> p k n", n=P)).then_inc(t_hi, 1)

            def q_end(name):
                names = list(seg)
                return seg[names[names.index(name) + 1]][1]

            def post_norm(n, tiles_evicted=None):
                if n < 2:
                    act.wait_ge(evicted, tiles_evicted)
                else:
                    act.wait_ge(d_add, 64 + 44)
                for b in range(SB):
                    ins = nc.scalar.activation(xn[:, 0], ybuf[:, b], ACT.Square, accum_out=s_psq[:, b:b + 1])
                    if b == 0:
                        link(ins)
                ins.then_inc(post_sq, 1)
                act.wait_ge(post_var, n + 1)
                nc.scalar.activation(s_pstd, s_pvar, ACT.Sqrt).then_inc(post_std, 1)

            def load_post_gain(name):
                act.dma_start(post_gain[:], a[name][0:1, :].to_broadcast([P, D])).then_inc(ld["gain"], 16)

            square_sums(0)
            to_hi("n0")
            linear("memkv", 0, 2, lambda t, b: mkv[:, b, t * NT:(t + 1) * NT])
            square_sums(1)
            to_hi("n1", q_end("memkv"))
            linear("xkv", 0, 2, lambda t, b: xkv[:, b, t * NT:(t + 1) * NT])
            square_sums(2)
            to_hi("n2", q_end("xkv"))
            looped("in1", T1 // 2)
            tail("tail1", TAIL1)
            act.wait_ge(pe_half, q_end("tail1"))
            act.dma_start(gw2[:], a["gla_a_w2"]).then_inc(ld["gw2"], 16)
            act.dma_start(fbias[:], a["fox_f_b"].rearrange("(r c) -> r c", c=1)).then_inc(ld["gw2"], 16)

            act.wait_ge(evicted, seg["wout"][2])
            nc.scalar.activation(proj1[:, :, GG:GG + 1024], proj1[:, :, GG:GG + 1024], ACT.Silu).then_inc(gate_done, 1)
            nc.scalar.activation(proj1[:, :, FG:FG + 512], proj1[:, :, FG:FG + 512], ACT.Sigmoid).then_inc(gate_done, 1)
            nc.scalar.activation(proj1[:, :, MG:MG + 512], proj1[:, :, MG:MG + 512], ACT.Sigmoid).then_inc(gate_done, 1)

            act.wait_ge(gla["z"], 1)
            link(nc.scalar.activation(ge[:, 0], gl[:], ACT.Abs))
            link(nc.scalar.activation(ge[:, 0], ge[:, 0], ACT.Exp, scale=-1.0))
            nc.scalar.activation(ge[:, 0], ge[:, 0], ACT.Ln, bias=1.0).then_inc(gla["ln"], 1)
            act.wait_ge(fx["z"], 1)
            link(nc.scalar.activation(fct[:, 1], fct[:, 0], ACT.Abs))
            link(nc.scalar.activation(fct[:, 1], fct[:, 1], ACT.Exp, scale=-1.0))
            nc.scalar.activation(fct[:, 1], fct[:, 1], ACT.Ln, bias=1.0).then_inc(fx["ln"], 1)
            for l in range(8):
                act.wait_ge(gla["d"], l + 1)
                link(nc.scalar.activation(ge[:, l % 2], ge[:, l % 2], ACT.Abs))
                nc.scalar.activation(ge[:, l % 2], ge[:, l % 2], ACT.Exp, scale=-1.0 / GLA_TAU).then_inc(gla["e"], 1)

            def softmax(n):
                act.wait_ge(a_sub, n + 1)
                nc.scalar.activation(pr[:], pr[:], ACT.Exp).then_inc(a_exp, 1)
                act.wait_ge(a_pps, n + 1)
                copy(pt[:, 0:4], ps_b[:, 0:1024].rearrange("p (x k n) -> p x k n", k=2, n=P)).then_inc(a_psb, 1)

            def attention(n, normed):
                if normed:
                    act.wait_ge(a_var, n + 1)
                    nc.scalar.activation(s_astd, s_ass, ACT.Sqrt).then_inc(a_std, 1)
                softmax(n)

            attention(0, True)
            attention(1, True)
            act.wait_ge(o_var, 1)
            nc.scalar.activation(s_ostd, s_oss, ACT.Sqrt).then_inc(o_std, 1)
            to_hi("o")
            linear("wout", 0, 4, None, evicting=False)
            square_sums(3)
            to_hi("n3", q_end("wout"))

            c0, q0, _ = seg["mlp"]

            def up_rows(g, i=None):
                more = 0 if i is None else i
                q = q0 + 8 if g == 0 else q0 + 16 + 16 * (g - 1)
                act.wait_ge(pe_half, q + more * 16)
                if g or i is not None:
                    act.wait_ge(u_tps, g + more)
                for b in range(SB):
                    nc.scalar.activation(g_row[:, b], bank(b), ACT.Relu).then_inc(silu_done, 1)
                for b in range(SB):
                    act.wait_ge(silu_done, 2 * g + b + 1 + (0 if i is None else i * 2))
                    ins = nc.scalar.activation(u_row[:, b], g_row[:, b], ACT.Square)
                ins.then_inc(u_row_done, 1)

            def up_hi(g, i=None, base_=0):
                more = 0 if i is None else i
                act.wait_ge(u_tps, base_ + g + 1 + more)
                copy(uhi[:].rearrange("p k (b n) -> p b k n", b=SB),
                     ps_b[:, 1024:2048].rearrange("p (b k n) -> p b k n", b=SB, k=4)).then_inc(u_hi, 1)

            for k in range(8):
                hi(q0 + k, 0, chunk=c0 + k // 2)
            for k in range(8, 16):
                hi(q0 + k, 0, chunk=c0 + k // 2)
                if k == 10:
                    up_rows(0)
                if k == 14:
                    up_hi(0)
            ng = D_FF // NT
            with act.Fori(0, ng - 2) as i:
                for k in range(16):
                    hi(q0 + 16 + k, 0, i=i, halves=16, chunk=c0 + 8 + k // 2)
                    if k == 2:
                        up_rows(1, i)
                    if k == 12:
                        up_hi(1, i)
            k0 = 16 + 16 * (ng - 2)
            for k in range(16):
                hi(q0 + k0 + k, 0, chunk=c0 + (k0 + k) // 2)
                if k == 2:
                    up_rows(ng - 1)
                if k == 10:
                    up_hi(ng - 1)

            square_sums(4)
            act.wait_ge(pe_half, q_end("mlp"))
            act.dma_start(hot[:], c_hot).then_inc(ld["hot"], 16)
            act.dma_start(relt[0:32, :], a["rel_bias_2"].rearrange("h b -> b h"), allow_slow_non_contiguous=True).then_inc(ld["rel"], 16)
            act.wait_ge(ns["tpsb"], 1)
            act.dma_start(toep_dram, toep[:]).then_inc(ld["toep"], 16)
            act.wait_ge(ld["toep"], 16)
            for hh in range(NSA_H):
                act.dma_start(flip[:, hh], bass.AP(toep_dram.tensor, hh * 512, [[1, P], [1, S]])).then_inc(ld["flip"], 16)
            to_hi("n4", q_end("mlp"))
            act.wait_ge(ns["flip"], 8)
            looped("in2", T2 // 2)
            linear("in2", T2 - 1, T2, None, evicting=False)
            tail("tail2", TAIL2)

            act.wait_ge(pe_half, q_end("tail2"))
            for kv in range(2):
                act.dma_start(pet[kv * HD2:(kv + 1) * HD2, :], a["cmp_pe_2"][0, kv].rearrange("l d -> d l"),
                              allow_slow_non_contiguous=True).then_inc(ld["cmp"], 16)
            for n, kv in enumerate((0, 0, 1)):
                act.dma_start(cw2[:, n], a["cmp_w2_2"][0, kv]).then_inc(ld["cmp"], 16)
            act.wait_ge(evicted, seg["special"][2])
            nc.scalar.activation(gates[:], proj2[:, :, NGL:NU], ACT.Sigmoid).then_inc(ns["gate"], 1)
            nc.scalar.activation(proj2[:, :, NM:NM + D], proj2[:, :, NM:NM + D], ACT.Sigmoid).then_inc(merge_gate, 1)
            nc.scalar.activation(proj2[:, :, NM + D:IN2], proj2[:, :, NM + D:IN2], ACT.Sigmoid).then_inc(merge_gate, 1)
            act.wait_ge(ns["hid"], 1)
            act.wait_ge(ns["hidr"], 1)
            nc.scalar.activation(hid[:, 0, :, 0:N_CMP], ps_a[:, 0:NSA_G * N_CMP].rearrange("p (g n) -> p g n", n=N_CMP),
                                 ACT.Gelu_apprx_tanh).then_inc(ns["gelu"], 1)
            nc.scalar.activation(hid[:, 1, :, 0:N_CMP], ps_a[:, NT:NT + NSA_G * N_CMP].rearrange("p (g n) -> p g n", n=N_CMP),
                                 ACT.Gelu_apprx_tanh).then_inc(ns["gelu"], 1)
            act.wait_ge(ns["sub"], 1)
            nc.scalar.activation(pc[:], pc[:], ACT.Exp).then_inc(ns["exp"], 1)
            for n in range(8):
                softmax(2 + n)
            to_hi("ap")
            linear("br", 0, 8, None, kchunks=2, evicting=False)
            to_hi("y1", q_end("br"))
            linear("mixo", 0, 4, lambda t, b: ybuf[:, b, t * NT:(t + 1) * NT])
            act.wait_ge(y1_done, 4)
            load_post_gain("ln_mix_post_2")
            post_norm(0, seg["xq"][2])

            square_sums(5)
            to_hi("n5", q_end("mixo"))
            load_post_gain("ln_x_post_2")
            linear("xq", 0, 1, lambda t, b: qx[:, b])
            softmax(10)
            to_hi("xo", q_end("xq"))
            linear("xo", 0, 4, lambda t, b: ybuf[:, b, t * NT:(t + 1) * NT], kchunks=1)
            post_norm(1, seg["ffn"][2])

            square_sums(6)
            to_hi("n6", q_end("xo"))
            load_post_gain("ln_ffn_post_2")
            c0, q0, _ = seg["ffn"]
            ng = D_FF2 // NT
            gbase, sbase = D_FF // NT, 2 * (D_FF // NT)

            def gate_rows(g, i=None):
                more = 0 if i is None else i
                q = q0 + 8 if g == 0 else q0 + 24 + 24 * (g - 1)
                act.wait_ge(pe_half, q + more * 24)
                if g or i is not None:
                    act.wait_ge(u_row_done, gbase + g + more)
                for b in range(SB):
                    nc.scalar.activation(g_row[:, b], bank(b), ACT.Silu).then_inc(silu_done, 1)

            for k in range(16):
                hi(q0 + k, 0, chunk=c0 + k // 2)
                if k == 10:
                    gate_rows(0)
            for k in range(16, 32):
                hi(q0 + k, 0, chunk=c0 + k // 2)
                if k == 26:
                    gate_rows(1)
                    up_hi(0, base_=gbase)
            with act.Fori(0, ng - 2) as i:
                for k in range(24):
                    hi(q0 + 32 + k, 0, i=i, halves=24, chunk=c0 + 16 + k // 2)
                    if k == 18:
                        gate_rows(2, i)
                        up_hi(1, i, gbase)
            k0 = 32 + 24 * (ng - 2)
            for k in range(16):
                hi(q0 + k0 + k, 0, chunk=c0 + (k0 + k) // 2)
                if k == 10:
                    up_hi(ng - 1, base_=gbase)
            post_norm(2)

        @block.vector
        def _(dve):
            order = [0]
            V = nc.vector

            def link(ins):
                order[0] += 1
                ins.then_inc(dve_order, 1)
                dve.wait_ge(dve_order, order[0])

            def lo(q, i=None, halves=0, chunk=None, kn_=None):
                more = 0 if i is None else i
                dve.wait_ge(hi_done, q + 1 + more * halves)
                j, c = q % 2, chunk
                if kn_ is None:
                    return V.tensor_tensor(wlo[:, q % 4], raw[:, c % SLOTS, 2 * j:2 * j + 2], whi[:, q % 4].bitcast(F32),
                                           ALU.subtract).then_inc(lo_done, 1)
                n = kn_ * KB // 2
                return V.tensor_tensor(wlo[:, q % 4].rearrange("p k n -> p (k n)")[:, 0:n],
                                       raw[:, c % SLOTS].rearrange("p k n -> p (k n)")[:, j * n:(j + 1) * n],
                                       whi[:, q % 4].rearrange("p k n -> p (k n)")[:, 0:n].bitcast(F32),
                                       ALU.subtract).then_inc(lo_done, 1)

            def q_end(name):
                names = list(seg)
                return seg[names[names.index(name) + 1]][1]

            def linear(name, first, last, evict=None, kchunks=4):
                c0, q0, t0 = seg[name]
                n = 2 * kchunks
                pend = []
                for k in range(first * n, last * n):
                    lo(q0 + k, chunk=c0 + k // 2)
                    if evict is not None:
                        if (k + 1) % n == 0:
                            pend.append((k + 3, k // n))
                        if pend and pend[0][0] <= k:
                            _, t = pend.pop(0)
                            dve.wait_ge(pe_half, q0 + (t + 1) * n)
                            evict(t, t0 + t)
                for _, t in pend:
                    dve.wait_ge(pe_half, q0 + (t + 1) * n)
                    evict(t, t0 + t)

            def looped(name, pairs, odd, proj):
                c0, q0, t0 = seg[name]

                def out_of(t, col):
                    for b in range(SB):
                        ins = V.tensor_scalar(proj[:, b, col], bank(2 * ((t0 + t) % 2) + b), 1.0, None, ALU.mult)
                    ins.then_inc(evicted, 1)

                for k in range(16):
                    lo(q0 + k, chunk=c0 + k // 2)
                    if k == 10:
                        dve.wait_ge(pe_half, q0 + 8)
                        out_of(0, slice(0, NT))
                with dve.Fori(1, pairs) as i:
                    for k in range(16):
                        lo(q0 + k, i, 16, chunk=c0 + k // 2)
                        if k == 2:
                            dve.wait_ge(pe_half, q0 + i * 16)
                            out_of(1, bass.ds(i * (2 * NT) - NT, NT))
                        if k == 10:
                            dve.wait_ge(pe_half, q0 + 8 + i * 16)
                            out_of(0, bass.ds(i * (2 * NT), NT))
                last = 2 * pairs - 1
                if odd:
                    for k in range(8):
                        lo(q0 + 16 * pairs + k, chunk=c0 + 8 * pairs + k // 2)
                        if k == 2:
                            dve.wait_ge(pe_half, q0 + 16 * pairs)
                            out_of(last, slice(last * NT, (last + 1) * NT))
                    last += 1
                return q0 + 8 * (last + 1), lambda: out_of(last, slice(last * NT, (last + 1) * NT))

            def tail(name, n, before, proj, c1):
                c0, q0, t0 = seg[name]
                for k in range(2):
                    lo(q0 + k, chunk=c0, kn_=n)
                q, out_of = before
                dve.wait_ge(pe_half, q)
                out_of()
                dve.wait_ge(pe_half, q0 + 2)
                for b in range(SB):
                    ins = V.tensor_copy(proj[:, b, c1:c1 + n], bank(2 * (t0 % 2) + b)[:, 0:n])
                ins.then_inc(evicted, 1)

            def normed_rows(n):
                src = norms[n][0]()
                dve.wait_ge(n_sq, n + 1)
                V.tensor_scalar(s_var, s_sq, 1.0 / D, EPS, ALU.mult, ALU.add).then_inc(n_var, 1)
                dve.wait_ge(n_std, n + 1)
                link(V.reciprocal(s_rstd, s_std))
                if n:
                    dve.wait_ge(t_ps, QUADS[f"n{n}"][0])
                for b in range(SB):
                    ins = V.tensor_scalar(xn[:, b], src[:, b], s_rstd[:, b:b + 1], None, ALU.mult)
                ins.then_inc(n_rows, 1)

            def to_lo(name, gain=None, lo_into=None):
                q0, n = QUADS[name]

                def low(k):
                    b, kb = quad_dst(name, k)
                    dve.wait_ge(t_hi, q0 + k + 1)
                    V.tensor_tensor(xlo[:, kb:kb + 4, b * P:(b + 1) * P],
                                    stage_t[:, (q0 + k) % 2].rearrange("p (k n) -> p k n", n=P),
                                    xhi[:, kb:kb + 4, b * P:(b + 1) * P].bitcast(F32), ALU.subtract).then_inc(t_lo, 1)

                for k in range(n):
                    b, kb = quad_dst(name, k)
                    dve.wait_ge(t_ps, q0 + k + 1)
                    if q0 + k >= 2:
                        dve.wait_ge(t_lo, q0 + k - 1)
                    ps = bank(4 + (q0 + k) % 4)
                    if gain is None:
                        ins = V.tensor_copy(stage_t[:, (q0 + k) % 2], ps)
                    else:
                        ins = V.tensor_tensor(stage_t[:, (q0 + k) % 2].rearrange("p (k n) -> p k n", n=P),
                                              ps.rearrange("p (k n) -> p k n", n=P),
                                              gain[:, kb:kb + 4].unsqueeze(2).to_broadcast([P, 4, P]), ALU.mult)
                    ins.then_inc(t_y, 1)
                    if k:
                        low(k - 1)
                low(n - 1)

            def post_norm(n):
                dve.wait_ge(post_sq, n + 1)
                V.tensor_scalar(s_pvar, s_psq, 1.0 / D, EPS, ALU.mult, ALU.add).then_inc(post_var, 1)
                dve.wait_ge(post_std, n + 1)
                link(V.reciprocal(s_prstd, s_pstd))
                dve.wait_ge(ld["gain"], 16 * (n + 1))
                for b in range(SB):
                    link(V.scalar_tensor_tensor(ybuf[:, b], ybuf[:, b], s_prstd[:, b:b + 1], post_gain[:], ALU.mult, ALU.mult))
                    V.tensor_tensor(h[:, b], h[:, b], ybuf[:, b], ALU.add).then_inc(post_done, 1)

            dve.wait_ge(gain_ps, 2)
            link(V.tensor_copy(gain_t[:], bank(7)[:, 0:P]))
            link(V.tensor_copy(gain2_t[:], bank(7)[:, P:P + 16]))
            link(V.memset(mix_gain[:], 1.0))
            V.tensor_copy(mix_gain[:, 8:16], gain2_t[:, G_POOL:G_POOL + 8]).then_inc(gain_sb, 1)
            dve.wait_ge(gain_sb, 1)

            normed_rows(0)
            to_lo("n0", gain_t[:, G_MEM:G_MEM + 16])
            linear("memkv", 0, 2)
            normed_rows(1)
            to_lo("n1", gain_t[:, G_MEM2:G_MEM2 + 16])
            linear("xkv", 0, 2)
            normed_rows(2)
            to_lo("n2", gain_t[:, G_ATTN:G_ATTN + 16])
            before = looped("in1", T1 // 2, False, proj1)
            tail("tail1", TAIL1, before, proj1, T1 * NT)

            dve.wait_ge(pe_half, q_end("tail1"))
            dve.wait_ge(gla["tps"], 1)
            V.tensor_scalar(gqt[:].rearrange("p x s -> p (x s)"), ps_b[:, 0:1024], GLA_DK ** -0.5, None, ALU.mult)
            V.tensor_copy(gkt[:].rearrange("p x s -> p (x s)"), ps_b[:, 1024:2048]).then_inc(gla["tsb"], 1)
            dve.wait_ge(gla["gaps"], 1)
            V.tensor_copy(gat[:], ps_a[0:GLA_RANK, 0:S]).then_inc(gla["gat"], 1)
            dve.wait_ge(gla["gaps"], 2)
            dve.wait_ge(ld["gw2"], 32)
            V.tensor_scalar(fct[:, 0], ps_a[0:4, NT:NT + S], fbias[:, 0:1], None, ALU.add).then_inc(fx["z"], 1)
            dve.wait_ge(gla["zps"], 1)
            V.tensor_tensor(gl[:], ps_a[:, 1024:2048].rearrange("p (x s) -> p x s", s=S),
                            gain2_t[:, B_GLA:B_GLA + 4].unsqueeze(2).to_broadcast([P, 4, S]), ALU.add).then_inc(gla["z"], 1)
            V.memset(att[:], 0.0)
            link(V.memset(g_ones[:], 1.0))
            dve.wait_ge(gla["ln"], 1)
            link(V.scalar_tensor_tensor(gl[:].rearrange("p x s -> p (x s)"), gl[:].rearrange("p x s -> p (x s)"), 0.0,
                                        ge[:, 0].rearrange("p x s -> p (x s)"), ALU.min, ALU.subtract))
            for x in range(4):
                ins = V.tensor_tensor_scan(gbt[:, x], g_ones[:], gl[:, x], 0.0, ALU.mult, ALU.add)
                if x == 3:
                    link(ins)
            dve.wait_ge(fx["z"], 1)
            dve.wait_ge(fx["ln"], 1)
            link(V.scalar_tensor_tensor(fct[:, 0], fct[:, 0], 0.0, fct[:, 1], ALU.min, ALU.subtract))
            link(V.tensor_tensor_scan(fct[:, 2], g_ones[0:4, :], fct[:, 0], 0.0, ALU.mult, ALU.add))
            V.tensor_scalar(fct[:, 3], fct[:, 2], -1.0, None, ALU.mult).then_inc(fx["c"], 1)

            def decays(l):
                w = (LEVELS + [P])[l]
                if l >= 2:
                    dve.wait_ge(gla["qk"], l - 1)
                v = gbt[:].rearrange("p x (m t) -> p (x m) t", t=2 * w)
                V.tensor_tensor(ge[:, l % 2].rearrange("p x (m t) -> p (x m) t", t=2 * w), v,
                                v[:, :, w - 1:w].to_broadcast([P, 4 * S // (2 * w), 2 * w]), ALU.subtract).then_inc(gla["d"], 1)

            def decayed(l):
                dve.wait_ge(gla["e"], l + 1)
                if l == 0:
                    dve.wait_ge(gla["tsb"], 1)
                if l >= 2:
                    dve.wait_ge(gla["s"], l - 1)
                V.tensor_tensor(gqe[:, l % 2], gqt[:], ge[:, l % 2], ALU.mult)
                V.tensor_tensor(gke[:, l % 2], gkt[:], ge[:, l % 2], ALU.mult).then_inc(gla["qk"], 1)

            def scores(l):
                dve.wait_ge(gla["s"], l + 1)
                if l == 7:
                    V.tensor_copy(att10[:].rearrange("p (x t) n -> p t x n", t=2),
                                  ps_b[:, :].rearrange("p (t u) -> p t u", t=2)[:, :, 0:512].rearrange("p t (x n) -> p t x n", n=P)
                                  ).then_inc(gla["att"], 1)
                    return
                m = base[:, C_MASK + l * P:C_MASK + (l + 1) * P] if l < 7 else base[:, C_MASK + 7 * P:C_MASK + 8 * P]
                if l == 8:
                    m = base[:, C_MASK + 7 * P:C_MASK + 8 * P]
                if l == 0:
                    dve.wait_ge(ld["base"], 16)
                V.copy_predicated(att[:].rearrange("p t x n -> p (t x) n"),
                                  m.bitcast(U32).unsqueeze(1).to_broadcast([P, 16, P]),
                                  ps_b[:, :].rearrange("p (y n) -> p y n", n=P)).then_inc(gla["att"], 1)

            decays(0)
            for l in range(8):
                if l + 1 < 8:
                    decays(l + 1)
                decayed(l)
                if l:
                    scores(l - 1)
            scores(7)
            scores(8)
            dve.wait_ge(gla["o"], 1)
            for b in range(SB):
                ins = V.tensor_copy(mix[:, b, 0:1024], ps_b[:, b * 1024:(b + 1) * 1024])
            ins.then_inc(gla["out"], 1)

            def softmax(n, n_pv, masked=None, gated=None, width=HD, store=None):
                lg = ps_b[:, :].rearrange("p (x b k) -> p x b k", b=SB, k=S)
                pv = pr[:].rearrange("p (x b) k -> p x b k", b=SB)
                dve.wait_ge(a_log, n + 1)
                if masked is None:
                    src = ps_b[:, :].rearrange("p (y k) -> p y k", k=S)
                else:
                    masked(lg, pv)
                    src = pr[:]
                link(V.reduce_max(s_max, src, axis=AX))
                V.tensor_tensor(pr[:], src, s_max.unsqueeze(2).to_broadcast([P, 8, S]), ALU.subtract).then_inc(a_sub, 1)
                dve.wait_ge(a_exp, n + 1)
                link(V.reduce_sum(s_sum, pr[:], axis=AX))
                link(V.reciprocal(s_co, s_sum))
                dve.wait_ge(a_pps, n + 1)
                V.tensor_copy(pt[:, 4:8], ps_b[:, 1024:2048].rearrange("p (x k n) -> p x k n", k=2, n=P)).then_inc(a_psb, 1)
                if gated is not None:
                    gated()
                dve.wait_ge(a_o, n + 1)
                store(ps_b[:, 0:8 * width].rearrange("p (t x b d) -> p t x b d", t=2, b=SB, d=width))

            def co_of(b, width):
                return s_co.rearrange("p (t x b) -> p t x b", t=2, b=SB)[:, :, :, b].unsqueeze(3).to_broadcast([P, 2, 2, width])

            def head_rows(n, q_src, k_src):
                V.tensor_tensor(qn[:], q_src, q_src, ALU.mult)
                link(V.tensor_tensor(kn[:], k_src, k_src, ALU.mult))
                V.reduce_sum(s_ass[:, 0:8], qn[:].rearrange("p b (h d) -> p (b h) d", d=HD), axis=AX)
                link(V.reduce_sum(s_ass[:, 8:16], kn[:].rearrange("p b (h d) -> p (b h) d", d=HD), axis=AX))
                V.tensor_scalar(s_ass, s_ass, 1.0 / HD, EPS, ALU.mult, ALU.add).then_inc(a_var, 1)
                dve.wait_ge(a_std, n + 1)
                link(V.reciprocal(s_arstd, s_astd))
                for dst, src, r in ((qn, q_src, s_arstd[:, 0:8]), (kn, k_src, s_arstd[:, 8:16])):
                    for b in range(SB):
                        ins = V.tensor_tensor(dst[:, b].rearrange("p (h d) -> p h d", d=HD),
                                              src[:, b].rearrange("p (h d) -> p h d", d=HD),
                                              r[:, 4 * b:4 * b + 4].unsqueeze(2).to_broadcast([P, 4, HD]), ALU.mult)
                ins.then_inc(a_rows, 1)

            def transposed(k, gq, gk):
                dve.wait_ge(a_tps, k + 1)
                V.tensor_scalar(qt[:].rearrange("p x s -> p (x s)"), ps_b[:, 0:1024], HD ** -0.5 if gq is None else gq,
                                None if gq is None else HD ** -0.5, ALU.mult, *(() if gq is None else (ALU.mult,)))
                if gk is None:
                    ins = V.tensor_copy(kt[:].rearrange("p x s -> p (x s)"), ps_b[:, 1024:2048])
                else:
                    ins = V.tensor_scalar(kt[:].rearrange("p x s -> p (x s)"), ps_b[:, 1024:2048], gk, None, ALU.mult)
                ins.then_inc(a_tsb, 1)

            def add_causal(lg, pv):
                for b in range(SB):
                    ins = V.tensor_tensor(pv[:, :, b], lg[:, :, b],
                                          base[:, C_CAUSAL + b * S:C_CAUSAL + (b + 1) * S].unsqueeze(1).to_broadcast([P, 4, S]),
                                          ALU.add)
                link(ins)

            def store_heads(col):
                def store(o):
                    for b in range(SB):
                        ins = V.tensor_tensor(mix[:, b, col:col + 512].rearrange("p (x t d) -> p t x d", t=2, d=HD),
                                              o[:, :, :, b], co_of(b, HD), ALU.mult)
                    ins.then_inc(a_out, 1)
                return store

            head_rows(0, proj1[:, :, FQ:FQ + 512], proj1[:, :, FK:FK + 512])
            transposed(0, gain2_t[:, G_FQ:G_FQ + 1], gain2_t[:, G_FK:G_FK + 1])
            softmax(0, 0, add_causal, None, HD, store_heads(1024))
            head_rows(1, proj1[:, :, MQ:MQ + 512], mkv[:, :, 0:512])
            transposed(1, gain2_t[:, G_MQ:G_MQ + 1], gain2_t[:, G_MK:G_MK + 1])
            softmax(1, 0, None, None, HD, store_heads(1536))

            dve.wait_ge(a_out, 2)
            dve.wait_ge(gla["out"], 1)
            sq = pr[:].rearrange("p x k -> p (x k)")
            for b in range(SB):
                link(V.tensor_tensor(sq, mix[:, b], mix[:, b], ALU.mult))
                link(V.reduce_sum(s_oss[:, 16 * b:16 * b + 16], sq.rearrange("p (h d) -> p h d", d=HD), axis=AX))
            V.tensor_scalar(s_oss, s_oss, 1.0 / HD, EPS, ALU.mult, ALU.add).then_inc(o_var, 1)
            dve.wait_ge(o_std, 1)
            link(V.reciprocal(s_orstd, s_ostd))
            dve.wait_ge(gate_done, 3)
            for b in range(SB):
                link(V.tensor_tensor(mix[:, b].rearrange("p (h d) -> p h d", d=HD), mix[:, b].rearrange("p (h d) -> p h d", d=HD),
                                     s_orstd[:, 16 * b:16 * b + 16].unsqueeze(2).to_broadcast([P, 16, HD]), ALU.mult))
                V.tensor_tensor(mix[:, b, 0:1024], mix[:, b, 0:1024], proj1[:, b, GG:GG + 1024], ALU.mult)
                V.tensor_tensor(mix[:, b, 1024:1536], mix[:, b, 1024:1536], proj1[:, b, FG:FG + 512], ALU.mult)
                ins = V.tensor_tensor(mix[:, b, 1536:2048], mix[:, b, 1536:2048], proj1[:, b, MG:MG + 512], ALU.mult)
            ins.then_inc(o_rows, 1)
            to_lo("o", gain_t[:, G_OUT:G_OUT + 16])

            def add_to(dst, sem_):
                def evict(t, tile):
                    for b in range(SB):
                        ins = V.tensor_tensor(dst[:, b, t * NT:(t + 1) * NT], dst[:, b, t * NT:(t + 1) * NT],
                                              bank(2 * (tile % 2) + b), ALU.add)
                    ins.then_inc(sem_, 1)
                return evict

            linear("wout", 0, 4, add_to(h, evicted))
            dve.wait_ge(evicted, seg["mlp"][2])
            normed_rows(3)
            to_lo("n3", gain_t[:, G_MLP:G_MLP + 16])

            def up_lo(g, i=None, base_=0):
                more = 0 if i is None else i
                dve.wait_ge(u_hi, base_ + g + 1 + more)
                V.tensor_tensor(ulo[:].rearrange("p k (b n) -> p b k n", b=SB),
                                ps_b[:, 1024:2048].rearrange("p (b k n) -> p b k n", b=SB, k=4),
                                uhi[:].rearrange("p k (b n) -> p b k n", b=SB).bitcast(F32), ALU.subtract).then_inc(u_lo, 1)

            def down_add(dst, t, q, i=None, per=16, first=False, n0=0, banks=2):
                dve.wait_ge(pe_half, q + (0 if i is None else i * per))
                if n0 or i is not None:
                    dve.wait_ge(d_add, n0 + (0 if i is None else i * 4))
                for b in range(SB):
                    ps = bank(banks + 2 * (t % 2) + b)
                    d = dst[:, b, t * NT:(t + 1) * NT]
                    ins = V.tensor_copy(d, ps) if first else V.tensor_tensor(d, d, ps, ALU.add)
                ins.then_inc(d_add, 1)

            c0, q0, _ = seg["mlp"]
            ng = D_FF // NT
            for k in range(16):
                lo(q0 + k, chunk=c0 + k // 2)
                if k == 14:
                    up_lo(0)
            for k in range(16):
                lo(q0 + 16 + k, chunk=c0 + 8 + k // 2)
                if k in (4, 6, 8, 10):
                    down_add(h, k // 2 - 2, q0 + 16 + k - 2)
                if k == 12:
                    up_lo(1)
            with dve.Fori(1, ng - 2) as i:
                for k in range(16):
                    lo(q0 + 16 + k, i, 16, chunk=c0 + 8 + k // 2)
                    if k in (4, 6, 8, 10):
                        t = k // 2 - 2
                        down_add(h, t, q0 + 16 + k - 2, i, n0=t - 3)
                    if k == 12:
                        up_lo(1, i)
            k0 = 16 + 16 * (ng - 2)
            for k in range(16):
                lo(q0 + k0 + k, chunk=c0 + (k0 + k) // 2)
                if k in (4, 6, 8):
                    t = k // 2 - 2
                    down_add(h, t, q0 + k0 + k - 2, n0=4 * (ng - 2) + t - 3)
                if k == 10:
                    down_add(h, 3, q0 + k0 + 8, n0=4 * (ng - 2))
                    up_lo(ng - 1)
                if k in (12, 14):
                    t = k // 2 - 6
                    down_add(h, t, q0 + k0 + 10 + 2 * t, n0=4 * (ng - 1) + t - 3)
            for t in (2, 3):
                down_add(h, t, q0 + k0 + 10 + 2 * t, n0=4 * (ng - 1) + t - 3)

            dve.wait_ge(d_add, 4 * ng)
            normed_rows(4)
            dve.wait_ge(ld["rel"], 16)
            V.memset(relt[32:33, :], 1.0).then_inc(ns["rel"], 1)
            dve.wait_ge(ns["tp"], 1)
            V.tensor_copy(toep[:], ps_a[0:16, 0:512]).then_inc(ns["tpsb"], 1)
            to_lo("n4", gain_t[:, G_MIX:G_MIX + 16])
            for n in range(8):
                dve.wait_ge(ns["flip"], n + 1)
                V.tensor_copy(bias[:, 2 * n:2 * n + 2].rearrange("p h k -> p (h k)"), bank(n % 4)).then_inc(ns["bias"], 1)
            before = looped("in2", T2 // 2, True, proj2)
            tail("tail2", TAIL2, before, proj2, T2 * NT)

            dve.wait_ge(pe_half, q_end("tail2"))
            dve.wait_ge(evicted, seg["special"][2])
            for b in range(SB):
                for r in range(2):
                    c0 = NKV + (2 + 2 * r) * 256
                    V.tensor_copy(kdup[:, b, r], proj2[:, b, c0:c0 + 256].rearrange("p (g d) -> p g d", d=HD2)
                                  .unsqueeze(2).to_broadcast([P, NSA_G, 2, HD2]))
                for v in range(2):
                    ins = V.tensor_copy(kvr[:, b, :, v], proj2[:, b, NKV + v * 256:NKV + (v + 1) * 256]
                                        .rearrange("p (g d) -> p g d", d=HD2))
            ins.then_inc(ns["rows"], 1)
            dve.wait_ge(ns["t1"], 1)
            V.tensor_scalar(nqt[:].rearrange("p x s -> p (x s)"), ps_b[:, :], HD2 ** -0.5, None, ALU.mult).then_inc(ns["t1s"], 1)
            dve.wait_ge(ns["t2"], 1)
            V.tensor_copy(nkt[:].rearrange("p r g s -> p (r g s)"), ps_a[:, :]).then_inc(ns["t2s"], 1)
            dve.wait_ge(ns["t3"], 1)
            V.tensor_copy(rawt[:].rearrange("p g s -> p (g s)"), ps_b[:, 0:1024]).then_inc(ns["t3s"], 1)
            V.memset(hid[:], 0.0).then_inc(ns["hidr"], 1)
            dve.wait_ge(ns["gelu"], 2)
            dve.wait_ge(ns["hidr"], 1)
            for g2 in range(2):
                for x in range(2):
                    ins = V.tensor_copy(hidr[:, g2, 4 * x:4 * x + 4], hid[:, 1, 2 * g2 + x].unsqueeze(1).to_broadcast([P, 4, 16]))
            ins.then_inc(ns["hidr"], 1)
            dve.wait_ge(ns["kv"], 1)
            V.tensor_copy(kct[:], ps_b[:, 0:64])
            for g2 in range(2):
                ins = V.tensor_tensor(vbd[:, g2], ps_b[:, NT + g2 * HD2:NT + (g2 + 1) * HD2].unsqueeze(1).to_broadcast([P, 8, HD2]),
                                      blkmask.unsqueeze(2).to_broadcast([P, 8, HD2]), ALU.mult)
            ins.then_inc(ns["kvs"], 1)
            V.memset(pc[:, 0, :, 7:16], NEG)
            link(V.memset(pc[:, 1, :, 15:16], NEG))
            dve.wait_ge(ns["log"], 1)
            lg = ps_a[:, 0:1024].rearrange("p (t b x n) -> p t b x n", t=2, b=SB, x=16)
            for b in range(SB):
                n = N_CMP if b else 7
                off = 31 if b else 159
                for t in range(2):
                    link(V.tensor_tensor(pc[:, b].rearrange("p (x t) n -> p t x n", t=2)[:, t, :, 0:n],
                                         lg[:, t, b, 0:8, 0:n],
                                         bias[:].rearrange("p (x t) k -> p t x k", t=2)[:, t, :, off:off + 16 * (n - 1) + 1:16], ALU.add))
            cview = pc[:].rearrange("p b h n -> p (b h) n")
            cmask = tmp[:, 0:512].rearrange("p (y n) -> p y n", n=16)
            V.tensor_scalar(cmask, cview, NEG / 2, None, ALU.is_gt)
            link(V.reduce_max(s_cmax, cview, axis=AX))
            V.tensor_tensor(cview, cview, s_cmax.unsqueeze(2).to_broadcast([P, 32, 16]), ALU.subtract).then_inc(ns["sub"], 1)
            dve.wait_ge(ns["exp"], 1)
            link(V.tensor_tensor(cview, cview, cmask, ALU.mult))
            link(V.reduce_sum(s_csum, cview, axis=AX))
            link(V.tensor_scalar(s_csum, s_csum, 1.0, None, ALU.max))
            link(V.reciprocal(s_cinv, s_csum))
            V.tensor_tensor(cview, cview, s_cinv.unsqueeze(2).to_broadcast([P, 32, 16]), ALU.mult).then_inc(ns["p"], 1)
            dve.wait_ge(ns["pps"], 1)
            V.tensor_copy(pct[:].rearrange("p b x n -> p (b x n)"), ps_a[:, 0:512]).then_inc(ns["psb"], 1)
            dve.wait_ge(ns["oc"], 1)
            dve.wait_ge(ns["gate"], 1)
            gt = gates[:].rearrange("p b (h c) -> p b h c", c=3)
            for b in range(SB):
                ins = V.tensor_tensor(mix[:, b, 0:1024].rearrange("p (h d) -> p h d", d=HD2),
                                      ps_b[:, b * 1024:(b + 1) * 1024].rearrange("p (h d) -> p h d", d=HD2),
                                      gt[:, b, :, 0:1].to_broadcast([P, NSA_H, HD2]), ALU.mult)
            ins.then_inc(ns["acc"], 1)
            dve.wait_ge(ns["yps"], 1)
            V.tensor_copy(yt[:].rearrange("p x s -> p (x s)"), ps_a[:, :]).then_inc(ns["ysb"], 1)
            dve.wait_ge(ns["pool"], 1)
            for b in range(SB):
                ins = V.tensor_copy(mix[:, b, 1024:2048], ps_a[:, b * 1024:(b + 1) * 1024])
            ins.then_inc(ns["pooled"], 1)

            def branch(br, g, n):
                def add_bias(lg, pv):
                    bv = bias[:, 4 * g:4 * g + 4].rearrange("p (x t) k -> p t x k", t=2)
                    V.memset(pv[:, :, 0, P:S], NEG)
                    V.tensor_tensor(pv[:, :, 0, 0:P].rearrange("p (t x) k -> p t x k", t=2),
                                    lg[:, :, 0, 0:P].rearrange("p (t x) k -> p t x k", t=2), bv[:, :, :, P:S], ALU.add)
                    link(V.tensor_tensor(pv[:, :, 1].rearrange("p (t x) k -> p t x k", t=2),
                                         lg[:, :, 1].rearrange("p (t x) k -> p t x k", t=2), bv, ALU.add))

                def gated():
                    cv = s_co.rearrange("p (t x b) -> p t x b", t=2, b=SB)
                    for b in range(SB):
                        gv = gt[:, b, 4 * g:4 * g + 4, br + 1].rearrange("p (x t) -> p t x", t=2)
                        link(V.tensor_tensor(cv[:, :, :, b], cv[:, :, :, b], gv, ALU.mult))

                def store(o):
                    tv = tmp[:, 0:512].rearrange("p (b t x d) -> p b t x d", b=SB, t=2, d=HD2)
                    for b in range(SB):
                        ins = V.tensor_tensor(tv[:, b], o[:, :, :, b], co_of(b, HD2), ALU.mult)
                    order[0] += 1
                    ins.then_inc(a_out, 1)
                    order[0] -= 1
                    dve.wait_ge(a_out, 3 + n)
                    for b in range(SB):
                        m = mix[:, b, 256 * g:256 * g + 256].rearrange("p (x t d) -> p t x d", t=2, d=HD2)
                        ins = V.tensor_tensor(m, m, tv[:, b], ALU.add)
                    ins.then_inc(ns["acc"], 1)

                softmax(2 + n, 0, add_bias, gated, HD2, store)

            dve.wait_ge(ns["acc"], 1)
            for n in range(8):
                branch(n // 4, n % 4, n)
                dve.wait_ge(ns["acc"], n + 2)
            to_lo("ap", mix_gain[:])

            dve.wait_ge(merge_gate, 2)

            def merge(t, tile):
                br, n = t % 2, t // 2
                for b in range(SB):
                    dst = mix[:, b, n * NT:(n + 1) * NT]
                    gv = proj2[:, b, NM + br * D + n * NT:NM + br * D + (n + 1) * NT]
                    if br == 0:
                        ins = V.tensor_tensor(dst, bank(2 * (tile % 2) + b), gv, ALU.mult)
                    else:
                        ins = V.tensor_tensor(gv, bank(2 * (tile % 2) + b), gv, ALU.mult)
                ins.then_inc(evicted, 1)
                if br == 1:
                    dve.wait_ge(evicted, tile + 1)
                    for b in range(SB):
                        dst = mix[:, b, n * NT:(n + 1) * NT]
                        ins = V.tensor_tensor(dst, dst, proj2[:, b, NM + D + n * NT:NM + D + (n + 1) * NT], ALU.add)
                    ins.then_inc(y1_done, 1)

            linear("br", 0, 8, merge, kchunks=2)
            to_lo("y1")
            linear("mixo", 0, 4)
            post_norm(0)
            dve.wait_ge(post_done, SB)
            normed_rows(5)
            to_lo("n5", gain_t[:, G_X:G_X + 16])
            linear("xq", 0, 1)
            dve.wait_ge(pe_half, q_end("xq"))
            transposed(2, None, None)
            softmax(10, 0, None, None, HD, store_heads(0))
            to_lo("xo")
            linear("xo", 0, 4, kchunks=1)
            post_norm(1)
            dve.wait_ge(post_done, 2 * SB)
            normed_rows(6)
            to_lo("n6", gain_t[:, G_FFN:G_FFN + 16])
            c0, q0, _ = seg["ffn"]
            gbase, sbase, dbase = D_FF // NT, 2 * (D_FF // NT), 4 * (D_FF // NT)
            ng = D_FF2 // NT

            def up_rows(g, i=None):
                more = 0 if i is None else i
                q = q0 + 16 if g == 0 else q0 + 32 + 24 * (g - 1)
                dve.wait_ge(pe_half, q + more * 24)
                dve.wait_ge(silu_done, sbase + 2 * g + 2 + more * 2)
                dve.wait_ge(u_tps, gbase + g + more)
                for b in range(SB):
                    ins = V.tensor_tensor(u_row[:, b], bank(2 + b), g_row[:, b], ALU.mult)
                ins.then_inc(u_row_done, 1)

            for k in range(32):
                lo(q0 + k, chunk=c0 + k // 2)
                if k == 18:
                    up_rows(0)
                if k == 26:
                    up_lo(0, base_=gbase)
            for k in range(24):
                lo(q0 + 32 + k, chunk=c0 + 16 + k // 2)
                if k == 2:
                    up_rows(1)
                if k in (4, 6, 8, 10):
                    down_add(ybuf, k // 2 - 2, q0 + 32 + k - 2, first=True, banks=4)
                if k == 18:
                    up_lo(1, base_=gbase)
            with dve.Fori(1, ng - 2) as i:
                for k in range(24):
                    lo(q0 + 32 + k, i, 24, chunk=c0 + 16 + k // 2)
                    if k == 2:
                        up_rows(1, i)
                    if k in (4, 6, 8, 10):
                        t = k // 2 - 2
                        down_add(ybuf, t, q0 + 32 + k - 2, i, 24, n0=dbase + t - 3, banks=4)
                    if k == 18:
                        up_lo(1, i, gbase)
            k0 = 32 + 24 * (ng - 2)
            for k in range(16):
                lo(q0 + k0 + k, chunk=c0 + (k0 + k) // 2)
                if k == 2:
                    up_rows(ng - 1)
                if k in (4, 6, 8):
                    t = k // 2 - 2
                    down_add(ybuf, t, q0 + k0 + k - 2, n0=dbase + 4 * (ng - 2) + t - 3, banks=4)
                if k == 10:
                    down_add(ybuf, 3, q0 + k0 + 8, n0=dbase + 4 * (ng - 2), banks=4)
                    up_lo(ng - 1, base_=gbase)
                if k in (12, 14):
                    t = k // 2 - 6
                    down_add(ybuf, t, q0 + k0 + 10 + 2 * t, n0=dbase + 4 * (ng - 1) + t - 3, banks=4)
            for t in (2, 3):
                down_add(ybuf, t, q0 + k0 + 10 + 2 * t, n0=dbase + 4 * (ng - 1) + t - 3, banks=4)
            dve.wait_ge(d_add, dbase + 4 * ng)
            post_norm(2)

        @block.tensor
        def _(pe):
            mm = nc.tensor.matmul

            def half(q, banks, kbs, first, last, cols=NT, i=None, halves=0, xh=None, xl=None):
                xh, xl = (xhi, xlo) if xh is None else (xh, xl)
                more = 0 if i is None else i
                pe.wait_ge(lo_done, q + 1 + more * halves)
                w0, w1_ = whi[:, q % 4], wlo[:, q % 4]
                if cols != NT:
                    w0 = w0.rearrange("p k n -> p (k n)")[:, 0:len(kbs) * cols].rearrange("p (k n) -> p k n", n=cols)
                    w1_ = w1_.rearrange("p k n -> p (k n)")[:, 0:len(kbs) * cols].rearrange("p (k n) -> p k n", n=cols)
                for j, kb in enumerate(kbs):
                    for b in range(SB):
                        o = bank(banks[b])[:, 0:cols]
                        x0, x1 = xh[:, kb, b * P:(b + 1) * P], xl[:, kb, b * P:(b + 1) * P]
                        mm(o, x0, w0[:, j], start=first and j == 0, stop=False)
                        mm(o, x0, w1_[:, j], start=False, stop=False)
                        ins = mm(o, x1, w0[:, j], start=False, stop=last and j == len(kbs) - 1)
                ins.then_inc(pe_half, 1)

            def free(t, i=None, tiles=0):
                if t >= 2:
                    pe.wait_ge(evicted, t - 1 + (0 if i is None else i * tiles))

            def tile(name, t, kchunks=4, kb0=0, i=None, tiles=0, halves=0, tt=None):
                c0, q0, t0 = seg[name]
                g = t0 + t
                free(g, i, tiles)
                n = 2 * kchunks
                for k in range(n):
                    half(q0 + t * n + k, (2 * (g % 2), 2 * (g % 2) + 1), (kb0 + 2 * k, kb0 + 2 * k + 1), k == 0, k == n - 1,
                         i=i, halves=halves)

            def looped(name, pairs):
                tile(name, 0)
                tile(name, 1)
                with pe.Fori(1, pairs) as i:
                    tile(name, 0, i=i, tiles=2, halves=16)
                    tile(name, 1, i=i, tiles=2, halves=16)

            def tail(name, n):
                c0, q0, t0 = seg[name]
                free(t0)
                for k in range(2):
                    half(q0 + k, (2 * (t0 % 2), 2 * (t0 % 2) + 1), tuple(range(8 * k, 8 * k + 8)), k == 0, k == 1, cols=n)

            def quads(name, src, ready):
                q0, n = QUADS[name]
                ready()
                for k in range(n):
                    b, kb = quad_dst(name, k)
                    if q0 + k >= 4:
                        pe.wait_ge(t_lo, q0 + k - 3)
                    o = bank(4 + (q0 + k) % 4)
                    for j in range(4):
                        ins = nc.tensor.transpose(o[:, j * P:(j + 1) * P], src[:, b, (kb + j) * P:(kb + j + 1) * P], ident)
                    ins.then_inc(t_ps, 1)

            def x_ready(name):
                pe.wait_ge(t_lo, sum(QUADS[name]))

            pe.wait_ge(ld["base"], 16)
            pe.wait_ge(ld["gains"], 16 * 8)
            nc.tensor.transpose(bank(7)[:, 0:P], gains[:], ident).then_inc(gain_ps, 1)
            pe.wait_ge(ld["gains2"], 16 * 6)
            nc.tensor.transpose(bank(7)[:, P:P + 16], gains2[:], base[0:16, C_ID:C_ID + 16]).then_inc(gain_ps, 1)
            pe.wait_ge(gain_sb, 1)

            def norm(n):
                quads(f"n{n}", xn, lambda: pe.wait_ge(n_rows, n + 1))
                x_ready(f"n{n}")

            norm(0)
            for t in range(2):
                tile("memkv", t)
            norm(1)
            for t in range(2):
                tile("xkv", t)
            norm(2)
            looped("in1", T1 // 2)
            tail("tail1", TAIL1)

            pe.wait_ge(evicted, seg["wout"][2])
            pe.wait_ge(t_lo, sum(QUADS["n2"]))
            for n, col in enumerate((GQ, GK)):
                for x in range(4):
                    for b in range(SB):
                        ins = nc.tensor.transpose(ps_b[:, n * 1024 + x * S + b * P:n * 1024 + x * S + (b + 1) * P],
                                                  proj1[:, b, col + x * P:col + (x + 1) * P], ident)
            ins.then_inc(gla["tps"], 1)
            for b in range(SB):
                ins = nc.tensor.transpose(ps_a[0:GLA_RANK, b * P:(b + 1) * P], proj1[:, b, GA:GA + GLA_RANK], ident)
            ins.then_inc(gla["gaps"], 1)
            for b in range(SB):
                ins = nc.tensor.transpose(ps_a[0:4, NT + b * P:NT + (b + 1) * P], proj1[:, b, FF:FF + 4], ident)
            ins.then_inc(gla["gaps"], 1)
            pe.wait_ge(gla["gat"], 1)
            pe.wait_ge(ld["gw2"], 32)
            for x in range(4):
                ins = mm(ps_a[:, 1024 + x * S:1024 + (x + 1) * S], gw2[:, x * P:(x + 1) * P], gat[:], start=True, stop=True)
            ins.then_inc(gla["zps"], 1)

            def level(l, q, k, wait):
                wait()
                for x in range(4):
                    for t in range(2):
                        r = slice(t * GLA_DK, (t + 1) * GLA_DK)
                        if l == 7:
                            ins = mm(ps_b[:, t * 1024 + x * P:t * 1024 + (x + 1) * P], k[r, x, 0:P], q[r, x, P:S], start=True, stop=True)
                            continue
                        for b in range(SB):
                            c = t * 1024 + (x * SB + b) * P
                            ins = mm(ps_b[:, c:c + P], k[r, x, b * P:(b + 1) * P], q[r, x, b * P:(b + 1) * P], start=True, stop=True)
                ins.then_inc(gla["s"], 1)

            for l in range(8):
                def ready():
                    pe.wait_ge(gla["qk"], l + 1)
                    if l == 0:
                        pe.wait_ge(gla["tsb"], 1)
                    else:
                        pe.wait_ge(gla["att"], l)
                level(l, gqe[:, l % 2], gke[:, l % 2], ready)
            level(8, gqt[:], gkt[:], lambda: pe.wait_ge(gla["att"], 8))
            pe.wait_ge(gla["att"], 9)
            for hh in range(GLA_H):
                x, t = hh // 2, hh % 2
                for b in range(SB):
                    o = ps_b[:, b * 1024 + hh * P:b * 1024 + (hh + 1) * P]
                    ins = mm(o, att[:, t, x * SB + b], proj1[:, b, GV + hh * P:GV + (hh + 1) * P], start=True, stop=b == 0)
                    if b:
                        ins = mm(o, att10[:, hh], proj1[:, 0, GV + hh * P:GV + (hh + 1) * P], start=False, stop=True)
            ins.then_inc(gla["o"], 1)

            def slot(hh, b):
                return (hh % 2) * 4 + (hh // 2) * 2 + b

            def transposes_of(k, qs, ks):
                for n, src in enumerate((qs, ks)):
                    for x in range(4):
                        for b in range(SB):
                            ins = nc.tensor.transpose(ps_b[:, n * 1024 + x * S + b * P:n * 1024 + x * S + (b + 1) * P],
                                                      src[:, b, x * P:(x + 1) * P], ident)
                ins.then_inc(a_tps, 1)

            def weigh(n, v, width, causal):
                pe.wait_ge(a_exp, n + 1)
                for hh in range(4):
                    for b in range(SB):
                        y = slot(hh, b)
                        for k in range(SB):
                            ins = nc.tensor.transpose(ps_b[:, y * S + k * P:y * S + (k + 1) * P], pr[:, y, k * P:(k + 1) * P], ident)
                ins.then_inc(a_pps, 1)
                pe.wait_ge(a_psb, 2 * (n + 1))
                for hh in range(4):
                    for b in range(SB):
                        y = slot(hh, b)
                        last = 0 if causal and b == 0 else 1
                        for k in range(last + 1):
                            ins = mm(ps_b[:, y * width:(y + 1) * width], pt[:, y, k], v(hh, k), start=k == 0, stop=k == last)
                ins.then_inc(a_o, 1)

            def logits(n, forget):
                for hh in range(4):
                    for b in range(SB):
                        y = slot(hh, b)
                        o = ps_b[:, y * S:(y + 1) * S]
                        ins = mm(o, qt[:, hh, b * P:(b + 1) * P], kt[:, hh], start=True, stop=not forget)
                        if forget:
                            one = base[0:4, C_SEL + hh * S:C_SEL + (hh + 1) * S]
                            mm(o, fct[:, 2, b * P:(b + 1) * P], one, start=False, stop=False)
                            ins = mm(o, one[:, 0:P], fct[:, 3], start=False, stop=True)
                ins.then_inc(a_log, 1)

            pe.wait_ge(gla["out"], 1)
            pe.wait_ge(a_rows, 1)
            transposes_of(0, qn, kn)
            pe.wait_ge(a_tsb, 1)
            pe.wait_ge(fx["c"], 1)
            logits(0, True)
            weigh(0, lambda hh, k: proj1[:, k, FV + hh * HD:FV + (hh + 1) * HD], HD, True)
            pe.wait_ge(a_out, 1)
            pe.wait_ge(a_rows, 2)
            transposes_of(1, qn, kn)
            pe.wait_ge(a_tsb, 2)
            logits(1, False)
            weigh(1, lambda hh, k: mkv[:, k, 512 + hh * HD:512 + (hh + 1) * HD], HD, False)
            pe.wait_ge(a_out, 2)
            quads("o", mix, lambda: pe.wait_ge(o_rows, 1))
            x_ready("o")
            for t in range(4):
                tile("wout", t)
            norm(3)

            c0, q0, _ = seg["mlp"]

            def up_tile(q, i=None, per=0, banks=(0, 1), between=None):
                for k in range(8):
                    half(q + k, banks, (2 * k, 2 * k + 1), k == 0, k == 7, i=i, halves=per)
                    if k == 2 and between is not None:
                        between()

            def u_transposes(g, i=None, base_=0):
                more = 0 if i is None else i
                pe.wait_ge(u_row_done, base_ + g + 1 + more)
                if base_ or g or i is not None:
                    pe.wait_ge(u_lo, base_ + g + more)
                for b in range(SB):
                    for j in range(4):
                        ins = nc.tensor.transpose(ps_b[:, 1024 + (b * 4 + j) * P:1024 + (b * 4 + j + 1) * P],
                                                  u_row[:, b, j * P:(j + 1) * P], ident)
                ins.then_inc(u_tps, 1)

            def down_tile(q, t, added, i=None, per=0, banks=2, add_step=4):
                if added is not None:
                    pe.wait_ge(d_add, added + (0 if i is None else i * add_step))
                for k in range(2):
                    half(q + k, (banks + 2 * (t % 2), banks + 2 * (t % 2) + 1), (2 * k, 2 * k + 1), k == 0, k == 1, i=i, halves=per,
                         xh=uhi, xl=ulo)

            def mlp_downs(q, g, i=None):
                more = 0 if i is None else i
                pe.wait_ge(u_lo, g + 1 + more)
                for t in range(4):
                    added = 4 * g + t - 1
                    down_tile(q + 2 * t, t, added if added > 0 else None, i, 16)

            ng = D_FF // NT
            pe.wait_ge(evicted, seg["mlp"][2])
            up_tile(q0)
            pe.wait_ge(u_row_done, 1)
            up_tile(q0 + 8, between=lambda: u_transposes(0))
            mlp_downs(q0 + 16, 0)
            pe.wait_ge(u_row_done, 2)
            up_tile(q0 + 24, between=lambda: u_transposes(1))
            with pe.Fori(1, ng - 2) as i:
                pe.wait_ge(u_lo, i + 1)
                for t in range(4):
                    down_tile(q0 + 16 + 2 * t, t, t - 1, i, 16)
                pe.wait_ge(u_row_done, i + 2)
                up_tile(q0 + 24, i, 16, between=lambda: u_transposes(1, i))
            k0 = 16 + 16 * (ng - 2)
            mlp_downs(q0 + k0, ng - 2)
            pe.wait_ge(d_add, 4 * (ng - 1))
            u_transposes(ng - 1)
            mlp_downs(q0 + k0 + 8, ng - 1)

            pe.wait_ge(ld["hot"], 16)
            pe.wait_ge(ns["rel"], 1)
            pe.wait_ge(d_add, 4 * ng)
            mm(ps_a[0:16, 0:512], relt[0:33, :], hot[0:33, 0:512], start=True, stop=True).then_inc(ns["tp"], 1)
            norm(4)
            pe.wait_ge(ns["tpsb"], 1)
            pe.wait_ge(ld["flip"], 16 * NSA_H)
            for n in range(8):
                if n >= 4:
                    pe.wait_ge(ns["bias"], n - 3)
                mm(bank(n % 4), hot[:, 512:512 + P], flip[:, 2 * n:2 * n + 2].rearrange("p h k -> p (h k)"),
                   start=True, stop=True).then_inc(ns["flip"], 1)
            pe.wait_ge(ns["bias"], 8)
            looped("in2", T2 // 2)
            tile("in2", T2 - 1)
            tail("tail2", TAIL2)

            pe.wait_ge(evicted, seg["special"][2])
            for x in range(8):
                for b in range(SB):
                    ins = nc.tensor.transpose(ps_b[:, x * S + b * P:x * S + (b + 1) * P],
                                              proj2[:, b, NQ + x * P:NQ + (x + 1) * P], ident)
            ins.then_inc(ns["t1"], 1)
            pe.wait_ge(ns["rows"], 1)
            for r in range(2):
                for g in range(NSA_G):
                    for b in range(SB):
                        ins = nc.tensor.transpose(ps_a[:, (r * 4 + g) * S + b * P:(r * 4 + g) * S + (b + 1) * P],
                                                  kdup[:, b, r, g].rearrange("p x d -> p (x d)"), ident)
            ins.then_inc(ns["t2"], 1)
            pe.wait_ge(ns["t1s"], 1)
            for g in range(NSA_G):
                for b in range(SB):
                    ins = nc.tensor.transpose(ps_b[:, g * S + b * P:g * S + (b + 1) * P],
                                              kvr[:, b, g].rearrange("p v d -> p (v d)"), ident)
            ins.then_inc(ns["t3"], 1)
            pe.wait_ge(ns["t3s"], 1)
            pe.wait_ge(ns["t2s"], 1)
            pe.wait_ge(ld["cmp"], 16 * 5)
            for s in range(2):
                pe.wait_ge(sp_loaded[s], 32)
            ncol = NSA_G * N_CMP
            for kv in range(2):
                r = slice(kv * HD2, (kv + 1) * HD2)
                for l in range(CMP_LEN):
                    w = raw[r, (special0 + l // 16) % SLOTS].rearrange("p k n -> p (k n)")[:, (l % 16) * P:(l % 16 + 1) * P]
                    o = ps_a[:, kv * NT:kv * NT + ncol]
                    mm(o, w, rawt[r, :, l:l + CMP_STRIDE * (N_CMP - 1) + 1:CMP_STRIDE], start=l == 0, stop=False)
                    ins = mm(o, w, pet[r, l:l + 1].to_broadcast([HD2, ncol]), start=False, stop=l == CMP_LEN - 1)
            ins.then_inc(ns["hid"], 1)
            pe.wait_ge(ns["hidr"], 2)
            mm(ps_b[:, 0:64], cw2[:, 0:2].rearrange("p x d -> p (x d)"), hid[:, 0].rearrange("p g n -> p (g n)"), start=True, stop=True)
            for g2 in range(2):
                ins = mm(ps_b[:, NT + g2 * HD2:NT + (g2 + 1) * HD2], hidr[:, g2].rearrange("p x n -> p (x n)"), cw2[:, 2],
                         start=True, stop=True)
            ins.then_inc(ns["kv"], 1)
            pe.wait_ge(ns["kvs"], 1)
            for hh in range(NSA_H):
                r = slice((hh % 2) * HD2, (hh % 2 + 1) * HD2)
                for b in range(SB):
                    c = (hh % 2) * 512 + (b * 16 + hh // 2) * 16
                    ins = mm(ps_a[:, c:c + N_CMP], nqt[r, hh // 2, b * P:(b + 1) * P], kct[r, (hh // 4) * 16:(hh // 4) * 16 + N_CMP],
                             start=True, stop=True)
            ins.then_inc(ns["log"], 1)
            pe.wait_ge(ns["p"], 1)
            for b in range(SB):
                for g2 in range(2):
                    ins = nc.tensor.transpose(ps_a[:, (b * 2 + g2) * P:(b * 2 + g2 + 1) * P],
                                              pc[:, b, 8 * g2:8 * g2 + 8].rearrange("p h n -> p (h n)"), ident)
            ins.then_inc(ns["pps"], 1)
            pe.wait_ge(ns["psb"], 1)
            for b in range(SB):
                for g2 in range(2):
                    ins = mm(bank(4 + b * 2 + g2), pct[:, b, g2], vbd[:, g2].rearrange("p h d -> p (h d)"), start=True, stop=True)
            ins.then_inc(ns["oc"], 1)
            pe.wait_ge(sp_loaded[2], 16)
            band = raw[:, (special0 + 2) % SLOTS].rearrange("p k n -> p (k n)").rearrange("p (b w s) -> p b w s", b=SB, w=4)
            for x in range(8):
                for b in range(SB):
                    ins = mm(ps_a[:, x * S:(x + 1) * S], proj2[:, b, NU + x * P:NU + (x + 1) * P], band[:, b, x // 2],
                             start=b == 0, stop=b == SB - 1)
            ins.then_inc(ns["yps"], 1)
            pe.wait_ge(ns["ysb"], 1)
            pe.wait_ge(sp_loaded[3], 16)
            wp = raw[:, (special0 + 3) % SLOTS].rearrange("p k n -> p (k n)").rearrange("p (g k n) -> p g k n", g=4, k=2)
            for b in range(SB):
                for g in range(4):
                    for k in range(2):
                        ins = mm(ps_a[:, b * 1024 + g * S:b * 1024 + (g + 1) * S], yt[:, 2 * g + k, b * P:(b + 1) * P], wp[:, g, k],
                                 start=k == 0, stop=k == 1)
            ins.then_inc(ns["pool"], 1)
            for n in range(8):
                br, g = n // 4, n % 4
                pe.wait_ge(ns["acc"], 1)
                if n:
                    pe.wait_ge(a_out, 2 + n)
                for hh in range(4):
                    r = slice((hh % 2) * HD2, (hh % 2 + 1) * HD2)
                    for b in range(SB):
                        y = slot(hh, b)
                        keys = P if b == 0 else S
                        ins = mm(ps_b[:, y * S:y * S + keys], nqt[r, 2 * g + hh // 2, b * P:(b + 1) * P], nkt[r, br, g, 0:keys],
                                 start=True, stop=True)
                ins.then_inc(a_log, 1)
                c0 = NKV + (3 + 2 * br) * 256 + g * HD2
                weigh(2 + n, lambda hh, k: proj2[:, k, c0:c0 + HD2], HD2, True)
            pe.wait_ge(a_out, 10)

            def rows_ready():
                pe.wait_ge(ns["acc"], 9)
                pe.wait_ge(ns["pooled"], 1)

            quads("ap", mix, rows_ready)
            x_ready("ap")
            for t in range(8):
                tile("br", t, 2, 8 * (t % 2))
            quads("y1", mix, lambda: pe.wait_ge(y1_done, 4))
            x_ready("y1")
            for t in range(4):
                tile("mixo", t)
            norm(5)
            tile("xq", 0)
            pe.wait_ge(evicted, seg["xo"][2])
            transposes_of(2, qx, xkv)
            pe.wait_ge(a_tsb, 3)
            logits(10, False)
            weigh(10, lambda hh, k: xkv[:, k, 512 + hh * HD:512 + (hh + 1) * HD], HD, False)
            quads("xo", mix, lambda: pe.wait_ge(a_out, 11))
            x_ready("xo")
            for t in range(4):
                tile("xo", t, 1)
            norm(6)

            c0, q0, _ = seg["ffn"]
            gbase, sbase, dbase = D_FF // NT, 2 * (D_FF // NT), 4 * (D_FF // NT)
            ng = D_FF2 // NT
            pe.wait_ge(evicted, seg["ffn"][2])
            up_tile(q0)
            up_tile(q0 + 8, banks=(2, 3))
            pe.wait_ge(silu_done, sbase + 2)
            up_tile(q0 + 16, between=None)
            pe.wait_ge(u_row_done, gbase + 1)
            u_transposes(0, base_=gbase)
            up_tile(q0 + 24, banks=(2, 3))

            def ffn_downs(q, g, i=None):
                pe.wait_ge(u_lo, gbase + g + 1 + (0 if i is None else i))
                for t in range(4):
                    down_tile(q + 2 * t, t, dbase + 4 * g + t - 1, i, 24, banks=4)

            def ffn_group(g, i=None):
                more = 0 if i is None else i
                ffn_downs(q0 + 32 + 24 * g, g, i)
                pe.wait_ge(silu_done, sbase + 2 * g + 4 + more * 2)
                up_tile(q0 + 40 + 24 * g, i, 24)
                u_tr(g, i)
                up_tile(q0 + 48 + 24 * g, i, 24, banks=(2, 3))

            def u_tr(g, i=None):
                pe.wait_ge(d_add, dbase + 4 * g + 4 + (0 if i is None else i * 4))
                u_transposes(g + 1, i, gbase)

            ffn_group(0)
            with pe.Fori(1, ng - 2) as i:
                ffn_group(0, i)
            k0 = 32 + 24 * (ng - 2)
            ffn_downs(q0 + k0, ng - 2)
            u_tr(ng - 2)
            ffn_downs(q0 + k0 + 8, ng - 1)


_INS = ["x", "mem", "attn_norm_g", "w_in", "gla_a_w2", "gla_a_b", "fox_f_b", "fox_q_norm_g", "fox_k_norm_g", "mem_norm_g",
        "w_mem_kv", "mem_q_norm_g", "mem_k_norm_g", "out_norm_g", "w_out", "mlp_norm_g", "w_up", "w_down", "mem_2", "rel_bias_2",
        "ln_mix_pre_2", "ln_mix_post_2", "ln_x_pre_2", "ln_x_post_2", "ln_mem_2", "ln_ffn_pre_2", "ln_ffn_post_2", "w_in_2",
        "cmp_pe_2", "cmp_w1_2", "cmp_w2_2", "w_pool_2", "pool_scale_2", "w_br_attn_2", "w_br_pool_2", "w_mix_out_2", "w_xq_2",
        "w_xkv_2", "w_xo_2", "w_gate_2", "w_up_2", "w_down_2"]


def kernel(**inputs):
    import concourse.bacc as _bacc
    from concourse.bass_utils import run_bass_kernel_spmd as _run

    nc = _bacc.Bacc("TRN2", target_bir_lowering=False, num_devices=1, dynamic_dma_scratch_size=1024)
    arrays, args = {}, {}
    for name in _INS:
        v = np.ascontiguousarray(inputs[name])
        arrays[f"in_{name}"] = v
        args[name] = nc.dram_tensor(f"in_{name}", v.shape, mybir.dt.from_np(v.dtype), kind="ExternalInput").ap()
    consts = []
    for name, v in zip(("base", "bands", "hot"), shape_constants()):
        arrays[f"const_{name}"] = v
        consts.append(nc.dram_tensor(f"const_{name}", v.shape, F32, kind="ExternalInput").ap())
    out = nc.dram_tensor("out", (1, S, D), F32, kind="ExternalOutput").ap()
    hybrid_blocks_kernel(nc, args, *consts, out)
    r = _run(nc, [arrays], core_ids=[0])
    return r.results[0]["out"]
```

```python
from contextlib import ExitStack

import numpy as np

import concourse.bass as bass
from concourse import mybir

F32 = mybir.dt.float32
F32R = mybir.dt.float32r
U32 = mybir.dt.uint32
ACT = mybir.ActivationFunctionType
ALU = mybir.AluOpType
AX = mybir.AxisListType.X

P = 128
S = 256
SB = S // P
D = 2048
KB = D // P
NT = 512
CK = 4
SLOTS = 4
EPS = 1e-6
NEG = -1e30

GLA_H, GLA_DK, GLA_DV, GLA_RANK, GLA_TAU = 8, 64, 128, 16, 16.0
HD = 128
GQ, GK, GV, GG = 0, 512, 1024, 2048
GA = 3072
FQ = GA + GLA_RANK
FK, FV, FG = FQ + 512, FQ + 1024, FQ + 1536
FF = FQ + 2048
MQ = FF + 4
MG = MQ + 512
IN1 = MG + 512
T1 = IN1 // NT
TAIL1 = IN1 - T1 * NT
D_FF = 4 * D
LEVELS = [1, 2, 4, 8, 16, 32, 64]

NSA_H, NSA_G, HD2 = 16, 4, 64
NQ, NKV, NGL = 0, 1024, 2560
NU = NGL + 3 * NSA_H
NM = NU + 1024
IN2 = NM + 2 * D
T2 = IN2 // NT
TAIL2 = IN2 - T2 * NT
CMP_LEN, CMP_STRIDE = 32, 16
N_CMP = (S - CMP_LEN) // CMP_STRIDE + 1
WINDOWS = (2, 4, 8, 16)
REL_BUCKETS, REL_MAX = 32, 2048
D_FF2 = 5632

G_ATTN, G_MEM, G_MLP, G_MIX, G_X, G_MEM2, G_FFN, G_OUT = (16 * n for n in range(8))
B_GLA, G_FQ, G_FK, G_MQ, G_MK, G_POOL = 0, 4, 5, 6, 7, 8


def shape_constants():
    j, i = np.arange(P)[:, None], np.arange(P)[None, :]
    ident = (j == i).astype(np.float32)
    masks = [((j // (2 * w) == i // (2 * w)) & (j % (2 * w) < w) & (i % (2 * w) >= w)).astype(np.float32)
             for w in LEVELS] + [ident]
    q = np.arange(S).reshape(SB, P).T[:, :, None]
    causal = np.where(q >= np.arange(S), 0.0, NEG).astype(np.float32).reshape(P, -1)
    sel = np.zeros((P, 4, S), np.float32)
    for h in range(4):
        sel[h, h] = 1.0
    blocks = (np.arange(P)[:, None] // 16 == np.arange(8)).astype(np.float32)
    base = np.concatenate([ident, blocks, *masks, causal, sel.reshape(P, -1)], 1)
    s0, s1 = np.arange(S)[:, None], np.arange(S)[None, :]
    bands = np.stack([((s1 - s0 >= 0) & (s1 - s0 < w)) / np.minimum(s1 + 1, w) - (s0 == s1) for w in WINDOWS])
    bands = bands.astype(np.float32).reshape(4, SB, P, S).transpose(2, 1, 0, 3).reshape(P, -1)
    y = np.arange(512)
    n = np.maximum(255 - y, 0)
    exact = REL_BUCKETS // 2
    large = exact + (np.log(np.maximum(n, 1).astype(np.float32) / np.float32(exact)) / np.float32(np.log(REL_MAX / exact))
                     * np.float32(REL_BUCKETS - exact)).astype(np.int32)
    bucket = np.where(n < exact, n, np.minimum(large, REL_BUCKETS - 1))
    hot = np.zeros((P, 512 + P), np.float32)
    hot[:REL_BUCKETS, :512] = np.arange(REL_BUCKETS)[:, None] == bucket
    hot[REL_BUCKETS, :512] = np.where(y > 255, NEG, 0.0)
    hot[:, 512:] = ident[::-1]
    return base, np.ascontiguousarray(bands), hot


C_ID, C_BLK = 0, P
C_MASK = C_BLK + 8
C_CAUSAL = C_MASK + 8 * P
C_SEL = C_CAUSAL + SB * S
C_ALL = C_SEL + 4 * S


def hybrid_blocks_kernel(nc, a, c_base, c_bands, c_hot, out):
    es = ExitStack()
    with es:
        place = [1152]

        def sb(name, shape, dt=F32, at=None):
            size = 4 * int(np.prod(shape[1:]))
            if at is None:
                at = place[0]
                place[0] += (size + 31) // 32 * 32
            t = nc.alloc_sbuf_tensor_at(name, shape, dt, offset=at)
            spots[name] = at
            return t

        spots = {}

        def sem(name):
            return es.enter_context(nc.semaphore(name))

        raw = sb("raw", [P, SLOTS, CK, NT])
        whi = sb("whi", [P, 4, 2, NT], F32R)
        wlo = sb("wlo", [P, 4, 2, NT], F32R)
        xhi = sb("xhi", [P, KB, S], F32R)
        xlo = sb("xlo", [P, KB, S], F32R)
        h = sb("h", [P, SB, D])
        mix = sb("mix", [P, SB, D])
        proj_at = place[0]
        proj1 = sb("proj1", [P, SB, IN1], at=proj_at)
        proj2 = sb("proj2", [P, SB, IN2])
        xkv = sb("xkv", [P, SB, 1024])
        base_at = place[0]
        base = sb("base", [P, C_ALL])
        mkv = sb("mkv", [P, SB, 1024])
        gains = sb("gains", [P, P])
        gain_t = sb("gain_t", [P, P])
        gains2 = sb("gains2", [16, P])
        gain2_t = sb("gain2_t", [P, 16])
        mix_gain = sb("mix_gain", [P, 16])
        small = sb("small", [P, 256])
        stage_t = sb("stage_t", [P, 2, NT])
        ybuf = sb("ybuf", [P, SB, D], at=proj_at)
        mem_rows = sb("mem_rows", [P, 2, SB, D], at=proj_at)
        junk = sb("junk", [P, D], at=proj_at + 49152)
        post_gain = sb("post_gain", [P, D], at=proj_at + 16384)
        u_row = sb("u_row", [P, SB, NT], at=proj_at + 24576)
        uhi = sb("uhi", [P, 4, S], F32R, at=proj_at + 28672)
        ulo = sb("ulo", [P, 4, S], F32R, at=proj_at + 53248)
        g_row = sb("g_row", [P, SB, NT], at=proj_at + 57344)
        wa = spots["xhi"]
        qn = sb("qn", [P, SB, 512], at=wa)
        kn = sb("kn", [P, SB, 512], at=wa + 4096)
        qt = sb("qt", [P, 4, S], at=wa + 8192)
        kt = sb("kt", [P, 4, S], at=wa + 12288)
        pr = sb("pr", [P, 8, S], at=wa + 16384)
        pt = sb("pt", [P, 8, 2, P], at=wa + 24576)
        gqt = sb("gqt", [P, 4, S], at=wa)
        gkt = sb("gkt", [P, 4, S], at=wa + 4096)
        gbt = sb("gbt", [P, 4, S], at=wa + 8192)
        gl = sb("gl", [P, 4, S], at=wa + 12288)
        ge = sb("ge", [P, 2, 4, S], at=wa + 16384)
        att = sb("att", [P, 2, 8, P], at=wa + 24576)
        wb = spots["whi"]
        gqe = sb("gqe", [P, 2, 4, S], at=wb)
        gke = sb("gke", [P, 2, 4, S], at=wb + 8192)
        att10 = sb("att10", [P, 8, P], at=wb + 16384)
        gat = sb("gat", [GLA_RANK, S], at=wb + 20480)
        gw2 = sb("gw2", [GLA_RANK, 512], at=wb + 21504)
        g_ones = sb("g_ones", [P, S], at=wb + 23552)
        fct = sb("fct", [4, 4, S], at=wb + 24576)
        fbias = sb("fbias", [4, 1], at=wb + 28672)
        nqt = sb("nqt", [P, 8, S], at=wa)
        nkt = sb("nkt", [P, NSA_G, 2, S], at=spots["xlo"] + 8192)
        kdup = sb("kdup", [P, SB, 4, NSA_G, 2, HD2], at=spots["mix"])
        yt = sb("yt", [P, 8, S], at=spots["mix"])
        cmp_o = sb("cmp_o", [P, 8, S], at=spots["mix"] + 8192)
        bias = sb("bias", [P, NSA_H, S], at=base_at + 4 * C_MASK)
        hot = sb("hot", [P, 512 + P], at=proj_at)
        relt = sb("relt", [P, 16], at=proj_at + 2560)
        toep = sb("toep", [16, 512], at=proj_at + 2688)
        flip = sb("flip", [P, NSA_H, S], at=proj_at + 32768)
        xpe = sb("xpe", [P, 2, CMP_LEN // 2, NSA_G, N_CMP], at=wb)
        pet = sb("pet", [P, 2, CMP_LEN // 2], at=wb + 7680)
        cw2 = sb("cw2", [P, 3, HD2], at=wb + 7936)
        hid = sb("hid", [P, 2, NSA_G, 16], at=wb + 8704)
        hidr = sb("hidr", [P, 2, 8, 16], at=wb + 9216)
        kcbd = sb("kcbd", [P, NSA_G, 2, 16], at=wb + 10240)
        vbd = sb("vbd", [P, 2, 8, HD2], at=wb + 10752)
        pc = sb("pc", [P, SB, NSA_H, 16], at=wb + 14848)
        pct = sb("pct", [P, SB, 2, P], at=wb + 16896)
        cmask = sb("cmask", [P, SB * NSA_H, 16], at=wb + 18944)
        prob = sb("prob", [P, 2, 2, 768], at=wb)
        probt = sb("probt", [P, 2, 1536], at=wb + 12288)
        diag = sb("diag", [P, 2, 8, P], at=wb + 24576)
        qx = sb("qx", [P, SB, 512], at=proj_at + 57344 - 4096)
        assert place[0] <= nc.sbuf_usable_end, place[0]
        assert base_at + 4 * C_MASK + 16384 <= spots["gains"]

        ident = base[:, C_ID:C_ID + P]
        blkmask = base[:, C_BLK:C_BLK + 8]

        ps_a = es.enter_context(nc.psum_tensor("ps_a", [P, 4 * NT], F32))
        ps_b = es.enter_context(nc.psum_tensor("ps_b", [P, 4 * NT], F32))

        def bank(n):
            t = ps_a if n < 4 else ps_b
            return t[:, (n % 4) * NT:(n % 4 + 1) * NT]

        vdup = proj2[:, :, NQ:NQ + 1024].rearrange("p b (r g x d) -> p b r g x d", r=2, g=NSA_G, x=2)
        gates = proj2[:, :, NGL:NU]

        toep_dram = nc.dram_tensor("toep_scratch", [16, 512], F32, kind="Internal").ap()

        w_loaded = [sem(f"w_loaded{i}") for i in range(SLOTS)]
        sp_loaded = [sem(f"sp_loaded{i}") for i in range(4)]
        hi_done, lo_done, pe_half, evicted = sem("hi_done"), sem("lo_done"), sem("pe_half"), sem("evicted")
        ld = {n: sem(f"ld_{n}") for n in ("ident", "gains", "gains2", "base", "gw2", "hot", "rel",
                                          "toep", "flip", "cmp", "gain")}
        gain_ps, gain_sb = sem("gain_ps"), sem("gain_sb")
        n_sq, n_var, n_std, n_rstd = sem("norm_sq"), sem("norm_var"), sem("norm_std"), sem("norm_rstd")
        t_ps, t_y, t_hi, t_lo = sem("t_ps"), sem("t_y"), sem("t_hi"), sem("t_lo")
        dve_order, act_order, pool_order = sem("dve_order"), sem("act_order"), sem("pool_order")
        post_sq, post_var, post_std, post_done = sem("post_sq"), sem("post_var"), sem("post_std"), sem("post_done")
        a_var, a_std, a_rows, a_tps, a_tsb = (sem(n) for n in ("att_var", "att_std", "att_rows", "att_tps", "att_tsb"))
        a_log, a_sub, a_exp, a_pps, a_psb, a_o, a_out = (
            sem(n) for n in ("att_logits", "att_sub", "att_exp", "att_pps", "att_psb", "att_o", "att_out"))
        gla = {n: sem("gla_" + n) for n in ("gaps", "gat", "zps", "z", "abs", "exp", "ln", "b", "d", "e", "qk",
                                            "tps", "tsb", "s", "att", "o", "out")}
        fx = {n: sem("fox_" + n) for n in ("tps", "z", "abs", "exp", "ln", "c")}
        gate_done, o_var, o_std, o_rows = sem("gate_done"), sem("o_var"), sem("o_std"), sem("o_rows")
        u_row_done, u_tps, u_hi, u_lo, d_add = sem("u_row"), sem("u_tps"), sem("u_hi"), sem("u_lo"), sem("down_added")
        ns = {n: sem("nsa_" + n) for n in ("rel", "tp", "tpsb", "flip", "bias", "dup", "t1", "t1s", "tk", "xpe", "t2", "t2s",
                                           "hid", "gelu", "hidr", "kv", "kvs", "log", "sub", "exp", "p", "pps", "psb",
                                           "oc", "cmp", "gate", "yps", "ysb", "pool", "pooled", "pool_hi", "vdup")}
        nb = {n: sem("branch_" + n) for n in ("logits", "max", "exp", "diag", "pt", "pts", "pv", "y", "hi", "lo")}
        merge_gate, y1_done = sem("merge_gate"), sem("y1_done")
        silu_done = sem("silu_done")
        stored = sem("stored")

        seg = {}
        at_c, at_q, at_t = 0, 0, 0
        q_after = []
        special0 = None
        for name, tiles, chunks in (("memkv", 2, 4), ("xkv", 2, 4), ("in1", T1, 4), ("tail1", 1, 1), ("wout", 4, 4),
                                    ("mlp", 16, 8), ("in2", T2, 4), ("tail2", 1, 1), ("special", 4, 1), ("br", 8, 2),
                                    ("mixo", 4, 4), ("xq", 1, 4), ("xo", 4, 1), ("ffn", 11, 12)):
            seg[name] = (at_c, at_q, at_t)
            n = tiles * chunks
            if name == "special":
                special0 = at_c
            q_after += [at_q + (0 if name == "special" else 2 * (k + 1)) for k in range(n)]
            at_c += n
            if name != "special":
                at_q += 2 * n
            if name not in ("mlp", "ffn", "special"):
                at_t += tiles
        seg["end"] = (at_c, at_q, at_t)

        def loads_before(c):
            return c // SLOTS - (1 if c >= special0 + 4 else 0)

        block = es.enter_context(nc.Block())

        w1 = {"memkv": a["w_mem_kv"], "xkv": a["w_xkv_2"][0], "in1": a["w_in"], "wout": a["w_out"],
              "in2": a["w_in_2"][0], "mixo": a["w_mix_out_2"][0], "xq": a["w_xq_2"][0], "xo": a["w_xo_2"][0]}

        @block.sync
        def _(sp):
            def load(c, src, dst=None, i=None, chunks=0):
                more = 0 if i is None else i
                if special0 + 4 <= c < special0 + 8:
                    s = c - 4 - special0
                    if s < 2:
                        sp.wait_ge(ns["hid"], 1)
                    elif s == 2:
                        sp.wait_ge(ns["yps"], 1)
                    else:
                        sp.wait_ge(ns["pool"], 1)
                elif c >= SLOTS:
                    sp.wait_ge(lo_done, q_after[c - SLOTS] + more * (2 * chunks))
                d = raw[:, c % SLOTS] if dst is None else dst
                sp.dma_start(d, src).then_inc(w_loaded[c % SLOTS], 16)

            def rows(w, r0, n, c0, cols=NT):
                return w[r0:r0 + n, c0:c0 + cols].rearrange("(k p) n -> p k n", p=P)

            def linear(name, first, last, kchunks=4):
                c0 = seg[name][0]
                for t in range(first, last):
                    for k in range(kchunks):
                        load(c0 + t * kchunks + k, rows(w1[name], k * CK * P, CK * P, t * NT))

            def looped(name, pairs):
                c0 = seg[name][0]
                linear(name, 0, 2)
                with sp.Fori(1, pairs) as i:
                    for j in range(8):
                        load(c0 + j, w1[name][(j % 4) * CK * P:(j % 4 + 1) * CK * P,
                                              bass.ds(i * (2 * NT) + (j // 4) * NT, NT)].rearrange("(k p) n -> p k n", p=P),
                             i=i, chunks=8)

            def tail(name, w, cols, n):
                c = seg[name][0]
                load(c, w[:, cols:cols + n].rearrange("(k p) n -> p k n", p=P),
                     raw[:, c % SLOTS].rearrange("p k n -> p (k n)")[:, 0:KB * n].rearrange("p (k n) -> p k n", n=n))

            linear("memkv", 0, 2)
            linear("xkv", 0, 2)
            looped("in1", T1 // 2)
            tail("tail1", a["w_in"], T1 * NT, TAIL1)
            linear("wout", 0, 4)

            c0 = seg["mlp"][0]

            def mlp_up(c, g, i=None):
                for k in range(4):
                    cols = slice(g * NT, (g + 1) * NT) if i is None else bass.ds(i * NT + g * NT, NT)
                    load(c + k, a["w_up"][k * CK * P:(k + 1) * CK * P, cols].rearrange("(k p) n -> p k n", p=P), i=i, chunks=8)

            def mlp_down(c, g, w, i=None, chunks=8):
                for t in range(4):
                    r = slice(g * NT, (g + 1) * NT) if i is None else bass.ds(i * NT + g * NT, NT)
                    load(c + t, w[r, t * NT:(t + 1) * NT].rearrange("(k p) n -> p k n", p=P), i=i, chunks=chunks)

            ng = D_FF // NT
            mlp_up(c0, 0)
            mlp_up(c0 + 4, 1)
            with sp.Fori(0, ng - 2) as i:
                mlp_down(c0 + 8, 0, a["w_down"], i)
                mlp_up(c0 + 12, 2, i)
            mlp_down(c0 + 8 * ng - 8, ng - 2, a["w_down"])
            mlp_down(c0 + 8 * ng - 4, ng - 1, a["w_down"])

            looped("in2", T2 // 2)
            linear("in2", T2 - 1, T2)
            tail("tail2", a["w_in_2"][0], T2 * NT, TAIL2)
            for s in range(4):
                c = special0 + s
                sp.wait_ge(lo_done, q_after[c - SLOTS])
                slot = raw[:, c % SLOTS]
                flat = slot.rearrange("p k n -> p (k n)")
                if s < 2:
                    sp.dma_start(flat.rearrange("p (l n) -> p l n", n=P),
                                 a["cmp_w1_2"][0, s].rearrange("(l p) n -> p l n", p=P)).then_inc(sp_loaded[s], 16)
                elif s == 2:
                    sp.dma_start(flat, c_bands).then_inc(sp_loaded[s], 16)
                else:
                    sp.dma_start(flat.rearrange("p (g k n) -> p (g k) n", g=4, k=2),
                                 a["w_pool_2"][0].rearrange("g (k p) n -> p (g k) n", p=P)).then_inc(sp_loaded[s], 16)
            c0 = seg["br"][0]
            for t in range(4):
                for k in range(2):
                    load(c0 + 4 * t + k, rows(a["w_br_attn_2"][0], k * 512, 512, t * NT))
                for k in range(2):
                    load(c0 + 4 * t + 2 + k, rows(a["w_br_pool_2"][0], k * 512, 512, t * NT))
            linear("mixo", 0, 4)
            linear("xq", 0, 1)
            linear("xo", 0, 4, 1)

            c0 = seg["ffn"][0]

            def ffn_in(c, g, i=None):
                for n, w in enumerate((a["w_gate_2"][0], a["w_up_2"][0])):
                    for k in range(4):
                        cols = slice(g * NT, (g + 1) * NT) if i is None else bass.ds(i * NT + g * NT, NT)
                        load(c + 4 * n + k, w[k * CK * P:(k + 1) * CK * P, cols].rearrange("(k p) n -> p k n", p=P),
                             i=i, chunks=12)

            ng = D_FF2 // NT
            wd = a["w_down_2"][0]
            ffn_in(c0, 0)
            ffn_in(c0 + 8, 1)
            with sp.Fori(0, ng - 2) as i:
                mlp_down(c0 + 16, 0, wd, i, 12)
                ffn_in(c0 + 20, 2, i)
            mlp_down(c0 + 12 * ng - 8, ng - 2, wd)
            mlp_down(c0 + 12 * ng - 4, ng - 1, wd)

            for b in range(SB):
                for t in range(4):
                    sp.wait_ge(post_done, 16 + 4 * b + t + 1)
                    sp.dma_start(out[0, b * P:(b + 1) * P, t * NT:(t + 1) * NT], h[:, b, t * NT:(t + 1) * NT]).then_inc(stored, 16)
            sp.wait_ge(stored, 16 * SB * 4)

        s_sq, s_var, s_std, s_rstd = (small[:, 2 * n:2 * n + 2] for n in range(4))
        s_pp = small[:, 8:16]
        s_psq, s_pvar, s_pstd, s_prstd = (small[:, 88 + 2 * n:90 + 2 * n] for n in range(4))
        s_ass, s_astd, s_arstd = small[:, 16:32], small[:, 32:48], small[:, 48:64]
        s_max, s_sum, s_co = small[:, 64:72], small[:, 72:80], small[:, 80:88]
        s_oss, s_ostd, s_orstd = small[:, 96:128], small[:, 128:160], small[:, 160:192]
        s_cmax, s_csum, s_cinv = small[:, 96:128], small[:, 128:160], small[:, 160:192]

        s_bmax, s_bneg, s_bsum, s_bco = (small[:, 96 + 16 * n:112 + 16 * n] for n in range(4))

        def branch_row(x, t, r, b):
            return 8 * (x % 2) + 4 * t + 2 * r + b

        def branch_prob(x, t, r, b):
            c = r * S if b else 2 * S + r * P
            return prob[:, x % 2, t, c:c + (S if b else P)]

        def branch_logits(x, t, r, b):
            c = t * 1024 + (r * S if b else 2 * S + r * P)
            return pair_bank(x)[:, c:c + (S if b else P)]

        def pair_bank(x):
            return ps_a if x % 2 else ps_b

        norms = [(lambda: mem_rows[:, 0], G_MEM), (lambda: mem_rows[:, 1], G_MEM2), (lambda: h[:], G_ATTN),
                 (lambda: h[:], G_MLP), (lambda: h[:], G_MIX), (lambda: h[:], G_X), (lambda: h[:], G_FFN)]
        norm_loaded = [[sem(f"{n}_loaded{j}") for j in range(4)] for n in ("mem", "mem2", "x")]
        QUADS = {}
        at = 0
        for name, kb in (("n0", 16), ("n1", 16), ("n2", 16), ("o", 16), ("n3", 16), ("n4", 16), ("y1", 16),
                         ("n5", 16), ("xo", 4), ("n6", 16)):
            QUADS[name] = (at, SB * kb // 4)
            at += SB * kb // 4
        XT_FREE = {"n1": "xkv", "n2": "in1", "o": "wout", "n3": "mlp", "n4": "in2", "y1": "mixo",
                   "n5": "xq", "xo": "xo", "n6": "ffn"}

        def quad_dst(name, k):
            return k % SB, 4 * (k // SB)

        def opening(groups, halves, group, half_):
            group(0)
            for j in range(groups):
                if j + 1 < groups:
                    group(j + 1)
                for k in range(2 * j, 2 * j + 2):
                    if k < halves:
                        half_(k)

        def kv_rows(b, n):
            return proj2[:, b, NKV + n * 256:NKV + (n + 1) * 256].rearrange("p (g d) -> p g d", d=HD2)

        @block.scalar
        def _(act):
            order = [0]

            def link(ins):
                order[0] += 1
                ins.then_inc(act_order, 1)
                act.wait_ge(act_order, order[0])

            def copy(o, i):
                return nc.scalar.copy(o, i)

            act.dma_start(base[:, 0:P], c_base[:, 0:P]).then_inc(ld["ident"], 16)
            for n, g in enumerate(("attn_norm_g", "mem_norm_g", "mlp_norm_g", "ln_mix_pre_2", "ln_x_pre_2", "ln_mem_2",
                                   "ln_ffn_pre_2", "out_norm_g")):
                g = a[g] if len(a[g].shape) == 1 else a[g][0]
                act.dma_start(gains[16 * n:16 * n + 16, :], g.rearrange("(r c) -> r c", c=P)).then_inc(ld["gains"], 16)
            act.dma_start(gains2[0:4, :], a["gla_a_b"].rearrange("(r c) -> r c", c=P)).then_inc(ld["gains2"], 16)
            for n, g in enumerate(("fox_q_norm_g", "fox_k_norm_g", "mem_q_norm_g", "mem_k_norm_g")):
                act.dma_start(gains2[4 + n:5 + n, :], a[g].rearrange("(r c) -> r c", c=P)).then_inc(ld["gains2"], 16)
            act.dma_start(gains2[8:16, :], a["pool_scale_2"][0].rearrange("(r c) -> r c", c=P)).then_inc(ld["gains2"], 16)

            def hi(q, slot, i=None, halves=0, chunk=None, kn_=None):
                c = chunk
                more = 0 if i is None else i
                act.wait_ge(w_loaded[c % SLOTS], 16 * (loads_before(c) + 1) + more * (16 * halves // 8))
                if q >= 4:
                    act.wait_ge(pe_half, q - 3 + more * halves)
                j = q % 2
                if kn_ is None:
                    return copy(whi[:, q % 4], raw[:, c % SLOTS, 2 * j:2 * j + 2]).then_inc(hi_done, 1)
                n = kn_ * KB // 2
                return copy(whi[:, q % 4].rearrange("p k n -> p (k n)")[:, 0:n],
                            raw[:, c % SLOTS].rearrange("p k n -> p (k n)")[:, j * n:(j + 1) * n]).then_inc(hi_done, 1)

            def evict(t, q_end, dst, n):
                act.wait_ge(pe_half, q_end)
                act.wait_ge(n_rstd, n + 1)
                for b in range(SB):
                    ins = nc.scalar.activation(dst(b), bank(2 * (t % 2) + b), ACT.Copy, scale=s_rstd[:, b:b + 1])
                ins.then_inc(evicted, 1)

            def post_squares(t, q_end):
                act.wait_ge(pe_half, q_end)
                if post_tile[0]:
                    act.wait_ge(post_sq, post_tile[0])
                for b in range(SB):
                    ins = nc.scalar.activation(junk[:, b * NT:(b + 1) * NT], bank(2 * (t % 2) + b), ACT.Square,
                                               accum_out=s_pp[:, 4 * b + post_tile[0] % 4:4 * b + post_tile[0] % 4 + 1])
                ins.then_inc(post_sq, 1)
                post_tile[0] += 1

            post_tile = [0]

            def linear(name, first, last, out_of=None, kchunks=4, opened=0):
                c0, q0, t0 = seg[name]
                n = 2 * kchunks
                pend = []
                for k in range(first * n, last * n):
                    if k >= opened:
                        hi(q0 + k, 0, chunk=c0 + k // 2)
                    if out_of is not None:
                        if (k + 1) % n == 0:
                            pend.append((k + 3, k // n))
                        if pend and pend[0][0] <= k:
                            _, t = pend.pop(0)
                            out_of(t, t0 + t, q0 + (t + 1) * n)
                for _, t in pend:
                    out_of(t, t0 + t, q0 + (t + 1) * n)

            def looped(name, pairs):
                c0, q0, _ = seg[name]
                for k in range(8, 16):
                    hi(q0 + k, 0, chunk=c0 + k // 2)
                with act.Fori(1, pairs) as i:
                    for k in range(16):
                        hi(q0 + k, 0, i=i, halves=16, chunk=c0 + k // 2)

            def tail(name, n):
                c0, q0, t0 = seg[name]
                for k in range(2):
                    hi(q0 + k, 0, chunk=c0, kn_=n)

            def square_sums(n):
                if n < 3:
                    for j in range(4):
                        act.wait_ge(norm_loaded[n][j], 16)
                elif n == 3:
                    act.wait_ge(evicted, seg["mlp"][2])
                elif n == 4:
                    act.wait_ge(d_add, 64)
                else:
                    act.wait_ge(post_done, 8 * (n - 4))
                src = norms[n][0]()
                for b in range(SB):
                    ins = nc.scalar.activation(junk[:], src[:, b], ACT.Square, accum_out=s_sq[:, b:b + 1])
                    if b == 0:
                        link(ins)
                ins.then_inc(n_sq, 1)
                act.wait_ge(n_var, n + 1)
                nc.scalar.activation(s_std, s_var, ACT.Sqrt).then_inc(n_std, 1)

            def enter(quads, name, free=None, halves=8, first=None):
                c0, q0, _ = seg[name]
                t0, n = QUADS[quads]

                def group(j):
                    if j == 0 and free is not None:
                        act.wait_ge(pe_half, free)
                    for k in range(2 * j, 2 * j + 2):
                        b, kb = quad_dst(quads, k)
                        act.wait_ge(t_y, t0 + k + 1)
                        copy(xhi[:, kb:kb + 4, b * P:(b + 1) * P],
                             stage_t[:, (t0 + k) % 2].rearrange("p (k n) -> p k n", n=P)).then_inc(t_hi, 1)

                def ahead(k):
                    if k + 4 < halves:
                        hi(q0 + k + 4, 0, chunk=c0 + (k + 4) // 2)

                for k in range(min(4, halves)):
                    hi(q0 + k, 0, chunk=c0 + k // 2)
                if first is not None:
                    first()
                opening(n // 2, halves, group, ahead)

            def q_end(name):
                names = list(seg)
                return seg[names[names.index(name) + 1]][1]

            def post_norm(n):
                act.wait_ge(post_var, n + 1)
                nc.scalar.activation(s_pstd, s_pvar, ACT.Sqrt).then_inc(post_std, 1)

            def load_post_gain(name):
                act.dma_start(post_gain[:], a[name][0:1, :].to_broadcast([P, D])).then_inc(ld["gain"], 16)

            enter("n0", "memkv")
            square_sums(0)
            linear("memkv", 0, 2, lambda t, tile, q: evict(tile, q, lambda b: mkv[:, b, t * NT:(t + 1) * NT], 0), opened=8)
            enter("n1", "xkv", q_end("memkv"))
            square_sums(1)
            linear("xkv", 0, 2, lambda t, tile, q: evict(tile, q, lambda b: xkv[:, b, t * NT:(t + 1) * NT], 1), opened=8)
            enter("n2", "in1", q_end("xkv"))
            square_sums(2)
            looped("in1", T1 // 2)
            tail("tail1", TAIL1)
            act.wait_ge(pe_half, q_end("tail1"))
            act.dma_start(gw2[:], a["gla_a_w2"]).then_inc(ld["gw2"], 16)
            act.dma_start(fbias[:], a["fox_f_b"].rearrange("(r c) -> r c", c=1)).then_inc(ld["gw2"], 16)

            act.wait_ge(evicted, seg["wout"][2])
            nc.scalar.activation(proj1[:, :, GG:GG + 1024], proj1[:, :, GG:GG + 1024], ACT.Silu).then_inc(gate_done, 1)
            nc.scalar.activation(proj1[:, :, FG:FG + 512], proj1[:, :, FG:FG + 512], ACT.Sigmoid).then_inc(gate_done, 1)
            nc.scalar.activation(proj1[:, :, MG:MG + 512], proj1[:, :, MG:MG + 512], ACT.Sigmoid).then_inc(gate_done, 1)

            act.wait_ge(gla["z"], 1)
            link(nc.scalar.activation(ge[:, 0], gl[:], ACT.Abs))
            link(nc.scalar.activation(ge[:, 0], ge[:, 0], ACT.Exp, scale=-1.0))
            nc.scalar.activation(ge[:, 0], ge[:, 0], ACT.Ln, bias=1.0).then_inc(gla["ln"], 1)
            act.wait_ge(fx["z"], 1)
            link(nc.scalar.activation(fct[:, 1], fct[:, 0], ACT.Abs))
            link(nc.scalar.activation(fct[:, 1], fct[:, 1], ACT.Exp, scale=-1.0))
            nc.scalar.activation(fct[:, 1], fct[:, 1], ACT.Ln, bias=1.0).then_inc(fx["ln"], 1)
            for l in range(8):
                act.wait_ge(gla["d"], l + 1)
                link(nc.scalar.activation(ge[:, l % 2], ge[:, l % 2], ACT.Abs))
                nc.scalar.activation(ge[:, l % 2], ge[:, l % 2], ACT.Exp, scale=-1.0 / GLA_TAU).then_inc(gla["e"], 1)

            def softmax(n):
                act.wait_ge(a_sub, n + 1)
                nc.scalar.activation(pr[:], pr[:], ACT.Exp).then_inc(a_exp, 1)
                act.wait_ge(a_pps, n + 1)
                copy(pt[:, 0:4], ps_b[:, 0:1024].rearrange("p (x k n) -> p x k n", k=2, n=P)).then_inc(a_psb, 1)

            def attention(n, normed):
                if normed:
                    act.wait_ge(a_var, n + 1)
                    nc.scalar.activation(s_astd, s_ass, ACT.Sqrt).then_inc(a_std, 1)
                softmax(n)

            attention(0, True)
            attention(1, True)
            act.wait_ge(o_var, 1)
            nc.scalar.activation(s_ostd, s_oss, ACT.Sqrt).then_inc(o_std, 1)
            enter("o", "wout")
            act.wait_ge(t_hi, sum(QUADS["o"]))
            act.dma_start(hot[:], c_hot).then_inc(ld["hot"], 16)
            act.dma_start(relt[0:32, :], a["rel_bias_2"].rearrange("h b -> b h"), allow_slow_non_contiguous=True).then_inc(ld["rel"], 16)
            linear("wout", 0, 2, opened=8)
            act.wait_ge(ns["tpsb"], 1)
            act.dma_start(toep_dram, toep[:]).then_inc(ld["toep"], 16)
            linear("wout", 2, 3)
            act.wait_ge(ld["toep"], 16)
            for hh in range(NSA_H):
                act.dma_start(flip[:, hh], bass.AP(toep_dram.tensor, hh * 512, [[1, P], [1, S]])).then_inc(ld["flip"], 16)
            linear("wout", 3, 4)
            enter("n3", "mlp", q_end("wout"))
            square_sums(3)

            c0, q0, _ = seg["mlp"]

            def up_rows(g, i=None):
                more = 0 if i is None else i
                q = q0 + 8 if g == 0 else q0 + 16 + 16 * (g - 1)
                act.wait_ge(pe_half, q + more * 16)
                if g or i is not None:
                    act.wait_ge(u_tps, g + more)
                else:
                    act.wait_ge(n_rstd, 4)
                for b in range(SB):
                    nc.scalar.activation(g_row[:, b], bank(b), ACT.Relu, scale=s_rstd[:, b:b + 1]).then_inc(silu_done, 1)
                for b in range(SB):
                    act.wait_ge(silu_done, 2 * g + b + 1 + (0 if i is None else i * 2))
                    ins = nc.scalar.activation(u_row[:, b], g_row[:, b], ACT.Square)
                ins.then_inc(u_row_done, 1)

            def up_hi(g, i=None, base_=0):
                more = 0 if i is None else i
                act.wait_ge(u_tps, base_ + g + 1 + more)
                copy(uhi[:].rearrange("p k (b n) -> p b k n", b=SB),
                     ps_b[:, 1024:2048].rearrange("p (b k n) -> p b k n", b=SB, k=4)).then_inc(u_hi, 1)

            for k in range(8, 16):
                hi(q0 + k, 0, chunk=c0 + k // 2)
                if k == 10:
                    up_rows(0)
                if k == 14:
                    up_hi(0)
            ng = D_FF // NT
            with act.Fori(0, ng - 2) as i:
                for k in range(16):
                    hi(q0 + 16 + k, 0, i=i, halves=16, chunk=c0 + 8 + k // 2)
                    if k == 2:
                        up_rows(1, i)
                    if k == 12:
                        up_hi(1, i)
            k0 = 16 + 16 * (ng - 2)
            for k in range(16):
                hi(q0 + k0 + k, 0, chunk=c0 + (k0 + k) // 2)
                if k == 2:
                    up_rows(ng - 1)
                if k == 10:
                    up_hi(ng - 1)

            enter("n4", "in2", q_end("mlp"))
            square_sums(4)
            looped("in2", T2 // 2)
            linear("in2", T2 - 1, T2)
            act.wait_ge(evicted, seg["in2"][2] + 6)
            for kv in range(2):
                for b in range(SB):
                    ins = copy(kdup[:, b, kv], kv_rows(b, kv).unsqueeze(2).to_broadcast([P, NSA_G, 2, HD2]))
            ins.then_inc(ns["dup"], 1)
            tail("tail2", TAIL2)

            act.wait_ge(pe_half, q_end("tail2"))
            for kv in range(2):
                for t in range(2):
                    act.dma_start(pet[t * HD2:(t + 1) * HD2, kv], a["cmp_pe_2"][0, kv].rearrange("(l t) d -> t d l", t=2)[t],
                                  allow_slow_non_contiguous=True).then_inc(ld["cmp"], 16)
            for n, kv in enumerate((0, 0, 1)):
                act.dma_start(cw2[:, n], a["cmp_w2_2"][0, kv]).then_inc(ld["cmp"], 16)
            act.wait_ge(evicted, seg["special"][2])
            nc.scalar.activation(gates, gates, ACT.Sigmoid).then_inc(ns["gate"], 1)
            act.wait_ge(ns["t1"], 1)
            nc.scalar.activation(nqt[:, 0:4].rearrange("p x s -> p (x s)"), ps_b[:, 0:1024], ACT.Copy,
                                 scale=HD2 ** -0.5).then_inc(ns["t1s"], 1)
            for r in range(2):
                for b in range(SB):
                    ins = copy(vdup[:, b, r], kv_rows(b, 3 + 2 * r).unsqueeze(2).to_broadcast([P, NSA_G, 2, HD2]))
            ins.then_inc(ns["vdup"], 1)
            act.wait_ge(ns["t2"], 1)
            copy(nkt[:, 0:2].rearrange("p g r s -> p (g r s)"), ps_b[:, 0:1024]).then_inc(ns["t2s"], 1)
            for n in range(2):
                c = slice(NM + n * D, NM + (n + 1) * D)
                nc.scalar.activation(proj2[:, :, c], proj2[:, :, c], ACT.Sigmoid).then_inc(merge_gate, 1)
            act.wait_ge(ns["yps"], 1)
            copy(yt[:, 0:4].rearrange("p x s -> p (x s)"), ps_a[:, 0:1024]).then_inc(ns["ysb"], 1)
            act.wait_ge(ns["hid"], 1)
            act.wait_ge(ns["hidr"], 1)
            for kv in range(2):
                nc.scalar.activation(hid[:, kv, :, 0:N_CMP], bank(4 + kv)[:, 0:NSA_G * N_CMP].rearrange("p (g n) -> p g n", n=N_CMP),
                                     ACT.Gelu_apprx_tanh).then_inc(ns["gelu"], 1)
            act.wait_ge(ns["sub"], 1)
            nc.scalar.activation(pc[:], pc[:], ACT.Exp).then_inc(ns["exp"], 1)
            act.wait_ge(ns["pooled"], 1)
            copy(xhi[:, 8:16], yt[:]).then_inc(ns["pool_hi"], 1)

            def exps(x):
                for t in range(2):
                    act.wait_ge(nb["max"], 2 * x + t + 1)
                    for r in range(2):
                        for b in range(SB):
                            y = branch_row(x, t, r, b)
                            p = branch_prob(x, t, r, b)
                            ins = nc.scalar.activation(p, p, ACT.Exp, bias=s_bneg[:, y:y + 1], accum_out=s_bsum[:, y:y + 1])
                    ins.then_inc(nb["exp"], 1)

            exps(0)
            for x in range(8):
                if x < 7:
                    exps(x + 1)
                act.wait_ge(nb["pt"], x + 1)
                copy(probt[:, x % 2, 0:1024], pair_bank(x)[:, 0:1024]).then_inc(nb["pts"], 1)
                act.wait_ge(nb["y"], x + 1)
                copy(xhi[:, x], stage_t[:, x % 2, 0:S]).then_inc(nb["hi"], 1)
            linear("br", 0, 2, kchunks=2)
            linear("br", 2, 8, kchunks=2)
            enter("y1", "mixo", q_end("br"))
            load_post_gain("ln_mix_post_2")
            linear("mixo", 0, 4, lambda t, tile, q: post_squares(tile, q), opened=8)

            enter("n5", "xq", q_end("mixo"), first=lambda: post_norm(0))
            act.wait_ge(post_done, 8)
            load_post_gain("ln_x_post_2")
            square_sums(5)
            evict(seg["xq"][2], q_end("xq"), lambda b: qx[:, b], 5)
            softmax(2)
            enter("xo", "xo", q_end("xq"), halves=2)
            linear("xo", 0, 4, lambda t, tile, q: post_squares(tile, q), kchunks=1, opened=2)

            enter("n6", "ffn", q_end("xo"), first=lambda: post_norm(1))
            square_sums(6)
            act.wait_ge(post_done, 16)
            load_post_gain("ln_ffn_post_2")
            c0, q0, _ = seg["ffn"]
            ng = D_FF2 // NT
            gbase, sbase = D_FF // NT, 2 * (D_FF // NT)

            def gate_rows(g, i=None):
                more = 0 if i is None else i
                q = q0 + 8 if g == 0 else q0 + 24 + 24 * (g - 1)
                act.wait_ge(pe_half, q + more * 24)
                if g or i is not None:
                    act.wait_ge(u_row_done, gbase + g + more)
                else:
                    act.wait_ge(n_rstd, 7)
                for b in range(SB):
                    nc.scalar.activation(g_row[:, b], bank(b), ACT.Silu, scale=s_rstd[:, b:b + 1]).then_inc(silu_done, 1)

            for k in range(8, 16):
                hi(q0 + k, 0, chunk=c0 + k // 2)
                if k == 10:
                    gate_rows(0)
            for k in range(16, 32):
                hi(q0 + k, 0, chunk=c0 + k // 2)
                if k == 26:
                    gate_rows(1)
                    up_hi(0, base_=gbase)
            with act.Fori(0, ng - 2) as i:
                for k in range(24):
                    hi(q0 + 32 + k, 0, i=i, halves=24, chunk=c0 + 16 + k // 2)
                    if k == 18:
                        gate_rows(2, i)
                        up_hi(1, i, gbase)
            k0 = 32 + 24 * (ng - 2)
            for k in range(16):
                hi(q0 + k0 + k, 0, chunk=c0 + (k0 + k) // 2)
                if k == 10:
                    up_hi(ng - 1, base_=gbase)
            for t in range(4):
                act.wait_ge(d_add, 4 * gbase + 4 * (ng - 1) + t + 1)
                act.wait_ge(post_sq, 8 + t)
                for b in range(SB):
                    ins = nc.scalar.activation(junk[:, b * NT:(b + 1) * NT], ybuf[:, b, t * NT:(t + 1) * NT], ACT.Square,
                                               accum_out=s_pp[:, 4 * b + t:4 * b + t + 1])
                ins.then_inc(post_sq, 1)
            post_norm(2)

        @block.gpsimd
        def _(pool):
            for n, (rows_, src) in enumerate(((mem_rows[:, 0], "mem"), (mem_rows[:, 1], "mem_2"), (h, "x"))):
                for j in range(4):
                    c = slice(j * NT, (j + 1) * NT)
                    pool.dma_start(rows_[:, :, c], a[src][0].rearrange("(b p) d -> p b d", p=P)[:, :, c]).then_inc(norm_loaded[n][j], 16)
            pool.dma_start(base[:, P:], c_base[:, P:]).then_inc(ld["base"], 16)

        @block.vector
        def _(dve):
            order = [0]
            V = nc.vector

            def link(ins):
                order[0] += 1
                ins.then_inc(dve_order, 1)
                dve.wait_ge(dve_order, order[0])

            def lo(q, i=None, halves=0, chunk=None, kn_=None):
                more = 0 if i is None else i
                dve.wait_ge(hi_done, q + 1 + more * halves)
                j, c = q % 2, chunk
                if kn_ is None:
                    return V.tensor_tensor(wlo[:, q % 4], raw[:, c % SLOTS, 2 * j:2 * j + 2], whi[:, q % 4].bitcast(F32),
                                           ALU.subtract).then_inc(lo_done, 1)
                n = kn_ * KB // 2
                return V.tensor_tensor(wlo[:, q % 4].rearrange("p k n -> p (k n)")[:, 0:n],
                                       raw[:, c % SLOTS].rearrange("p k n -> p (k n)")[:, j * n:(j + 1) * n],
                                       whi[:, q % 4].rearrange("p k n -> p (k n)")[:, 0:n].bitcast(F32),
                                       ALU.subtract).then_inc(lo_done, 1)

            def q_end(name):
                names = list(seg)
                return seg[names[names.index(name) + 1]][1]

            def linear(name, first, last, evict=None, kchunks=4, opened=0):
                c0, q0, t0 = seg[name]
                n = 2 * kchunks
                pend = []
                for k in range(first * n, last * n):
                    if k >= opened:
                        lo(q0 + k, chunk=c0 + k // 2)
                    if evict is not None:
                        if (k + 1) % n == 0:
                            pend.append((k + 3, k // n))
                        if pend and pend[0][0] <= k:
                            _, t = pend.pop(0)
                            dve.wait_ge(pe_half, q0 + (t + 1) * n)
                            evict(t, t0 + t)
                for _, t in pend:
                    dve.wait_ge(pe_half, q0 + (t + 1) * n)
                    evict(t, t0 + t)

            def looped(name, pairs, odd, proj):
                c0, q0, t0 = seg[name]

                def out_of(t, col):
                    for b in range(SB):
                        ins = V.tensor_scalar(proj[:, b, col], bank(2 * ((t0 + t) % 2) + b), s_rstd[:, b:b + 1], None, ALU.mult)
                    ins.then_inc(evicted, 1)

                for k in range(8, 16):
                    lo(q0 + k, chunk=c0 + k // 2)
                    if k == 10:
                        dve.wait_ge(pe_half, q0 + 8)
                        out_of(0, slice(0, NT))
                with dve.Fori(1, pairs) as i:
                    for k in range(16):
                        lo(q0 + k, i, 16, chunk=c0 + k // 2)
                        if k == 2:
                            dve.wait_ge(pe_half, q0 + i * 16)
                            out_of(1, bass.ds(i * (2 * NT) - NT, NT))
                        if k == 10:
                            dve.wait_ge(pe_half, q0 + 8 + i * 16)
                            out_of(0, bass.ds(i * (2 * NT), NT))
                last = 2 * pairs - 1
                if odd:
                    for k in range(8):
                        lo(q0 + 16 * pairs + k, chunk=c0 + 8 * pairs + k // 2)
                        if k == 2:
                            dve.wait_ge(pe_half, q0 + 16 * pairs)
                            out_of(last, slice(last * NT, (last + 1) * NT))
                    last += 1
                return q0 + 8 * (last + 1), lambda: out_of(last, slice(last * NT, (last + 1) * NT))

            def tail(name, n, before, proj, c1):
                c0, q0, t0 = seg[name]
                for k in range(2):
                    lo(q0 + k, chunk=c0, kn_=n)
                q, out_of = before
                dve.wait_ge(pe_half, q)
                out_of()
                dve.wait_ge(pe_half, q0 + 2)
                for b in range(SB):
                    ins = V.tensor_scalar(proj[:, b, c1:c1 + n], bank(2 * (t0 % 2) + b)[:, 0:n], s_rstd[:, b:b + 1], None, ALU.mult)
                ins.then_inc(evicted, 1)

            def row_scale(n):
                dve.wait_ge(n_sq, n + 1)
                V.tensor_scalar(s_var, s_sq, 1.0 / D, EPS, ALU.mult, ALU.add).then_inc(n_var, 1)
                dve.wait_ge(n_std, n + 1)
                V.reciprocal(s_rstd, s_std).then_inc(n_rstd, 1)
                dve.wait_ge(n_rstd, n + 1)

            def enter(quads, name, gain=None, halves=8, first=None):
                c0, q0, _ = seg[name]
                t0, n = QUADS[quads]

                def group(j):
                    for k in range(2 * j, 2 * j + 2):
                        b, kb = quad_dst(quads, k)
                        dve.wait_ge(t_ps, t0 + k + 1)
                        if t0 + k >= 2:
                            dve.wait_ge(t_lo, t0 + k - 1)
                        ps = bank(4 + (t0 + k + 2) % 4)
                        if gain is None:
                            ins = V.tensor_copy(stage_t[:, (t0 + k) % 2], ps)
                        else:
                            ins = V.tensor_tensor(stage_t[:, (t0 + k) % 2].rearrange("p (k n) -> p k n", n=P),
                                                  ps.rearrange("p (k n) -> p k n", n=P),
                                                  gain[:, kb:kb + 4].unsqueeze(2).to_broadcast([P, 4, P]), ALU.mult)
                        ins.then_inc(t_y, 1)
                    for k in range(2 * j, 2 * j + 2):
                        b, kb = quad_dst(quads, k)
                        dve.wait_ge(t_hi, t0 + k + 1)
                        V.tensor_tensor(xlo[:, kb:kb + 4, b * P:(b + 1) * P],
                                        stage_t[:, (t0 + k) % 2].rearrange("p (k n) -> p k n", n=P),
                                        xhi[:, kb:kb + 4, b * P:(b + 1) * P].bitcast(F32), ALU.subtract).then_inc(t_lo, 1)

                def ahead(k):
                    if k + 4 < halves:
                        lo(q0 + k + 4, chunk=c0 + (k + 4) // 2)

                for k in range(min(4, halves)):
                    lo(q0 + k, chunk=c0 + k // 2)
                if first is not None:
                    first()
                opening(n // 2, halves, group, ahead)

            def post_gained(n):
                def evict(t, tile):
                    dve.wait_ge(post_sq, 4 * n + t + 1)
                    dve.wait_ge(ld["gain"], 16 * (n + 1))
                    for b in range(SB):
                        ins = V.tensor_tensor(ybuf[:, b, t * NT:(t + 1) * NT], bank(2 * (tile % 2) + b),
                                              post_gain[:, t * NT:(t + 1) * NT], ALU.mult)
                    ins.then_inc(evicted, 1)
                return evict

            def post_norm(n, by_rows=False):
                dve.wait_ge(post_sq, 4 * (n + 1))
                link(V.reduce_sum(s_psq, s_pp.rearrange("p (b t) -> p b t", t=4), axis=AX))
                V.tensor_scalar(s_pvar, s_psq, 1.0 / D, EPS, ALU.mult, ALU.add).then_inc(post_var, 1)
                dve.wait_ge(post_std, n + 1)
                link(V.reciprocal(s_prstd, s_pstd))
                for t, b in ([(t, b) for b in range(SB) for t in range(4)] if by_rows else
                             [(t, b) for t in range(4) for b in range(SB)]):
                    c = slice(t * NT, (t + 1) * NT)
                    V.scalar_tensor_tensor(h[:, b, c], ybuf[:, b, c], s_prstd[:, b:b + 1], h[:, b, c], ALU.mult,
                                           ALU.add).then_inc(post_done, 1)

            dve.wait_ge(gain_ps, 2)
            link(V.tensor_copy(gain_t[:], bank(7)[:, 0:P]))
            link(V.tensor_copy(gain2_t[:], bank(7)[:, P:P + 16]))
            link(V.memset(mix_gain[:], 1.0))
            V.tensor_copy(mix_gain[:, 8:16], gain2_t[:, G_POOL:G_POOL + 8]).then_inc(gain_sb, 1)
            dve.wait_ge(gain_sb, 1)

            enter("n0", "memkv", gain_t[:, G_MEM:G_MEM + 16])
            row_scale(0)
            linear("memkv", 0, 2, opened=8)
            enter("n1", "xkv", gain_t[:, G_MEM2:G_MEM2 + 16])
            row_scale(1)
            linear("xkv", 0, 2, opened=8)
            enter("n2", "in1", gain_t[:, G_ATTN:G_ATTN + 16])
            row_scale(2)
            before = looped("in1", T1 // 2, False, proj1)
            tail("tail1", TAIL1, before, proj1, T1 * NT)

            dve.wait_ge(pe_half, q_end("tail1"))
            dve.wait_ge(gla["tps"], 1)
            V.tensor_scalar(gqt[:].rearrange("p x s -> p (x s)"), ps_b[:, 0:1024], GLA_DK ** -0.5, None, ALU.mult)
            V.tensor_copy(gkt[:].rearrange("p x s -> p (x s)"), ps_b[:, 1024:2048]).then_inc(gla["tsb"], 1)
            dve.wait_ge(gla["gaps"], 1)
            V.tensor_copy(gat[:], ps_a[0:GLA_RANK, 0:S]).then_inc(gla["gat"], 1)
            dve.wait_ge(gla["gaps"], 2)
            dve.wait_ge(ld["gw2"], 32)
            V.tensor_scalar(fct[:, 0], ps_a[0:4, NT:NT + S], fbias[:, 0:1], None, ALU.add).then_inc(fx["z"], 1)
            dve.wait_ge(gla["zps"], 1)
            V.tensor_tensor(gl[:], ps_a[:, 1024:2048].rearrange("p (x s) -> p x s", s=S),
                            gain2_t[:, B_GLA:B_GLA + 4].unsqueeze(2).to_broadcast([P, 4, S]), ALU.add).then_inc(gla["z"], 1)
            V.memset(att[:], 0.0)
            link(V.memset(g_ones[:], 1.0))
            dve.wait_ge(gla["ln"], 1)
            link(V.scalar_tensor_tensor(gl[:].rearrange("p x s -> p (x s)"), gl[:].rearrange("p x s -> p (x s)"), 0.0,
                                        ge[:, 0].rearrange("p x s -> p (x s)"), ALU.min, ALU.subtract))
            for x in range(4):
                ins = V.tensor_tensor_scan(gbt[:, x], g_ones[:], gl[:, x], 0.0, ALU.mult, ALU.add)
                if x == 3:
                    link(ins)
            dve.wait_ge(fx["z"], 1)
            dve.wait_ge(fx["ln"], 1)
            link(V.scalar_tensor_tensor(fct[:, 0], fct[:, 0], 0.0, fct[:, 1], ALU.min, ALU.subtract))
            link(V.tensor_tensor_scan(fct[:, 2], g_ones[0:4, :], fct[:, 0], 0.0, ALU.mult, ALU.add))
            V.tensor_scalar(fct[:, 3], fct[:, 2], -1.0, None, ALU.mult).then_inc(fx["c"], 1)

            def decays(l):
                w = (LEVELS + [P])[l]
                if l >= 2:
                    dve.wait_ge(gla["qk"], l - 1)
                v = gbt[:].rearrange("p x (m t) -> p (x m) t", t=2 * w)
                V.tensor_tensor(ge[:, l % 2].rearrange("p x (m t) -> p (x m) t", t=2 * w), v,
                                v[:, :, w - 1:w].to_broadcast([P, 4 * S // (2 * w), 2 * w]), ALU.subtract).then_inc(gla["d"], 1)

            def decayed(l):
                dve.wait_ge(gla["e"], l + 1)
                if l == 0:
                    dve.wait_ge(gla["tsb"], 1)
                if l >= 2:
                    dve.wait_ge(gla["s"], l - 1)
                V.tensor_tensor(gqe[:, l % 2], gqt[:], ge[:, l % 2], ALU.mult)
                V.tensor_tensor(gke[:, l % 2], gkt[:], ge[:, l % 2], ALU.mult).then_inc(gla["qk"], 1)

            def scores(l):
                dve.wait_ge(gla["s"], l + 1)
                if l == 7:
                    V.tensor_copy(att10[:].rearrange("p (x t) n -> p t x n", t=2),
                                  ps_b[:, :].rearrange("p (t u) -> p t u", t=2)[:, :, 0:512].rearrange("p t (x n) -> p t x n", n=P)
                                  ).then_inc(gla["att"], 1)
                    return
                m = base[:, C_MASK + l * P:C_MASK + (l + 1) * P] if l < 7 else base[:, C_MASK + 7 * P:C_MASK + 8 * P]
                if l == 8:
                    m = base[:, C_MASK + 7 * P:C_MASK + 8 * P]
                if l == 0:
                    dve.wait_ge(ld["base"], 16)
                V.copy_predicated(att[:].rearrange("p t x n -> p (t x) n"),
                                  m.bitcast(U32).unsqueeze(1).to_broadcast([P, 16, P]),
                                  ps_b[:, :].rearrange("p (y n) -> p y n", n=P)).then_inc(gla["att"], 1)

            decays(0)
            for l in range(8):
                if l + 1 < 8:
                    decays(l + 1)
                decayed(l)
                if l:
                    scores(l - 1)
            scores(7)
            scores(8)
            dve.wait_ge(gla["o"], 1)
            for b in range(SB):
                ins = V.tensor_copy(mix[:, b, 0:1024], ps_b[:, b * 1024:(b + 1) * 1024])
            ins.then_inc(gla["out"], 1)

            def softmax(n, n_pv, masked=None, gated=None, width=HD, store=None):
                lg = ps_b[:, :].rearrange("p (x b k) -> p x b k", b=SB, k=S)
                pv = pr[:].rearrange("p (x b) k -> p x b k", b=SB)
                dve.wait_ge(a_log, n + 1)
                if masked is None:
                    src = ps_b[:, :].rearrange("p (y k) -> p y k", k=S)
                else:
                    masked(lg, pv)
                    src = pr[:]
                link(V.reduce_max(s_max, src, axis=AX))
                V.tensor_tensor(pr[:], src, s_max.unsqueeze(2).to_broadcast([P, 8, S]), ALU.subtract).then_inc(a_sub, 1)
                dve.wait_ge(a_exp, n + 1)
                link(V.reduce_sum(s_sum, pr[:], axis=AX))
                link(V.reciprocal(s_co, s_sum))
                dve.wait_ge(a_pps, n + 1)
                V.tensor_copy(pt[:, 4:8], ps_b[:, 1024:2048].rearrange("p (x k n) -> p x k n", k=2, n=P)).then_inc(a_psb, 1)
                if gated is not None:
                    gated()
                dve.wait_ge(a_o, n + 1)
                store(ps_b[:, 0:8 * width].rearrange("p (t x b d) -> p t x b d", t=2, b=SB, d=width))

            def co_of(b, width):
                return s_co.rearrange("p (t x b) -> p t x b", t=2, b=SB)[:, :, :, b].unsqueeze(3).to_broadcast([P, 2, 2, width])

            def head_rows(n, q_src, k_src):
                V.tensor_tensor(qn[:], q_src, q_src, ALU.mult)
                link(V.tensor_tensor(kn[:], k_src, k_src, ALU.mult))
                V.reduce_sum(s_ass[:, 0:8], qn[:].rearrange("p b (h d) -> p (b h) d", d=HD), axis=AX)
                link(V.reduce_sum(s_ass[:, 8:16], kn[:].rearrange("p b (h d) -> p (b h) d", d=HD), axis=AX))
                V.tensor_scalar(s_ass, s_ass, 1.0 / HD, EPS, ALU.mult, ALU.add).then_inc(a_var, 1)
                dve.wait_ge(a_std, n + 1)
                link(V.reciprocal(s_arstd, s_astd))
                for dst, src, r in ((qn, q_src, s_arstd[:, 0:8]), (kn, k_src, s_arstd[:, 8:16])):
                    for b in range(SB):
                        ins = V.tensor_tensor(dst[:, b].rearrange("p (h d) -> p h d", d=HD),
                                              src[:, b].rearrange("p (h d) -> p h d", d=HD),
                                              r[:, 4 * b:4 * b + 4].unsqueeze(2).to_broadcast([P, 4, HD]), ALU.mult)
                ins.then_inc(a_rows, 1)

            def transposed(k, gq, gk):
                dve.wait_ge(a_tps, k + 1)
                V.tensor_scalar(qt[:].rearrange("p x s -> p (x s)"), ps_b[:, 0:1024], HD ** -0.5 if gq is None else gq,
                                None if gq is None else HD ** -0.5, ALU.mult, *(() if gq is None else (ALU.mult,)))
                if gk is None:
                    ins = V.tensor_copy(kt[:].rearrange("p x s -> p (x s)"), ps_b[:, 1024:2048])
                else:
                    ins = V.tensor_scalar(kt[:].rearrange("p x s -> p (x s)"), ps_b[:, 1024:2048], gk, None, ALU.mult)
                ins.then_inc(a_tsb, 1)

            def add_causal(lg, pv):
                for b in range(SB):
                    ins = V.tensor_tensor(pv[:, :, b], lg[:, :, b],
                                          base[:, C_CAUSAL + b * S:C_CAUSAL + (b + 1) * S].unsqueeze(1).to_broadcast([P, 4, S]),
                                          ALU.add)
                link(ins)

            def store_heads(col):
                def store(o):
                    for b in range(SB):
                        ins = V.tensor_tensor(mix[:, b, col:col + 512].rearrange("p (x t d) -> p t x d", t=2, d=HD),
                                              o[:, :, :, b], co_of(b, HD), ALU.mult)
                    ins.then_inc(a_out, 1)
                return store

            head_rows(0, proj1[:, :, FQ:FQ + 512], proj1[:, :, FK:FK + 512])
            transposed(0, gain2_t[:, G_FQ:G_FQ + 1], gain2_t[:, G_FK:G_FK + 1])
            softmax(0, 0, add_causal, None, HD, store_heads(1024))
            head_rows(1, proj1[:, :, MQ:MQ + 512], mkv[:, :, 0:512])
            transposed(1, gain2_t[:, G_MQ:G_MQ + 1], gain2_t[:, G_MK:G_MK + 1])
            softmax(1, 0, None, None, HD, store_heads(1536))

            dve.wait_ge(a_out, 2)
            dve.wait_ge(gla["out"], 1)
            sq = pr[:].rearrange("p x k -> p (x k)")
            for b in range(SB):
                link(V.tensor_tensor(sq, mix[:, b], mix[:, b], ALU.mult))
                link(V.reduce_sum(s_oss[:, 16 * b:16 * b + 16], sq.rearrange("p (h d) -> p h d", d=HD), axis=AX))
            V.tensor_scalar(s_oss, s_oss, 1.0 / HD, EPS, ALU.mult, ALU.add).then_inc(o_var, 1)
            dve.wait_ge(o_std, 1)
            link(V.reciprocal(s_orstd, s_ostd))
            dve.wait_ge(gate_done, 3)
            for b in range(SB):
                link(V.tensor_tensor(mix[:, b].rearrange("p (h d) -> p h d", d=HD), mix[:, b].rearrange("p (h d) -> p h d", d=HD),
                                     s_orstd[:, 16 * b:16 * b + 16].unsqueeze(2).to_broadcast([P, 16, HD]), ALU.mult))
                V.tensor_tensor(mix[:, b, 0:1024], mix[:, b, 0:1024], proj1[:, b, GG:GG + 1024], ALU.mult)
                V.tensor_tensor(mix[:, b, 1024:1536], mix[:, b, 1024:1536], proj1[:, b, FG:FG + 512], ALU.mult)
                ins = V.tensor_tensor(mix[:, b, 1536:2048], mix[:, b, 1536:2048], proj1[:, b, MG:MG + 512], ALU.mult)
            ins.then_inc(o_rows, 1)
            enter("o", "wout", gain_t[:, G_OUT:G_OUT + 16])

            def add_to(dst, sem_):
                def evict(t, tile):
                    for b in range(SB):
                        ins = V.tensor_tensor(dst[:, b, t * NT:(t + 1) * NT], dst[:, b, t * NT:(t + 1) * NT],
                                              bank(2 * (tile % 2) + b), ALU.add)
                    ins.then_inc(sem_, 1)
                return evict

            dve.wait_ge(t_ps, sum(QUADS["o"]))
            dve.wait_ge(ld["rel"], 16)
            V.memset(relt[32:33, :], 1.0).then_inc(ns["rel"], 1)
            linear("wout", 0, 2, add_to(h, evicted), opened=8)
            dve.wait_ge(ns["tp"], 1)
            V.tensor_copy(toep[:], bank(4)[0:16, :]).then_inc(ns["tpsb"], 1)
            linear("wout", 2, 4, add_to(h, evicted))
            for n in range(8):
                dve.wait_ge(ns["flip"], n + 1)
                V.tensor_copy(bias[:, 2 * n:2 * n + 2].rearrange("p h k -> p (h k)"), bank(4 + n % 4)).then_inc(ns["bias"], 1)
            enter("n3", "mlp", gain_t[:, G_MLP:G_MLP + 16])
            row_scale(3)

            def up_lo(g, i=None, base_=0):
                more = 0 if i is None else i
                dve.wait_ge(u_hi, base_ + g + 1 + more)
                V.tensor_tensor(ulo[:].rearrange("p k (b n) -> p b k n", b=SB),
                                ps_b[:, 1024:2048].rearrange("p (b k n) -> p b k n", b=SB, k=4),
                                uhi[:].rearrange("p k (b n) -> p b k n", b=SB).bitcast(F32), ALU.subtract).then_inc(u_lo, 1)

            def down_add(dst, t, q, i=None, per=16, first=False, n0=0, banks=2):
                dve.wait_ge(pe_half, q + (0 if i is None else i * per))
                if n0 or i is not None:
                    dve.wait_ge(d_add, n0 + (0 if i is None else i * 4))
                for b in range(SB):
                    ps = bank(banks + 2 * (t % 2) + b)
                    d = dst[:, b, t * NT:(t + 1) * NT]
                    ins = V.tensor_copy(d, ps) if first else V.tensor_tensor(d, d, ps, ALU.add)
                ins.then_inc(d_add, 1)

            c0, q0, _ = seg["mlp"]
            ng = D_FF // NT
            for k in range(8, 16):
                lo(q0 + k, chunk=c0 + k // 2)
                if k == 14:
                    up_lo(0)
            for k in range(16):
                lo(q0 + 16 + k, chunk=c0 + 8 + k // 2)
                if k in (4, 6, 8, 10):
                    down_add(h, k // 2 - 2, q0 + 16 + k - 2)
                if k == 12:
                    up_lo(1)
            with dve.Fori(1, ng - 2) as i:
                for k in range(16):
                    lo(q0 + 16 + k, i, 16, chunk=c0 + 8 + k // 2)
                    if k in (4, 6, 8, 10):
                        t = k // 2 - 2
                        down_add(h, t, q0 + 16 + k - 2, i, n0=t - 3)
                    if k == 12:
                        up_lo(1, i)
            k0 = 16 + 16 * (ng - 2)
            for k in range(16):
                lo(q0 + k0 + k, chunk=c0 + (k0 + k) // 2)
                if k in (4, 6, 8):
                    t = k // 2 - 2
                    down_add(h, t, q0 + k0 + k - 2, n0=4 * (ng - 2) + t - 3)
                if k == 10:
                    down_add(h, 3, q0 + k0 + 8, n0=4 * (ng - 2))
                    up_lo(ng - 1)
                if k in (12, 14):
                    t = k // 2 - 6
                    down_add(h, t, q0 + k0 + 10 + 2 * t, n0=4 * (ng - 1) + t - 3)
            for t in (2, 3):
                down_add(h, t, q0 + k0 + 10 + 2 * t, n0=4 * (ng - 1) + t - 3)

            enter("n4", "in2", gain_t[:, G_MIX:G_MIX + 16])
            row_scale(4)
            before = looped("in2", T2 // 2, True, proj2)
            for r in range(2):
                for b in range(SB):
                    ins = V.tensor_copy(kdup[:, b, 2 + r], kv_rows(b, 2 + 2 * r).unsqueeze(2).to_broadcast([P, NSA_G, 2, HD2]))
            ins.then_inc(ns["dup"], 1)
            tail("tail2", TAIL2, before, proj2, T2 * NT)

            dve.wait_ge(pe_half, q_end("tail2"))
            V.memset(hid[:], 0.0)
            V.memset(kcbd[:], 0.0)
            V.memset(pc[:, 0, :, 7:16], NEG)
            V.memset(pc[:, 1, :, 15:16], NEG).then_inc(ns["hidr"], 1)
            dve.wait_ge(ns["hidr"], 1)
            dve.wait_ge(ns["t1"], 1)
            V.tensor_scalar(nqt[:, 4:8].rearrange("p x s -> p (x s)"), ps_b[:, 1024:2048], HD2 ** -0.5, None, ALU.mult
                            ).then_inc(ns["t1s"], 1)
            dve.wait_ge(ns["tk"], 1)
            dve.wait_ge(ld["cmp"], 16 * 7)
            for kv in range(2):
                rawt = ps_a[:, kv * 1024:(kv + 1) * 1024].rearrange("p (g s) -> p g s", s=S)
                for t in range(2):
                    r = slice(t * HD2, (t + 1) * HD2)
                    for g in range(NSA_G):
                        v = rawt[r, g, t:t + 1]
                        win = bass.AP(v.tensor, v.offset, [list(v.ap[0]), [2, CMP_LEN // 2], [CMP_STRIDE, N_CMP]])
                        ins = V.tensor_tensor(xpe[r, kv, :, g], win, pet[r, kv].unsqueeze(2).to_broadcast([HD2, CMP_LEN // 2, N_CMP]),
                                              ALU.add)
            ins.then_inc(ns["xpe"], 1)
            dve.wait_ge(ns["t2"], 1)
            V.tensor_copy(nkt[:, 2:4].rearrange("p g r s -> p (g r s)"), ps_b[:, 1024:2048]).then_inc(ns["t2s"], 1)
            dve.wait_ge(ns["yps"], 1)
            V.tensor_copy(yt[:, 4:8].rearrange("p x s -> p (x s)"), ps_a[:, 1024:2048]).then_inc(ns["ysb"], 1)
            dve.wait_ge(ns["gelu"], 2)
            for g2 in range(2):
                for x in range(2):
                    ins = V.tensor_copy(hidr[:, g2, 4 * x:4 * x + 4], hid[:, 1, 2 * g2 + x].unsqueeze(1).to_broadcast([P, 4, 16]))
            ins.then_inc(ns["hidr"], 1)
            dve.wait_ge(ns["kv"], 1)
            for t in range(2):
                V.tensor_copy(kcbd[t * HD2:(t + 1) * HD2, :, t], bank(6)[t * HD2:(t + 1) * HD2, 0:64].rearrange("p (g n) -> p g n", n=16))
            for g2 in range(2):
                ins = V.tensor_tensor(vbd[:, g2], bank(7)[:, g2 * HD2:(g2 + 1) * HD2].unsqueeze(1).to_broadcast([P, 8, HD2]),
                                      blkmask.unsqueeze(2).to_broadcast([P, 8, HD2]), ALU.mult)
            ins.then_inc(ns["kvs"], 1)
            dve.wait_ge(ns["log"], 1)
            lg = bank(4).rearrange("p (b h n) -> p b h n", b=SB, n=16)
            for b in range(SB):
                n = N_CMP if b else 7
                off = 31 if b else 159
                link(V.tensor_tensor(pc[:, b, :, 0:n], lg[:, b, :, 0:n], bias[:, :, off:off + 16 * (n - 1) + 1:16], ALU.add))
            cview = pc[:].rearrange("p b h n -> p (b h) n")
            V.tensor_scalar(cmask[:], cview, NEG / 2, None, ALU.is_gt)
            link(V.reduce_max(s_cmax, cview, axis=AX))
            V.tensor_tensor(cview, cview, s_cmax.unsqueeze(2).to_broadcast([P, 32, 16]), ALU.subtract).then_inc(ns["sub"], 1)
            dve.wait_ge(ns["exp"], 1)
            link(V.tensor_tensor(cview, cview, cmask[:], ALU.mult))
            link(V.reduce_sum(s_csum, cview, axis=AX))
            link(V.tensor_scalar(s_csum, s_csum, 1.0, None, ALU.max))
            link(V.reciprocal(s_cinv, s_csum))
            dve.wait_ge(ns["gate"], 1)
            cinv = s_cinv.rearrange("p (b h) -> p b h", b=SB)
            link(V.tensor_tensor(cinv, cinv, gates.rearrange("p b (h c) -> p b h c", c=3)[:, :, :, 0], ALU.mult))
            V.tensor_tensor(cview, cview, s_cinv.unsqueeze(2).to_broadcast([P, 32, 16]), ALU.mult).then_inc(ns["p"], 1)
            dve.wait_ge(ns["pool"], 1)
            V.tensor_tensor(yt[:], ps_a[:, :].rearrange("p (x s) -> p x s", s=S),
                            gain2_t[:, G_POOL:G_POOL + 8].unsqueeze(2).to_broadcast([P, 8, S]), ALU.mult).then_inc(ns["pooled"], 1)
            dve.wait_ge(ns["pps"], 1)
            V.tensor_copy(pct[:].rearrange("p b x n -> p (b x n)"), bank(5)).then_inc(ns["psb"], 1)
            dve.wait_ge(ns["oc"], 1)
            V.tensor_copy(cmp_o[:].rearrange("p x s -> p (x s)"), ps_a[:, :]).then_inc(ns["cmp"], 1)

            def maxima(x):
                if x >= 2:
                    dve.wait_ge(nb["pt"], x - 1)
                for t in range(2):
                    dve.wait_ge(nb["logits"], 2 * x + t + 1)
                    for r in range(2):
                        for b in range(SB):
                            y = branch_row(x, t, r, b)
                            ins = V.tensor_tensor_reduce(branch_prob(x, t, r, b), branch_logits(x, t, r, b),
                                                         bias[:, 2 * x + t, (0 if b else P):S], 1.0, 3 * NEG, ALU.add, ALU.max,
                                                         accum_out=s_bmax[:, y:y + 1])
                    link(ins)
                    y = branch_row(x, t, 0, 0)
                    V.tensor_scalar(s_bneg[:, y:y + 4], s_bmax[:, y:y + 4], -1.0, None, ALU.mult).then_inc(nb["max"], 1)

            def weights(x):
                dve.wait_ge(nb["exp"], 2 * x + 2)
                y = branch_row(x, 0, 0, 0)
                link(V.reciprocal(s_bco[:, y:y + 8], s_bsum[:, y:y + 8]))
                for t in range(2):
                    gv = gates[:, :, 3 * (2 * x + t) + 1:3 * (2 * x + t) + 3].rearrange("p b r -> p r b")
                    co = s_bco[:, y + 4 * t:y + 4 * t + 4].rearrange("p (r b) -> p r b", r=2)
                    ins = V.tensor_tensor(co, co, gv, ALU.mult)
                link(ins)
                V.tensor_tensor(diag[:, x % 2], ident.unsqueeze(1).to_broadcast([P, 8, P]),
                                s_bco[:, y:y + 8].unsqueeze(2).to_broadcast([P, 8, P]), ALU.mult).then_inc(nb["diag"], 1)

            def outputs(x):
                dve.wait_ge(nb["pt"], x + 1)
                V.tensor_copy(probt[:, x % 2, 1024:1536], pair_bank(x)[:, 1024:1536]).then_inc(nb["pts"], 1)
                dve.wait_ge(nb["pv"], x + 1)
                for t in range(2):
                    r = slice(t * HD2, (t + 1) * HD2)
                    ins = V.tensor_tensor(stage_t[r, x % 2, 0:S], pair_bank(x)[r, 1536 + t * S:1536 + (t + 1) * S], cmp_o[r, x], ALU.add)
                ins.then_inc(nb["y"], 1)
                dve.wait_ge(nb["hi"], x + 1)
                V.tensor_tensor(xlo[:, x], stage_t[:, x % 2, 0:S], xhi[:, x].bitcast(F32), ALU.subtract).then_inc(nb["lo"], 1)

            maxima(0)
            for x in range(8):
                weights(x)
                if x < 7:
                    maxima(x + 1)
                outputs(x)

            dve.wait_ge(ns["pool_hi"], 1)
            V.tensor_tensor(xlo[:, 8:16], yt[:], xhi[:, 8:16].bitcast(F32), ALU.subtract).then_inc(nb["lo"], 1)

            dve.wait_ge(merge_gate, 2)

            def merge(t, tile):
                br, n = t % 2, t // 2
                for b in range(SB):
                    dst = mix[:, b, n * NT:(n + 1) * NT]
                    gv = proj2[:, b, NM + br * D + n * NT:NM + br * D + (n + 1) * NT]
                    if br == 0:
                        ins = V.tensor_tensor(dst, bank(2 * (tile % 2) + b), gv, ALU.mult)
                    else:
                        ins = V.tensor_tensor(gv, bank(2 * (tile % 2) + b), gv, ALU.mult)
                ins.then_inc(evicted, 1)
                if br == 1:
                    dve.wait_ge(evicted, tile + 1)
                    for b in range(SB):
                        dst = mix[:, b, n * NT:(n + 1) * NT]
                        ins = V.tensor_tensor(dst, dst, proj2[:, b, NM + D + n * NT:NM + D + (n + 1) * NT], ALU.add)
                    ins.then_inc(y1_done, 1)

            linear("br", 0, 8, merge, kchunks=2)
            enter("y1", "mixo")
            linear("mixo", 0, 4, post_gained(0), opened=8)
            enter("n5", "xq", gain_t[:, G_X:G_X + 16], first=lambda: post_norm(0))
            row_scale(5)
            dve.wait_ge(pe_half, q_end("xq"))
            transposed(2, None, None)
            softmax(2, 0, None, None, HD, store_heads(0))
            enter("xo", "xo", halves=2)
            linear("xo", 0, 4, post_gained(1), kchunks=1, opened=2)
            enter("n6", "ffn", gain_t[:, G_FFN:G_FFN + 16], first=lambda: post_norm(1))
            row_scale(6)
            c0, q0, _ = seg["ffn"]
            gbase, sbase, dbase = D_FF // NT, 2 * (D_FF // NT), 4 * (D_FF // NT)
            ng = D_FF2 // NT

            def up_rows(g, i=None):
                more = 0 if i is None else i
                q = q0 + 16 if g == 0 else q0 + 32 + 24 * (g - 1)
                dve.wait_ge(pe_half, q + more * 24)
                dve.wait_ge(silu_done, sbase + 2 * g + 2 + more * 2)
                dve.wait_ge(u_tps, gbase + g + more)
                for b in range(SB):
                    ins = V.scalar_tensor_tensor(u_row[:, b], bank(2 + b), s_rstd[:, b:b + 1], g_row[:, b], ALU.mult, ALU.mult)
                ins.then_inc(u_row_done, 1)

            for k in range(8, 32):
                lo(q0 + k, chunk=c0 + k // 2)
                if k == 18:
                    up_rows(0)
                if k == 26:
                    up_lo(0, base_=gbase)
            for k in range(24):
                lo(q0 + 32 + k, chunk=c0 + 16 + k // 2)
                if k == 2:
                    up_rows(1)
                if k in (4, 6, 8, 10):
                    down_add(ybuf, k // 2 - 2, q0 + 32 + k - 2, first=True, banks=4)
                if k == 18:
                    up_lo(1, base_=gbase)
            with dve.Fori(1, ng - 2) as i:
                for k in range(24):
                    lo(q0 + 32 + k, i, 24, chunk=c0 + 16 + k // 2)
                    if k == 2:
                        up_rows(1, i)
                    if k in (4, 6, 8, 10):
                        t = k // 2 - 2
                        down_add(ybuf, t, q0 + 32 + k - 2, i, 24, n0=dbase + t - 3, banks=4)
                    if k == 18:
                        up_lo(1, i, gbase)
            k0 = 32 + 24 * (ng - 2)
            for k in range(16):
                lo(q0 + k0 + k, chunk=c0 + (k0 + k) // 2)
                if k == 2:
                    up_rows(ng - 1)
                if k in (4, 6, 8):
                    t = k // 2 - 2
                    down_add(ybuf, t, q0 + k0 + k - 2, n0=dbase + 4 * (ng - 2) + t - 3, banks=4)
                if k == 10:
                    down_add(ybuf, 3, q0 + k0 + 8, n0=dbase + 4 * (ng - 2), banks=4)
                    up_lo(ng - 1, base_=gbase)
                if k in (12, 14):
                    t = k // 2 - 6
                    down_add(ybuf, t, q0 + k0 + 10 + 2 * t, n0=dbase + 4 * (ng - 1) + t - 3, banks=4)
            dve.wait_ge(ld["gain"], 16 * 3)

            def times_gain(t):
                dve.wait_ge(post_sq, 8 + t + 1)
                for b in range(SB):
                    c = slice(t * NT, (t + 1) * NT)
                    ins = V.tensor_tensor(ybuf[:, b, c], ybuf[:, b, c], post_gain[:, c], ALU.mult)
                return ins

            times_gain(0)
            down_add(ybuf, 2, q0 + k0 + 14, n0=dbase + 4 * (ng - 1) - 1, banks=4)
            times_gain(1)
            down_add(ybuf, 3, q0 + k0 + 16, n0=dbase + 4 * (ng - 1), banks=4)
            times_gain(2)
            link(times_gain(3))
            post_norm(2, by_rows=True)

        @block.tensor
        def _(pe):
            mm = nc.tensor.matmul

            def half(q, banks, kbs, first, last, cols=NT, i=None, halves=0, xh=None, xl=None):
                xh, xl = (xhi, xlo) if xh is None else (xh, xl)
                more = 0 if i is None else i
                pe.wait_ge(lo_done, q + 1 + more * halves)
                w0, w1_ = whi[:, q % 4], wlo[:, q % 4]
                if cols != NT:
                    w0 = w0.rearrange("p k n -> p (k n)")[:, 0:len(kbs) * cols].rearrange("p (k n) -> p k n", n=cols)
                    w1_ = w1_.rearrange("p k n -> p (k n)")[:, 0:len(kbs) * cols].rearrange("p (k n) -> p k n", n=cols)
                for j, kb in enumerate(kbs):
                    for b in range(SB):
                        o = bank(banks[b])[:, 0:cols]
                        x0, x1 = xh[:, kb, b * P:(b + 1) * P], xl[:, kb, b * P:(b + 1) * P]
                        mm(o, x0, w0[:, j], start=first and j == 0, stop=False)
                        mm(o, x0, w1_[:, j], start=False, stop=False)
                        ins = mm(o, x1, w0[:, j], start=False, stop=last and j == len(kbs) - 1)
                ins.then_inc(pe_half, 1)

            def free(t, i=None, tiles=0):
                if t >= 2:
                    pe.wait_ge(evicted, t - 1 + (0 if i is None else i * tiles))

            def tile(name, t, kchunks=4, kb0=0, i=None, tiles=0, halves=0, tt=None):
                c0, q0, t0 = seg[name]
                g = t0 + t
                free(g, i, tiles)
                n = 2 * kchunks
                for k in range(n):
                    half(q0 + t * n + k, (2 * (g % 2), 2 * (g % 2) + 1), (kb0 + 2 * k, kb0 + 2 * k + 1), k == 0, k == n - 1,
                         i=i, halves=halves)

            def looped(name, pairs):
                tile(name, 1)
                with pe.Fori(1, pairs) as i:
                    tile(name, 0, i=i, tiles=2, halves=16)
                    tile(name, 1, i=i, tiles=2, halves=16)

            def tail(name, n):
                c0, q0, t0 = seg[name]
                free(t0)
                for k in range(2):
                    half(q0 + k, (2 * (t0 % 2), 2 * (t0 % 2) + 1), tuple(range(8 * k, 8 * k + 8)), k == 0, k == 1, cols=n)

            def enter(quads, name, src, ready, halves=8):
                c0, q0, tile0 = seg[name]
                t0, n = QUADS[quads]

                def group(j):
                    ready(j)
                    for k in range(2 * j, 2 * j + 2):
                        b, kb = quad_dst(quads, k)
                        if t0 + k >= 4:
                            pe.wait_ge(t_y, t0 + k - 3)
                        o = bank(4 + (t0 + k + 2) % 4)
                        for m in range(4):
                            ins = nc.tensor.transpose(o[:, m * P:(m + 1) * P], src[:, b, (kb + m) * P:(kb + m + 1) * P], ident)
                        ins.then_inc(t_ps, 1)

                def first_half(k):
                    g, per = (tile0 + k // 4, 4) if name == "br" else (tile0, halves)
                    if k % per == 0 and name not in ("mlp", "ffn"):
                        free(g)
                    elif k == 0:
                        pe.wait_ge(evicted, tile0)
                    if k % 2 == 0:
                        pe.wait_ge(t_lo, t0 + k + 2)
                    bk = (0, 1) if name in ("mlp", "ffn") else (2 * (g % 2), 2 * (g % 2) + 1)
                    half(q0 + k, bk, (2 * k, 2 * k + 1), k % per == 0, k % per == per - 1)

                opening(n // 2, halves, group, first_half)

            pe.wait_ge(ld["ident"], 16)
            pe.wait_ge(ld["gains"], 16 * 8)
            nc.tensor.transpose(bank(7)[:, 0:P], gains[:], ident).then_inc(gain_ps, 1)
            pe.wait_ge(ld["gains2"], 16 * 6)
            nc.tensor.transpose(bank(7)[:, P:P + 16], gains2[:], base[0:16, C_ID:C_ID + 16]).then_inc(gain_ps, 1)
            pe.wait_ge(gain_sb, 1)

            def loaded(n):
                return lambda j: pe.wait_ge(norm_loaded[n][j], 16)

            enter("n0", "memkv", mem_rows[:, 0], loaded(0))
            tile("memkv", 1)
            enter("n1", "xkv", mem_rows[:, 1], loaded(1))
            tile("xkv", 1)
            enter("n2", "in1", h, loaded(2))
            looped("in1", T1 // 2)
            tail("tail1", TAIL1)

            pe.wait_ge(evicted, seg["wout"][2])
            pe.wait_ge(t_lo, sum(QUADS["n2"]))
            for n, col in enumerate((GQ, GK)):
                for x in range(4):
                    for b in range(SB):
                        ins = nc.tensor.transpose(ps_b[:, n * 1024 + x * S + b * P:n * 1024 + x * S + (b + 1) * P],
                                                  proj1[:, b, col + x * P:col + (x + 1) * P], ident)
            ins.then_inc(gla["tps"], 1)
            for b in range(SB):
                ins = nc.tensor.transpose(ps_a[0:GLA_RANK, b * P:(b + 1) * P], proj1[:, b, GA:GA + GLA_RANK], ident)
            ins.then_inc(gla["gaps"], 1)
            for b in range(SB):
                ins = nc.tensor.transpose(ps_a[0:4, NT + b * P:NT + (b + 1) * P], proj1[:, b, FF:FF + 4], ident)
            ins.then_inc(gla["gaps"], 1)
            pe.wait_ge(gla["gat"], 1)
            pe.wait_ge(ld["gw2"], 32)
            for x in range(4):
                ins = mm(ps_a[:, 1024 + x * S:1024 + (x + 1) * S], gw2[:, x * P:(x + 1) * P], gat[:], start=True, stop=True)
            ins.then_inc(gla["zps"], 1)

            def level(l, q, k, wait):
                wait()
                for x in range(4):
                    for t in range(2):
                        r = slice(t * GLA_DK, (t + 1) * GLA_DK)
                        if l == 7:
                            ins = mm(ps_b[:, t * 1024 + x * P:t * 1024 + (x + 1) * P], k[r, x, 0:P], q[r, x, P:S], start=True, stop=True)
                            continue
                        for b in range(SB):
                            c = t * 1024 + (x * SB + b) * P
                            ins = mm(ps_b[:, c:c + P], k[r, x, b * P:(b + 1) * P], q[r, x, b * P:(b + 1) * P], start=True, stop=True)
                ins.then_inc(gla["s"], 1)

            for l in range(8):
                def ready():
                    pe.wait_ge(gla["qk"], l + 1)
                    if l == 0:
                        pe.wait_ge(gla["tsb"], 1)
                    else:
                        pe.wait_ge(gla["att"], l)
                level(l, gqe[:, l % 2], gke[:, l % 2], ready)
            level(8, gqt[:], gkt[:], lambda: pe.wait_ge(gla["att"], 8))
            pe.wait_ge(gla["att"], 9)
            for hh in range(GLA_H):
                x, t = hh // 2, hh % 2
                for b in range(SB):
                    o = ps_b[:, b * 1024 + hh * P:b * 1024 + (hh + 1) * P]
                    ins = mm(o, att[:, t, x * SB + b], proj1[:, b, GV + hh * P:GV + (hh + 1) * P], start=True, stop=b == 0)
                    if b:
                        ins = mm(o, att10[:, hh], proj1[:, 0, GV + hh * P:GV + (hh + 1) * P], start=False, stop=True)
            ins.then_inc(gla["o"], 1)

            def slot(hh, b):
                return (hh % 2) * 4 + (hh // 2) * 2 + b

            def transposes_of(k, qs, ks):
                for n, src in enumerate((qs, ks)):
                    for x in range(4):
                        for b in range(SB):
                            ins = nc.tensor.transpose(ps_b[:, n * 1024 + x * S + b * P:n * 1024 + x * S + (b + 1) * P],
                                                      src[:, b, x * P:(x + 1) * P], ident)
                ins.then_inc(a_tps, 1)

            def weigh(n, v, width, causal):
                pe.wait_ge(a_exp, n + 1)
                for hh in range(4):
                    for b in range(SB):
                        y = slot(hh, b)
                        for k in range(SB):
                            ins = nc.tensor.transpose(ps_b[:, y * S + k * P:y * S + (k + 1) * P], pr[:, y, k * P:(k + 1) * P], ident)
                ins.then_inc(a_pps, 1)
                pe.wait_ge(a_psb, 2 * (n + 1))
                for hh in range(4):
                    for b in range(SB):
                        y = slot(hh, b)
                        last = 0 if causal and b == 0 else 1
                        for k in range(last + 1):
                            ins = mm(ps_b[:, y * width:(y + 1) * width], pt[:, y, k], v(hh, k), start=k == 0, stop=k == last)
                ins.then_inc(a_o, 1)

            def logits(n, forget):
                for hh in range(4):
                    for b in range(SB):
                        y = slot(hh, b)
                        o = ps_b[:, y * S:(y + 1) * S]
                        ins = mm(o, qt[:, hh, b * P:(b + 1) * P], kt[:, hh], start=True, stop=not forget)
                        if forget:
                            one = base[0:4, C_SEL + hh * S:C_SEL + (hh + 1) * S]
                            mm(o, fct[:, 2, b * P:(b + 1) * P], one, start=False, stop=False)
                            ins = mm(o, one[:, 0:P], fct[:, 3], start=False, stop=True)
                ins.then_inc(a_log, 1)

            pe.wait_ge(gla["out"], 1)
            pe.wait_ge(a_rows, 1)
            transposes_of(0, qn, kn)
            pe.wait_ge(a_tsb, 1)
            pe.wait_ge(fx["c"], 1)
            logits(0, True)
            weigh(0, lambda hh, k: proj1[:, k, FV + hh * HD:FV + (hh + 1) * HD], HD, True)
            pe.wait_ge(a_out, 1)
            pe.wait_ge(a_rows, 2)
            transposes_of(1, qn, kn)
            pe.wait_ge(a_tsb, 2)
            logits(1, False)
            weigh(1, lambda hh, k: mkv[:, k, 512 + hh * HD:512 + (hh + 1) * HD], HD, False)
            pe.wait_ge(a_out, 2)
            enter("o", "wout", mix, lambda j: pe.wait_ge(o_rows, 1))
            tile("wout", 1)
            pe.wait_ge(ld["hot"], 16)
            pe.wait_ge(ns["rel"], 1)
            pe.wait_ge(t_y, sum(QUADS["o"]))
            mm(bank(4)[0:16, :], relt[0:33, :], hot[0:33, 0:512], start=True, stop=True).then_inc(ns["tp"], 1)
            tile("wout", 2)
            tile("wout", 3)
            pe.wait_ge(ns["tpsb"], 1)
            pe.wait_ge(ld["flip"], 16 * NSA_H)
            for n in range(8):
                if n >= 4:
                    pe.wait_ge(ns["bias"], n - 3)
                mm(bank(4 + n % 4), hot[:, 512:512 + P], flip[:, 2 * n:2 * n + 2].rearrange("p h k -> p (h k)"),
                   start=True, stop=True).then_inc(ns["flip"], 1)
            pe.wait_ge(ns["bias"], 8)
            enter("n3", "mlp", h, lambda j: pe.wait_ge(evicted, seg["wout"][2] + j + 1))

            c0, q0, _ = seg["mlp"]

            def up_tile(q, i=None, per=0, banks=(0, 1), between=None):
                for k in range(8):
                    half(q + k, banks, (2 * k, 2 * k + 1), k == 0, k == 7, i=i, halves=per)
                    if k == 2 and between is not None:
                        between()

            def u_transposes(g, i=None, base_=0):
                more = 0 if i is None else i
                pe.wait_ge(u_row_done, base_ + g + 1 + more)
                if base_ or g or i is not None:
                    pe.wait_ge(u_lo, base_ + g + more)
                for b in range(SB):
                    for j in range(4):
                        ins = nc.tensor.transpose(ps_b[:, 1024 + (b * 4 + j) * P:1024 + (b * 4 + j + 1) * P],
                                                  u_row[:, b, j * P:(j + 1) * P], ident)
                ins.then_inc(u_tps, 1)

            def down_tile(q, t, added, i=None, per=0, banks=2, add_step=4):
                if added is not None:
                    pe.wait_ge(d_add, added + (0 if i is None else i * add_step))
                for k in range(2):
                    half(q + k, (banks + 2 * (t % 2), banks + 2 * (t % 2) + 1), (2 * k, 2 * k + 1), k == 0, k == 1, i=i, halves=per,
                         xh=uhi, xl=ulo)

            def mlp_downs(q, g, i=None):
                more = 0 if i is None else i
                pe.wait_ge(u_lo, g + 1 + more)
                for t in range(4):
                    added = 4 * g + t - 1
                    down_tile(q + 2 * t, t, added if added > 0 else None, i, 16)

            ng = D_FF // NT
            pe.wait_ge(u_row_done, 1)
            up_tile(q0 + 8, between=lambda: u_transposes(0))
            mlp_downs(q0 + 16, 0)
            pe.wait_ge(u_row_done, 2)
            up_tile(q0 + 24, between=lambda: u_transposes(1))
            with pe.Fori(1, ng - 2) as i:
                pe.wait_ge(u_lo, i + 1)
                for t in range(4):
                    down_tile(q0 + 16 + 2 * t, t, t - 1, i, 16)
                pe.wait_ge(u_row_done, i + 2)
                up_tile(q0 + 24, i, 16, between=lambda: u_transposes(1, i))
            k0 = 16 + 16 * (ng - 2)
            mlp_downs(q0 + k0, ng - 2)
            pe.wait_ge(d_add, 4 * (ng - 1))
            u_transposes(ng - 1)
            mlp_downs(q0 + k0 + 8, ng - 1)

            enter("n4", "in2", h, lambda j: pe.wait_ge(d_add, 4 * ng if j else 4 * (ng - 1) + 1))
            looped("in2", T2 // 2)
            tile("in2", T2 - 1)
            tail("tail2", TAIL2)

            pe.wait_ge(evicted, seg["special"][2])

            def dup_transposes(ps, kinds, swap):
                for n, kind in enumerate(kinds):
                    for g in range(NSA_G):
                        for b in range(SB):
                            c = ((2 * g + n) if swap else (4 * n + g)) * S + b * P
                            ins = nc.tensor.transpose(ps[:, c:c + P], kdup[:, b, kind, g].rearrange("p x d -> p (x d)"), ident)
                return ins

            pe.wait_ge(ns["dup"], 2)
            dup_transposes(ps_a, (0, 1), False).then_inc(ns["tk"], 1)
            for x in range(8):
                for b in range(SB):
                    ins = nc.tensor.transpose(ps_b[:, x * S + b * P:x * S + (b + 1) * P],
                                              proj2[:, b, NQ + x * P:NQ + (x + 1) * P], ident)
            ins.then_inc(ns["t1"], 1)
            pe.wait_ge(ns["t1s"], 2)
            dup_transposes(ps_b, (2, 3), True).then_inc(ns["t2"], 1)
            pe.wait_ge(ns["xpe"], 1)
            pe.wait_ge(ns["t2s"], 2)
            for kv in range(2):
                pe.wait_ge(sp_loaded[kv], 16)
                for l in range(CMP_LEN // 2):
                    w = raw[:, (special0 + kv) % SLOTS].rearrange("p k n -> p (k n)")[:, l * P:(l + 1) * P]
                    ins = mm(bank(4 + kv)[:, 0:NSA_G * N_CMP], w, xpe[:, kv, l].rearrange("p g n -> p (g n)"),
                             start=l == 0, stop=l == CMP_LEN // 2 - 1)
            ins.then_inc(ns["hid"], 1)
            pe.wait_ge(sp_loaded[2], 16)
            band = raw[:, (special0 + 2) % SLOTS].rearrange("p k n -> p (k n)").rearrange("p (b w s) -> p b w s", b=SB, w=4)
            for x in range(8):
                for b in range(SB):
                    ins = mm(ps_a[:, x * S:(x + 1) * S], proj2[:, b, NU + x * P:NU + (x + 1) * P], band[:, b, x // 2],
                             start=b == 0, stop=b == SB - 1)
            ins.then_inc(ns["yps"], 1)
            pe.wait_ge(ns["hidr"], 2)
            mm(bank(6)[:, 0:64], cw2[:, 0:2].rearrange("p x d -> p (x d)"), hid[:, 0].rearrange("p g n -> p (g n)"), start=True, stop=True)
            for g2 in range(2):
                ins = mm(bank(7)[:, g2 * HD2:(g2 + 1) * HD2], hidr[:, g2].rearrange("p x n -> p (x n)"), cw2[:, 2],
                         start=True, stop=True)
            ins.then_inc(ns["kv"], 1)
            pe.wait_ge(ns["kvs"], 1)
            for b in range(SB):
                for x in range(8):
                    ins = mm(bank(4)[:, (b * 8 + x) * 32:(b * 8 + x + 1) * 32], nqt[:, x, b * P:(b + 1) * P],
                             kcbd[:, x // 2].rearrange("p t n -> p (t n)"), start=True, stop=True)
            ins.then_inc(ns["log"], 1)
            pe.wait_ge(ns["ysb"], 2)
            pe.wait_ge(sp_loaded[3], 16)
            wp = raw[:, (special0 + 3) % SLOTS].rearrange("p k n -> p (k n)").rearrange("p (g k n) -> p g k n", g=4, k=2)
            for x in range(8):
                g = x // 2
                for k in range(2):
                    ins = mm(ps_a[:, x * S:(x + 1) * S], wp[:, g, k, (x % 2) * P:(x % 2 + 1) * P], yt[:, 2 * g + k],
                             start=k == 0, stop=k == 1)
            ins.then_inc(ns["pool"], 1)
            pe.wait_ge(ns["p"], 1)
            for b in range(SB):
                for g2 in range(2):
                    ins = nc.tensor.transpose(bank(5)[:, (b * 2 + g2) * P:(b * 2 + g2 + 1) * P],
                                              pc[:, b, 8 * g2:8 * g2 + 8].rearrange("p h n -> p (h n)"), ident)
            ins.then_inc(ns["pps"], 1)
            pe.wait_ge(ns["psb"], 1)
            pe.wait_ge(ns["pooled"], 1)
            for x in range(8):
                ins = mm(ps_a[:, x * S:(x + 1) * S], vbd[:, x // 4, 2 * (x % 4):2 * (x % 4) + 2].rearrange("p h d -> p (h d)"),
                         pct[:, :, x // 4], start=True, stop=True)
            ins.then_inc(ns["oc"], 1)

            def branch_qk(x):
                if x == 1:
                    pe.wait_ge(ns["cmp"], 1)
                if x >= 2:
                    pe.wait_ge(nb["y"], x - 1)
                for t in range(2):
                    r = slice(t * HD2, (t + 1) * HD2)
                    c = t * 1024
                    mm(pair_bank(x)[:, c:c + 2 * S], nqt[r, x, P:S], nkt[r, x // 2].rearrange("p r s -> p (r s)"), start=True, stop=True)
                    mm(pair_bank(x)[:, c + 2 * S:c + 3 * S], nqt[r, x, 0:P], nkt[r, x // 2, :, 0:P], start=True, stop=True
                       ).then_inc(nb["logits"], 1)

            branch_qk(0)
            for x in range(8):
                if x < 7:
                    branch_qk(x + 1)
                ps = pair_bank(x)
                pe.wait_ge(nb["diag"], x + 1)
                for t in range(2):
                    for r in range(2):
                        for b in range(SB):
                            for k in range(b + 1):
                                c = (r * 2 + t) * S + b * P if k == 0 else 1024 + (r * 2 + t) * P
                                ins = mm(ps[:, c:c + P], branch_prob(x, t, r, b)[:, k * P:(k + 1) * P],
                                         diag[:, x % 2, 4 * t + 2 * r + b], start=True, stop=True)
                ins.then_inc(nb["pt"], 1)
                pe.wait_ge(nb["pts"], 2 * (x + 1))
                if x == 0:
                    pe.wait_ge(ns["vdup"], 1)
                o = ps[:, 1536:2048]
                for r in range(2):
                    v0, v1 = (vdup[:, k, r, x // 2].rearrange("p x d -> p (x d)") for k in range(2))
                    mm(o, v0, probt[:, x % 2, r * 512:(r + 1) * 512], start=r == 0, stop=False)
                    ins = mm(o.rearrange("p (t s) -> p t s", t=2)[:, :, P:S], v1,
                             probt[:, x % 2, 1024 + r * S:1024 + (r + 1) * S].rearrange("p (t s) -> p t s", t=2),
                             start=False, stop=r == 1)
                ins.then_inc(nb["pv"], 1)

            pe.wait_ge(nb["lo"], 8)
            tile("br", 0, 2, 0)
            pe.wait_ge(nb["lo"], 9)
            for t in range(1, 8):
                tile("br", t, 2, 8 * (t % 2))
            enter("y1", "mixo", mix, lambda j: pe.wait_ge(y1_done, j + 1))
            for t in range(1, 4):
                tile("mixo", t)
            enter("n5", "xq", h, lambda j: pe.wait_ge(post_done, 2 * (j + 1)))
            pe.wait_ge(evicted, seg["xo"][2])
            transposes_of(2, qx, xkv)
            pe.wait_ge(a_tsb, 3)
            logits(2, False)
            weigh(2, lambda hh, k: xkv[:, k, 512 + hh * HD:512 + (hh + 1) * HD], HD, False)
            enter("xo", "xo", mix, lambda j: pe.wait_ge(a_out, 3), halves=2)
            for t in range(1, 4):
                tile("xo", t, 1)
            enter("n6", "ffn", h, lambda j: pe.wait_ge(post_done, 8 + 2 * (j + 1)))

            c0, q0, _ = seg["ffn"]
            gbase, sbase, dbase = D_FF // NT, 2 * (D_FF // NT), 4 * (D_FF // NT)
            ng = D_FF2 // NT
            up_tile(q0 + 8, banks=(2, 3))
            pe.wait_ge(silu_done, sbase + 2)
            up_tile(q0 + 16, between=None)
            pe.wait_ge(u_row_done, gbase + 1)
            u_transposes(0, base_=gbase)
            up_tile(q0 + 24, banks=(2, 3))

            def ffn_downs(q, g, i=None):
                pe.wait_ge(u_lo, gbase + g + 1 + (0 if i is None else i))
                for t in range(4):
                    down_tile(q + 2 * t, t, dbase + 4 * g + t - 1, i, 24, banks=4)

            def ffn_group(g, i=None):
                more = 0 if i is None else i
                ffn_downs(q0 + 32 + 24 * g, g, i)
                pe.wait_ge(silu_done, sbase + 2 * g + 4 + more * 2)
                up_tile(q0 + 40 + 24 * g, i, 24)
                u_tr(g, i)
                up_tile(q0 + 48 + 24 * g, i, 24, banks=(2, 3))

            def u_tr(g, i=None):
                pe.wait_ge(d_add, dbase + 4 * g + 4 + (0 if i is None else i * 4))
                u_transposes(g + 1, i, gbase)

            ffn_group(0)
            with pe.Fori(1, ng - 2) as i:
                ffn_group(0, i)
            k0 = 32 + 24 * (ng - 2)
            ffn_downs(q0 + k0, ng - 2)
            u_tr(ng - 2)
            ffn_downs(q0 + k0 + 8, ng - 1)


_INS = ["x", "mem", "attn_norm_g", "w_in", "gla_a_w2", "gla_a_b", "fox_f_b", "fox_q_norm_g", "fox_k_norm_g", "mem_norm_g",
        "w_mem_kv", "mem_q_norm_g", "mem_k_norm_g", "out_norm_g", "w_out", "mlp_norm_g", "w_up", "w_down", "mem_2", "rel_bias_2",
        "ln_mix_pre_2", "ln_mix_post_2", "ln_x_pre_2", "ln_x_post_2", "ln_mem_2", "ln_ffn_pre_2", "ln_ffn_post_2", "w_in_2",
        "cmp_pe_2", "cmp_w1_2", "cmp_w2_2", "w_pool_2", "pool_scale_2", "w_br_attn_2", "w_br_pool_2", "w_mix_out_2", "w_xq_2",
        "w_xkv_2", "w_xo_2", "w_gate_2", "w_up_2", "w_down_2"]


def kernel(**inputs):
    import concourse.bacc as _bacc
    from concourse.bass_utils import run_bass_kernel_spmd as _run

    nc = _bacc.Bacc("TRN2", target_bir_lowering=False, num_devices=1, dynamic_dma_scratch_size=1024)
    arrays, args = {}, {}
    for name in _INS:
        v = np.ascontiguousarray(inputs[name])
        arrays[f"in_{name}"] = v
        args[name] = nc.dram_tensor(f"in_{name}", v.shape, mybir.dt.from_np(v.dtype), kind="ExternalInput").ap()
    consts = []
    for name, v in zip(("base", "bands", "hot"), shape_constants()):
        arrays[f"const_{name}"] = v
        consts.append(nc.dram_tensor(f"const_{name}", v.shape, F32, kind="ExternalInput").ap())
    out = nc.dram_tensor("out", (1, S, D), F32, kind="ExternalOutput").ap()
    hybrid_blocks_kernel(nc, args, *consts, out)
    r = _run(nc, [arrays], core_ids=[0])
    return r.results[0]["out"]
```

```python
from contextlib import ExitStack

import numpy as np

import concourse.bass as bass
from concourse import mybir

F32 = mybir.dt.float32
F32R = mybir.dt.float32r
U32 = mybir.dt.uint32
BF16 = mybir.dt.bfloat16
ACT = mybir.ActivationFunctionType
ALU = mybir.AluOpType
AX = mybir.AxisListType.X

P = 128
S = 256
SB = S // P
D = 2048
KB = D // P
NT = 512
CK = 4
SLOTS = 4
EPS = 1e-6
NEG = -1e30

GLA_H, GLA_DK, GLA_RANK, GLA_TAU = 8, 64, 16, 16.0
HD = 128
GQ, GK, GV, GG = 0, 512, 1024, 2048
GA = 3072
FQ = GA + GLA_RANK
FK, FV, FG = FQ + 512, FQ + 1024, FQ + 1536
FF = FQ + 2048
MQ = FF + 4
MG = MQ + 512
IN1 = MG + 512
T1 = IN1 // NT
TAIL1 = IN1 - T1 * NT
D_FF = 4 * D
LEVELS = [1, 2, 4, 8, 16, 32, 64]
LEVELS_ALL = LEVELS + [P]

NSA_H, NSA_G, HD2 = 16, 4, 64
NQ, NKV, NGL = 0, 1024, 2560
NU = NGL + 3 * NSA_H
NM = NU + 1024
IN2 = NM + 2 * D
T2 = IN2 // NT
TAIL2 = IN2 - T2 * NT
CMP_LEN, CMP_STRIDE = 32, 16
N_CMP = (S - CMP_LEN) // CMP_STRIDE + 1
WINDOWS = (2, 4, 8, 16)
REL_BUCKETS, REL_MAX = 32, 2048
D_FF2 = 5632

G_ATTN, G_MEM, G_MLP, G_MIX, G_X, G_MEM2, G_FFN, G_OUT = (16 * n for n in range(8))
B_GLA, G_FQ, G_FK, G_MQ, G_MK, G_POOL = 0, 4, 5, 6, 7, 8


def shape_constants():
    j, i = np.arange(P)[:, None], np.arange(P)[None, :]
    ident = (j == i).astype(np.float32)
    masks = [((j // (2 * w) == i // (2 * w)) & (j % (2 * w) < w) & (i % (2 * w) >= w)).astype(np.float32)
             for w in LEVELS] + [ident]
    q = np.arange(S).reshape(SB, P).T[:, :, None]
    causal = np.where(q >= np.arange(S), 0.0, NEG).astype(np.float32).reshape(P, -1)
    sel = np.zeros((P, 4, S + P), np.uint16)
    for h in range(4):
        sel[h, h, :S] = 0x3F80
        sel[h, h, S:] = 0xBF80
    sel = sel.reshape(P, -1).view(np.float32)
    blocks = (np.arange(P)[:, None] // 16 == np.arange(8)).astype(np.float32)
    base = np.concatenate([ident, blocks, *masks, causal, sel], 1)
    s0, s1 = np.arange(S)[:, None], np.arange(S)[None, :]
    bands = np.stack([((s1 - s0 >= 0) & (s1 - s0 < w)) / np.minimum(s1 + 1, w) - (s0 == s1) for w in WINDOWS])
    bands = bands.astype(np.float32).reshape(4, SB, P, S).transpose(2, 1, 0, 3).reshape(P, -1)
    y = np.arange(512)
    n = np.maximum(255 - y, 0)
    exact = REL_BUCKETS // 2
    large = exact + (np.log(np.maximum(n, 1).astype(np.float32) / np.float32(exact)) / np.float32(np.log(REL_MAX / exact))
                     * np.float32(REL_BUCKETS - exact)).astype(np.int32)
    bucket = np.where(n < exact, n, np.minimum(large, REL_BUCKETS - 1))
    hot = np.zeros((P, 512 + P), np.float32)
    hot[:REL_BUCKETS, :512] = np.arange(REL_BUCKETS)[:, None] == bucket
    hot[REL_BUCKETS, :512] = np.where(y > 255, NEG, 0.0)
    hot[:, 512:] = ident[::-1]
    return base, np.ascontiguousarray(bands), hot


C_ID, C_BLK = 0, P
C_MASK = C_BLK + 8
C_CAUSAL = C_MASK + 8 * P
C_SEL = C_CAUSAL + SB * S
C_ALL = C_SEL + 4 * (S + P) // 2


def hybrid_blocks_kernel(nc, a, c_base, c_bands, c_hot, out):
    es = ExitStack()
    with es:
        place = [1152]

        def sb(name, shape, dt=F32, at=None):
            size = 4 * int(np.prod(shape[1:]))
            if at is None:
                at = place[0]
                place[0] += (size + 31) // 32 * 32
            t = nc.alloc_sbuf_tensor_at(name, shape, dt, offset=at)
            spots[name] = at
            return t

        spots = {}

        def sem(name):
            return es.enter_context(nc.semaphore(name))

        raw = sb("raw", [P, SLOTS, CK, NT])
        whi = sb("whi", [P, 4, 2, NT], F32R)
        wlo = sb("wlo", [P, 4, 2, NT], F32R)
        xhi = sb("xhi", [P, KB, S], F32R)
        xlo = sb("xlo", [P, KB, S], F32R)
        h = sb("h", [P, SB, D])
        mix = sb("mix", [P, SB, D])
        proj_at = place[0]
        proj1 = sb("proj1", [P, SB, IN1], at=proj_at)
        proj2 = sb("proj2", [P, SB, IN2])
        xkv = sb("xkv", [P, SB, 1024])
        base_at = place[0]
        base = sb("base", [P, C_ALL])
        mkv = sb("mkv", [P, SB, 1024])
        gains = sb("gains", [P, P])
        gain_t = sb("gain_t", [P, P])
        gains2 = sb("gains2", [16, P])
        gain2_t = sb("gain2_t", [P, 16])
        fbias = sb("fbias", [4, 1])
        small = sb("small", [P, 256])
        stage_t = sb("stage_t", [P, 2, NT])
        ybuf = sb("ybuf", [P, SB, D], at=proj_at)
        mem_rows = sb("mem_rows", [P, SB, D], at=proj_at)
        junk = sb("junk", [P, D], at=proj_at + 49152)
        post_gain = sb("post_gain", [P, D], at=proj_at + 16384)
        u_row = sb("u_row", [P, SB, NT], at=proj_at + 24576)
        uhi = sb("uhi", [P, 4, S], F32R, at=proj_at + 28672)
        ulo = sb("ulo", [P, 4, S], F32R, at=proj_at + 53248)
        g_row = sb("g_row", [P, SB, NT], at=proj_at + 57344)
        wa = spots["xhi"]
        qt = sb("qt", [P, 4, S], at=wa)
        kt = sb("kt", [P, 4, S], at=wa + 4096)
        qt1 = sb("qt1", [P, 4, S], at=spots["xkv"])
        kt1 = sb("kt1", [P, 4, S], at=spots["xkv"] + 4096)
        pr = sb("pr", [P, 8, S], at=wa + 8192)
        pt = sb("pt", [P, 8, 2, P], at=wa + 16384)
        att = sb("att", [P, 16, P], at=wa + 24576)
        wb = spots["whi"]
        ge = sb("ge", [P, 2, 4, S], at=wb)
        gqe = sb("gqe", [P, 2, 4, 2, P], at=wb + 8192)
        gke = sb("gke", [P, 2, 4, S], at=wb + 16384)
        att10 = sb("att10", [P, 8, P], at=wb + 24576)
        fox_o = sb("fox_o", [P, SB, 512], at=wb + 28672)
        gl = sb("gl", [P, 4, S], at=proj_at + 49408)
        gbt = sb("gbt", [P, 4, S], at=proj_at + 53504)
        fct = sb("fct", [4, 4, S], at=proj_at + 57600)
        fc_parts = fct[:, 0:2].rearrange("p n s -> p (n s)").bitcast(BF16).rearrange("p (n s) -> p n s", s=S)
        squares = sb("squares", [P, SB, 512], at=spots["mix"])
        gz = sb("gz", [P, 4, S], at=spots["mix"] + 4096)
        head_junk = sb("head_junk", [P, 16, HD], at=proj_at + 49408)
        gqt = sb("gqt", [P, 4, S], at=spots["mix"] + 8192)
        gkt = sb("gkt", [P, 4, S], at=spots["mix"] + 12288)
        gw2 = sb("gw2", [GLA_RANK, 512], at=spots["stage_t"])
        gat = sb("gat", [GLA_RANK, S], at=spots["stage_t"] + 2048)
        g_ones = sb("g_ones", [P, S], at=spots["stage_t"] + 3072)
        nqt = sb("nqt", [P, 8, S], at=wa)
        nkt = sb("nkt", [P, NSA_G, 2, S], at=spots["xlo"] + 8192)
        kdup = sb("kdup", [P, SB, 4, NSA_G, 2, HD2], at=spots["mix"])
        yt = sb("yt", [P, 8, S], at=spots["mix"])
        cmp_o = sb("cmp_o", [P, 8, S], at=spots["mix"] + 8192)
        bias = sb("bias", [P, NSA_H, S], at=base_at + 4 * C_MASK)
        hot = sb("hot", [P, 512 + P], at=proj_at)
        relt = sb("relt", [P, 16], at=proj_at + 2560)
        toep = sb("toep", [16, 512], at=proj_at + 2688)
        flip = sb("flip", [P, NSA_H, S], at=proj_at + 32768)
        xpe = sb("xpe", [P, 2, CMP_LEN // 2, NSA_G, N_CMP], at=wb)
        pet = sb("pet", [P, 2, CMP_LEN // 2], at=wb + 7680)
        cw2 = sb("cw2", [P, 3, HD2], at=wb + 7936)
        hid = sb("hid", [P, 2, NSA_G, 16], at=wb + 8704)
        hidr = sb("hidr", [P, 2, 8, 16], at=wb + 9216)
        kcbd = sb("kcbd", [P, NSA_G, 2, 16], at=wb + 10240)
        vbd = sb("vbd", [P, 2, 8, HD2], at=wb + 10752)
        pc = sb("pc", [P, SB, NSA_H, 16], at=wb + 14848)
        pct = sb("pct", [P, SB, 2, P], at=wb + 16896)
        cmask = sb("cmask", [P, SB * NSA_H, 16], at=wb + 18944)
        prob = sb("prob", [P, 2, 2, 768], at=wb)
        probt = sb("probt", [P, 2, 1536], at=wb + 12288)
        diag = sb("diag", [P, 2, 8, P], at=wb + 24576)
        x2hi = sb("x2hi", [P, KB, S], F32R, at=proj_at + 24576)
        x2lo = sb("x2lo", [P, KB, S], F32R, at=proj_at + 40960)
        qx = sb("qx", [P, SB, 512], at=proj_at + 57344)
        junk2 = sb("junk2", [P, SB * NT], at=base_at + 4 * C_MASK)
        junk3 = sb("junk3", [P, D], at=base_at + 4 * C_MASK + 8192)
        assert place[0] <= nc.sbuf_usable_end, place[0]
        assert base_at + 4 * C_MASK + 16384 <= spots["gains"]

        ident = base[:, C_ID:C_ID + P]
        blkmask = base[:, C_BLK:C_BLK + 8]

        ps_a = es.enter_context(nc.psum_tensor("ps_a", [P, 4 * NT], F32))
        ps_b = es.enter_context(nc.psum_tensor("ps_b", [P, 4 * NT], F32))

        def bank(n):
            t = ps_a if n < 4 else ps_b
            return t[:, (n % 4) * NT:(n % 4 + 1) * NT]

        vdup = proj2[:, :, NQ:NQ + 1024].rearrange("p b (r g x d) -> p b r g x d", r=2, g=NSA_G, x=2)
        gates = proj2[:, :, NGL:NU]

        toep_dram = nc.dram_tensor("toep_scratch", [16, 512], F32, kind="Internal").ap()

        w_loaded = [sem(f"w_loaded{i}") for i in range(SLOTS)]
        sp_loaded = [sem(f"sp_loaded{i}") for i in range(4)]
        hi_done, lo_done, pe_half, evicted = sem("hi_done"), sem("lo_done"), sem("pe_half"), sem("evicted")
        ld = {n: sem(f"ld_{n}") for n in ("ident", "gains", "gains2", "base", "gw2", "hot", "rel",
                                          "toep", "flip", "cmp", "gain")}
        gain_ps, gain_sb = sem("gain_ps"), sem("gain_sb")
        tail_sb, tail_ps = sem("tail_turning"), sem("tail_turned")
        n_sq, n_var, n_std, n_rstd = sem("norm_sq"), sem("norm_var"), sem("norm_std"), sem("norm_rstd")
        t_ps, t_y, t_hi, t_lo = sem("t_ps"), sem("t_y"), sem("t_hi"), sem("t_lo")
        dve_order, act_order = sem("dve_order"), sem("act_order")
        post_sq, post_var, post_std, post_done = sem("post_sq"), sem("post_var"), sem("post_std"), sem("post_done")
        a_tps, a_tsb = sem("att_tps"), sem("att_tsb")
        a_log, a_max, a_exp, a_pps, a_psb, a_o, a_out = (
            sem(n) for n in ("att_logits", "att_max", "att_exp", "att_pps", "att_psb", "att_o", "att_out"))
        hn = {n: sem("headnorm_" + n) for n in ("var", "std", "rstd", "rows")}
        gla = {n: sem("gla_" + n) for n in ("gaps", "gat", "zps", "z", "ln", "b", "d", "e", "q", "k", "zero",
                                            "tps", "tsb", "s", "att", "att0", "o")}
        fx = {n: sem("fox_" + n) for n in ("z", "ln", "c", "rstd", "over", "mixed")}
        gate_done, o_sq, o_var, o_std, o_rows = sem("gate_done"), sem("o_squares"), sem("o_var"), sem("o_std"), sem("o_rows")
        u_row_done, u_tps, u_hi, u_lo, d_add = sem("u_row"), sem("u_tps"), sem("u_hi"), sem("u_lo"), sem("down_added")
        ns = {n: sem("nsa_" + n) for n in ("rel", "tp", "tpsb", "flip", "bias", "dup", "t1", "t1s", "tk", "xpe", "t2", "t2_act", "t2_dve",
                                           "hid", "gelu", "hidr", "kv", "kvs", "log", "sub", "exp", "p", "pps", "psb",
                                           "oc", "cmp", "gate", "yps", "ysb", "pool", "pooled", "pool_hi", "vdup")}
        nb = {n: sem("branch_" + n) for n in ("logits", "max", "exp", "diag", "pt", "pt_act", "pt_dve", "pv", "y", "hi", "lo")}
        merge_gate, y1_done = sem("merge_gate"), sem("y1_done")
        silu_done = sem("silu_done")
        stored = sem("stored")

        seg = {}
        at_c, at_q, at_t = 0, 0, 0
        q_after = []
        special0 = None
        for name, tiles, chunks in (("memkv", 2, 4), ("in1", T1, 4), ("tail1", 1, 1), ("wout", 4, 4),
                                    ("mlp", 16, 8), ("in2", T2, 4), ("tail2", 1, 1), ("special", 4, 1), ("br", 8, 2),
                                    ("mixo", 4, 4), ("xk", 1, 4), ("xq", 1, 4), ("xv", 1, 4), ("xo", 4, 1), ("ffn", 11, 12)):
            seg[name] = (at_c, at_q, at_t)
            n = tiles * chunks
            if name == "special":
                special0 = at_c
            q_after += [at_q + (0 if name == "special" else 2 * (k + 1)) for k in range(n)]
            at_c += n
            if name != "special":
                at_q += 2 * n
            if name not in ("mlp", "ffn", "special"):
                at_t += tiles
        seg["end"] = (at_c, at_q, at_t)

        IN1_FIRST, IN1_LOOP, IN1_LAST = (0, 1, 2, 3), (6, 12), (GG // NT, GG // NT + 1)

        def loads_before(c):
            return c // SLOTS - (1 if c >= special0 + 4 else 0)

        block = es.enter_context(nc.Block())

        w1 = {"memkv": a["w_mem_kv"], "xk": a["w_xkv_2"][0][:, 0:512], "xv": a["w_xkv_2"][0][:, 512:1024], "in1": a["w_in"], "wout": a["w_out"],
              "in2": a["w_in_2"][0], "mixo": a["w_mix_out_2"][0], "xq": a["w_xq_2"][0], "xo": a["w_xo_2"][0]}

        @block.sync
        def _(sp):
            def load(c, src, dst=None, i=None, chunks=0):
                more = 0 if i is None else i
                if special0 + 4 <= c < special0 + 8:
                    s = c - 4 - special0
                    if s < 2:
                        sp.wait_ge(ns["hid"], 1)
                    elif s == 2:
                        sp.wait_ge(ns["yps"], 1)
                    else:
                        sp.wait_ge(ns["pool"], 1)
                elif c >= SLOTS:
                    sp.wait_ge(lo_done, q_after[c - SLOTS] + more * (2 * chunks))
                d = raw[:, c % SLOTS] if dst is None else dst
                sp.dma_start(d, src).then_inc(w_loaded[c % SLOTS], 16)

            def rows(w, r0, n, c0, cols=NT):
                return w[r0:r0 + n, c0:c0 + cols].rearrange("(k p) n -> p k n", p=P)

            def linear(name, first, last, kchunks=4):
                c0 = seg[name][0]
                for t in range(first, last):
                    for k in range(kchunks):
                        load(c0 + t * kchunks + k, rows(w1[name], k * CK * P, CK * P, t * NT))

            def looped(name, pairs):
                c0 = seg[name][0]
                linear(name, 0, 2)
                with sp.Fori(1, pairs) as i:
                    for j in range(8):
                        load(c0 + j, w1[name][(j % 4) * CK * P:(j % 4 + 1) * CK * P,
                                              bass.ds(i * (2 * NT) + (j // 4) * NT, NT)].rearrange("(k p) n -> p k n", p=P),
                             i=i, chunks=8)

            def tail(name, w, cols, n):
                c = seg[name][0]
                load(c, w[:, cols:cols + n].rearrange("(k p) n -> p k n", p=P),
                     raw[:, c % SLOTS].rearrange("p k n -> p (k n)")[:, 0:KB * n].rearrange("p (k n) -> p k n", n=n))

            load(0, rows(w1["memkv"], 0, CK * P, 0))
            sp.wait_ge(ld["gains"], 16 * 8)
            sp.wait_ge(ld["gains2"], 16 * 6)
            for k in range(1, 4):
                load(k, rows(w1["memkv"], k * CK * P, CK * P, 0))
            linear("memkv", 1, 2)

            def in1_tile(pos, t):
                for k in range(4):
                    load(seg["in1"][0] + 4 * pos + k, rows(a["w_in"], k * CK * P, CK * P, t * NT))

            for pos, t in enumerate(IN1_FIRST):
                in1_tile(pos, t)
            c0 = seg["in1"][0]
            with sp.Fori(2, 2 + (IN1_LOOP[1] - IN1_LOOP[0]) // 2) as i:
                for j in range(8):
                    load(c0 + j, a["w_in"][(j % 4) * CK * P:(j % 4 + 1) * CK * P,
                                           bass.ds(i * (2 * NT) + (IN1_LOOP[0] - 4 + j // 4) * NT, NT)].rearrange("(k p) n -> p k n", p=P),
                         i=i, chunks=8)
            for n, t in enumerate(IN1_LAST):
                in1_tile(T1 - 2 + n, t)
            tail("tail1", a["w_in"], T1 * NT, TAIL1)
            linear("wout", 0, 4)

            c0 = seg["mlp"][0]

            def mlp_up(c, g, i=None):
                for k in range(4):
                    cols = slice(g * NT, (g + 1) * NT) if i is None else bass.ds(i * NT + g * NT, NT)
                    load(c + k, a["w_up"][k * CK * P:(k + 1) * CK * P, cols].rearrange("(k p) n -> p k n", p=P), i=i, chunks=8)

            def mlp_down(c, g, w, i=None, chunks=8):
                for t in range(4):
                    r = slice(g * NT, (g + 1) * NT) if i is None else bass.ds(i * NT + g * NT, NT)
                    load(c + t, w[r, t * NT:(t + 1) * NT].rearrange("(k p) n -> p k n", p=P), i=i, chunks=chunks)

            ng = D_FF // NT
            mlp_up(c0, 0)
            mlp_up(c0 + 4, 1)
            with sp.Fori(0, ng - 2) as i:
                mlp_down(c0 + 8, 0, a["w_down"], i)
                mlp_up(c0 + 12, 2, i)
            mlp_down(c0 + 8 * ng - 8, ng - 2, a["w_down"])
            mlp_down(c0 + 8 * ng - 4, ng - 1, a["w_down"])

            looped("in2", T2 // 2)
            linear("in2", T2 - 1, T2)
            tail("tail2", a["w_in_2"][0], T2 * NT, TAIL2)
            for s in range(4):
                c = special0 + s
                sp.wait_ge(lo_done, q_after[c - SLOTS])
                slot = raw[:, c % SLOTS]
                flat = slot.rearrange("p k n -> p (k n)")
                if s < 2:
                    sp.dma_start(flat.rearrange("p (l n) -> p l n", n=P),
                                 a["cmp_w1_2"][0, s].rearrange("(l p) n -> p l n", p=P)).then_inc(sp_loaded[s], 16)
                elif s == 2:
                    sp.dma_start(flat, c_bands).then_inc(sp_loaded[s], 16)
                else:
                    sp.dma_start(flat.rearrange("p (g k n) -> p (g k) n", g=4, k=2),
                                 a["w_pool_2"][0].rearrange("g (k p) n -> p (g k) n", p=P)).then_inc(sp_loaded[s], 16)
            c0 = seg["br"][0]
            for t in range(4):
                for k in range(2):
                    load(c0 + 4 * t + k, rows(a["w_br_attn_2"][0], k * 512, 512, t * NT))
                for k in range(2):
                    load(c0 + 4 * t + 2 + k, rows(a["w_br_pool_2"][0], k * 512, 512, t * NT))
            linear("mixo", 0, 4)
            linear("xk", 0, 1)
            linear("xq", 0, 1)
            linear("xv", 0, 1)
            linear("xo", 0, 4, 1)

            c0 = seg["ffn"][0]

            def ffn_in(c, g, i=None):
                for n, w in enumerate((a["w_gate_2"][0], a["w_up_2"][0])):
                    for k in range(4):
                        cols = slice(g * NT, (g + 1) * NT) if i is None else bass.ds(i * NT + g * NT, NT)
                        load(c + 4 * n + k, w[k * CK * P:(k + 1) * CK * P, cols].rearrange("(k p) n -> p k n", p=P),
                             i=i, chunks=12)

            ng = D_FF2 // NT
            wd = a["w_down_2"][0]
            ffn_in(c0, 0)
            ffn_in(c0 + 8, 1)
            with sp.Fori(0, ng - 2) as i:
                mlp_down(c0 + 16, 0, wd, i, 12)
                ffn_in(c0 + 20, 2, i)
            mlp_down(c0 + 12 * ng - 8, ng - 2, wd)
            mlp_down(c0 + 12 * ng - 4, ng - 1, wd)

            for b in range(SB):
                for t in range(4):
                    sp.wait_ge(post_done, 16 + 4 * b + t + 1)
                    sp.dma_start(out[0, b * P:(b + 1) * P, t * NT:(t + 1) * NT], h[:, b, t * NT:(t + 1) * NT]).then_inc(stored, 16)
            sp.wait_ge(stored, 16 * SB * 4)

        s_rstd2 = small[:, 250:252]
        s_sq, s_var, s_std, s_rstd = (small[:, 2 * n:2 * n + 2] for n in range(4))
        s_pp = small[:, 8:16]
        s_psq, s_pvar, s_pstd, s_prstd = (small[:, 88 + 2 * n:90 + 2 * n] for n in range(4))
        s_diag = small[:, 16:32]
        s_max, s_sum, s_co, s_neg = small[:, 64:72], small[:, 72:80], small[:, 80:88], small[:, 240:248]
        s_hss, s_hstd, s_hrstd = small[:, 96:128], small[:, 128:160], small[:, 160:192]
        s_oco = small[:, 192:224]
        s_oss, s_ostd, s_orstd = small[:, 96:128], small[:, 128:160], small[:, 160:192]
        s_cmax, s_csum, s_cinv = small[:, 96:128], small[:, 128:160], small[:, 160:192]
        s_bmax, s_bneg, s_bsum, s_bco = (small[:, 96 + 16 * n:112 + 16 * n] for n in range(4))

        O_PARTS = (slice(8, 12), slice(0, 8), slice(12, 16))
        FOX_AT = GLA_H * HD

        def by_head(v):
            return v.rearrange("p (b h) -> p b h", b=SB)

        def branch_row(x, t, r, b):
            return 8 * (x % 2) + 4 * t + 2 * r + b

        def branch_prob(x, t, r, b):
            c = r * S if b else 2 * S + r * P
            return prob[:, x % 2, t, c:c + (S if b else P)]

        def branch_logits(x, t, r, b):
            c = t * 1024 + (r * S if b else 2 * S + r * P)
            return pair_bank(x)[:, c:c + (S if b else P)]

        def pair_bank(x):
            return ps_a if x % 2 else ps_b

        norms = [mem_rows, h, h, h, mix, h, h]
        norm_loaded = [[sem(f"{n}_loaded{j}") for j in range(4)] for n in ("mem", "x", "mem2")]
        QUADS = {}
        at = 0
        for name, kb in (("n0", 16), ("n2", 16), ("o", 16), ("n3", 16), ("n4", 16), ("y1", 16), ("m2", 16),
                         ("n5", 16), ("xo", 4), ("n6", 16)):
            QUADS[name] = (at, SB * kb // 4)
            at += SB * kb // 4

        def quad_dst(name, k):
            return k % SB, 4 * (k // SB)

        def opening(groups, halves, group, half_):
            group(0)
            for j in range(groups):
                if j + 1 < groups:
                    group(j + 1)
                for k in range(2 * j, 2 * j + 2):
                    if k < halves:
                        half_(k)

        def kv_rows(b, n):
            return proj2[:, b, NKV + n * 256:NKV + (n + 1) * 256].rearrange("p (g d) -> p g d", d=HD2)

        @block.scalar
        def _(act):
            order = [0]

            def link(ins):
                order[0] += 1
                ins.then_inc(act_order, 1)
                act.wait_ge(act_order, order[0])

            def copy(o, i):
                return nc.scalar.copy(o, i)

            act.dma_start(base[:, 0:P], c_base[:, 0:P]).then_inc(ld["ident"], 16)
            for n, g in enumerate(("attn_norm_g", "mem_norm_g", "mlp_norm_g", "ln_mix_pre_2", "ln_x_pre_2", "ln_mem_2",
                                   "ln_ffn_pre_2", "out_norm_g")):
                g = a[g] if len(a[g].shape) == 1 else a[g][0]
                act.dma_start(gains[16 * n:16 * n + 16, :], g.rearrange("(r c) -> r c", c=P)).then_inc(ld["gains"], 16)
            act.dma_start(gains2[0:4, :], a["gla_a_b"].rearrange("(r c) -> r c", c=P)).then_inc(ld["gains2"], 16)
            for n, g in enumerate(("fox_q_norm_g", "fox_k_norm_g", "mem_q_norm_g", "mem_k_norm_g")):
                act.dma_start(gains2[4 + n:5 + n, :], a[g].rearrange("(r c) -> r c", c=P)).then_inc(ld["gains2"], 16)
            act.dma_start(gains2[8:16, :], a["pool_scale_2"][0].rearrange("(r c) -> r c", c=P)).then_inc(ld["gains2"], 16)

            def hi(q, i=None, halves=0, chunk=None, kn_=None):
                c = chunk
                more = 0 if i is None else i
                act.wait_ge(w_loaded[c % SLOTS], 16 * (loads_before(c) + 1) + more * (16 * halves // 8))
                if q >= 4:
                    act.wait_ge(pe_half, q - 3 + more * halves)
                j = q % 2
                if kn_ is None:
                    return copy(whi[:, q % 4], raw[:, c % SLOTS, 2 * j:2 * j + 2]).then_inc(hi_done, 1)
                n = kn_ * KB // 2
                return copy(whi[:, q % 4].rearrange("p k n -> p (k n)")[:, 0:n],
                            raw[:, c % SLOTS].rearrange("p k n -> p (k n)")[:, j * n:(j + 1) * n]).then_inc(hi_done, 1)

            def evict(t, q_end, dst, n):
                act.wait_ge(pe_half, q_end)
                act.wait_ge(n_rstd, n + 1)
                rstd = s_rstd2 if n == 4 else s_rstd
                for b in range(SB):
                    ins = nc.scalar.activation(dst(b), bank(2 * (t % 2) + b), ACT.Copy, scale=rstd[:, b:b + 1])
                ins.then_inc(evicted, 1)

            def post_squares(t, q_end):
                act.wait_ge(pe_half, q_end)
                if post_tile[0]:
                    act.wait_ge(post_sq, SB * post_tile[0])
                for b in range(SB):
                    nc.scalar.activation(junk2[:, b * NT:(b + 1) * NT], bank(2 * (t % 2) + b), ACT.Square,
                                               accum_out=s_pp[:, 4 * b + post_tile[0] % 4:4 * b + post_tile[0] % 4 + 1]
                                               ).then_inc(post_sq, 1)
                post_tile[0] += 1

            def load_sqrt():
                nc.scalar.activation(small[:, 248:250], s_var, ACT.Sqrt)

            post_tile = [0]

            def linear(name, first, last, out_of=None, kchunks=4, opened=0, behind={}):
                c0, q0, t0 = seg[name]
                n = 2 * kchunks
                pend = []
                for k in range(first * n, last * n):
                    if k >= opened:
                        hi(q0 + k, chunk=c0 + k // 2)
                    if k in behind:
                        behind[k]()
                    if out_of is not None:
                        if (k + 1) % n == 0:
                            pend.append((k + 3, k // n))
                        if pend and pend[0][0] <= k:
                            _, t = pend.pop(0)
                            out_of(t, t0 + t, q0 + (t + 1) * n)

                def rest():
                    for _, t in pend:
                        out_of(t, t0 + t, q0 + (t + 1) * n)
                return rest

            def looped(name, pairs):
                c0, q0, _ = seg[name]
                for k in range(8, 16):
                    hi(q0 + k, chunk=c0 + k // 2)
                with act.Fori(1, pairs) as i:
                    for k in range(16):
                        hi(q0 + k, i=i, halves=16, chunk=c0 + k // 2)

            def tail(name, n):
                c0, q0, t0 = seg[name]
                for k in range(2):
                    hi(q0 + k, chunk=c0, kn_=n)

            def square_sums(n):
                if n in (0, 1, 4):
                    for j in range(4):
                        act.wait_ge(norm_loaded[2 if n == 4 else n][j], 16)
                elif n == 2:
                    act.wait_ge(evicted, seg["mlp"][2])
                elif n == 3:
                    act.wait_ge(d_add, 64)
                else:
                    act.wait_ge(post_done, 8 * (n - 4))
                to = junk if n < 4 else junk3
                src = norms[n]
                for b in range(SB):
                    ins = nc.scalar.activation(to[:], src[:, b], ACT.Square, accum_out=s_sq[:, b:b + 1])
                    if b == 0:
                        link(ins)
                ins.then_inc(n_sq, 1)
                act.wait_ge(n_var, n + 1)
                nc.scalar.activation(s_std, s_var, ACT.Sqrt).then_inc(n_std, 1)

            def ahead_of(name):
                c0, q0, _ = seg[name]
                for k in range(2):
                    hi(q0 + k, chunk=c0)

            def hi_group(quads, j, x):
                t0 = QUADS[quads][0]
                for k in range(2 * j, 2 * j + 2):
                    b, kb = quad_dst(quads, k)
                    act.wait_ge(t_y, t0 + k + 1)
                    copy(x[:, kb:kb + 4, b * P:(b + 1) * P],
                         stage_t[:, (t0 + k) % 2].rearrange("p (k n) -> p k n", n=P)).then_inc(t_hi, 1)

            def enter(quads, name, free=None, halves=8, first=None, early=False, ahead_=3):
                c0, q0, _ = seg[name]
                t0, n = QUADS[quads]

                def group(j):
                    if j == 0 and free is not None:
                        act.wait_ge(pe_half, free)
                    hi_group(quads, j, xhi)

                def ahead(k):
                    if k + 4 < halves:
                        hi(q0 + k + 4, chunk=c0 + (k + 4) // 2)

                def begin(j):
                    if j == 0 and first is not None and not early:
                        first()
                    group(j)
                    if j == 0 and first is not None and early:
                        first()
                    if j == 0 and halves > 2:
                        for k in range(ahead_, 4):
                            hi(q0 + k, chunk=c0 + k // 2)

                if halves > 2:
                    for k in range(ahead_):
                        hi(q0 + k, chunk=c0 + k // 2)
                opening(n // 2, halves, begin, ahead)

            def q_end(name):
                names = list(seg)
                return seg[names[names.index(name) + 1]][1]

            def post_norm(n):
                act.wait_ge(post_var, n + 1)
                nc.scalar.activation(s_pstd, s_pvar, ACT.Sqrt).then_inc(post_std, 1)

            def load_post_gain(name):
                act.dma_start(post_gain[:], a[name][0:1, :].to_broadcast([P, D])).then_inc(ld["gain"], 16)

            enter("n0", "memkv", ahead_=2)
            square_sums(0)
            rest = linear("memkv", 0, 2, lambda t, tile, q: evict(tile, q, lambda b: mkv[:, b, t * NT:(t + 1) * NT], 0), opened=8)
            enter("n2", "in1", q_end("memkv"), first=rest, early=True)
            square_sums(1)
            c0, q0, _ = seg["in1"]
            act.dma_start(gw2[:], a["gla_a_w2"]).then_inc(ld["gw2"], 16)
            act.dma_start(fbias[:], a["fox_f_b"].rearrange("(r c) -> r c", c=1)).then_inc(ld["gw2"], 16)
            for k in range(8, 32):
                hi(q0 + k, chunk=c0 + k // 2)
            with act.Fori(2, T1 // 2 - 1) as i:
                for k in range(16):
                    hi(q0 + k, i=i, halves=16, chunk=c0 + k // 2)
            for k in range(16):
                kk = 8 * (T1 - 2) + k
                hi(q0 + kk, chunk=c0 + kk // 2)
                if k == 9:
                    act.wait_ge(hn["var"], 1)
                    nc.scalar.activation(s_hstd, s_hss, ACT.Sqrt).then_inc(hn["std"], 1)
                if k == 13:
                    act.wait_ge(gla["z"], 1)
                    link(nc.scalar.activation(gz[:], gz[:], ACT.Exp, scale=-1.0))
                    act.wait_ge(fx["z"], 2)
                    link(nc.scalar.activation(fct[:, 1], fct[:, 1], ACT.Exp, scale=-1.0))
                if k == 14:
                    nc.scalar.activation(gz[:], gz[:], ACT.Ln, bias=1.0).then_inc(gla["ln"], 1)
                    nc.scalar.activation(fct[:, 1], fct[:, 1], ACT.Ln, bias=1.0).then_inc(fx["ln"], 1)
            tail("tail1", TAIL1)

            def attn_rows(n, ps, q_scale, k_scale):
                act.wait_ge(a_tps, n + 1)
                q, k = (qt1, kt1) if n < 2 else (qt, kt)
                nc.scalar.activation(q[:].rearrange("p x s -> p (x s)"), ps[:, 0:1024], ACT.Copy, scale=q_scale)
                nc.scalar.activation(k[:].rearrange("p x s -> p (x s)"), ps[:, 1024:2048], ACT.Copy, scale=k_scale
                                     ).then_inc(a_tsb, 1)

            def exps(n, causal, ps=None):
                for half_ in range(2):
                    act.wait_ge(a_max, 2 * n + half_ + 1)
                    for y in range(4 * half_, 4 * half_ + 4):
                        keys = P if causal and y % 2 == 0 else S
                        src = pr[:, y, 0:keys] if causal else ps[:, y * S:(y + 1) * S]
                        ins = nc.scalar.activation(pr[:, y, 0:keys], src, ACT.Exp, bias=s_neg[:, y:y + 1],
                                                   accum_out=s_sum[:, y:y + 1])
                ins.then_inc(a_exp, 1)

            def probs(n, ps):
                act.wait_ge(a_pps, n + 1)
                copy(pt[:, 0:4], ps[:, 0:1024].rearrange("p (x k n) -> p x k n", k=2, n=P)).then_inc(a_psb, 1)

            def head_squares(heads, src, col, blocks=range(SB)):
                if squared:
                    act.wait_ge(o_sq, len(squared))
                squared.append(col)
                for b in blocks:
                    for hh in range(heads):
                        y = 16 * b + col + hh
                        ins = nc.scalar.activation(head_junk[:, b * heads + hh], src(hh, b), ACT.Square, accum_out=s_oss[:, y:y + 1])
                ins.then_inc(o_sq, 1)

            squared = []
            attn_rows(0, ps_b, gain2_t[:, G_FQ:G_FQ + 1], gain2_t[:, G_FK:G_FK + 1])

            def decay(l):
                act.wait_ge(gla["d"], l + 1)
                w = LEVELS_ALL[l]
                v = ge[:, l % 2].rearrange("p x (m t) -> p (x m) t", t=2 * w)
                nc.scalar.activation(v[:, :, w:], v[:, :, w:], ACT.Exp, scale=1.0 / GLA_TAU)
                nc.scalar.activation(v[:, :, 0:w], v[:, :, 0:w], ACT.Exp, scale=-1.0 / GLA_TAU).then_inc(gla["e"], 1)

            def head_std(n):
                act.wait_ge(o_var, n + 1)
                c = O_PARTS[n]
                nc.scalar.activation(by_head(s_ostd)[:, :, c], by_head(s_oss)[:, :, c], ACT.Sqrt).then_inc(o_std, 1)

            decay(0)
            decay(1)
            act.wait_ge(evicted, seg["wout"][2])
            nc.scalar.activation(proj1[:, :, GG:GG + 1024], proj1[:, :, GG:GG + 1024], ACT.Silu).then_inc(gate_done, 1)
            nc.scalar.activation(proj1[:, :, FG:FG + 512], proj1[:, :, FG:FG + 512], ACT.Sigmoid).then_inc(gate_done, 1)
            nc.scalar.activation(proj1[:, :, MG:MG + 512], proj1[:, :, MG:MG + 512], ACT.Sigmoid).then_inc(gate_done, 1)
            exps(0, True)
            decay(2)
            probs(0, ps_a)
            decay(3)
            act.wait_ge(a_o, 1)
            head_squares(4, lambda hh, b: ps_a[:, (2 * hh + b) * HD:(2 * hh + b + 1) * HD], 8)
            decay(4)
            attn_rows(1, ps_a, gain2_t[:, G_MQ:G_MQ + 1], gain2_t[:, G_MK:G_MK + 1])
            decay(5)
            decay(6)
            decay(7)
            head_std(0)
            exps(1, False, ps_a)
            probs(1, ps_a)
            act.wait_ge(gla["o"], 1)
            head_squares(8, lambda hh, b: ps_b[:, b * 1024 + hh * HD:b * 1024 + (hh + 1) * HD], 0, range(1))
            head_std(1)
            act.wait_ge(a_o, 2)
            head_squares(4, lambda hh, b: ps_a[:, (2 * hh + b) * HD:(2 * hh + b + 1) * HD], 12)
            head_std(2)
            enter("o", "wout")
            act.wait_ge(t_hi, sum(QUADS["o"]))
            act.dma_start(hot[:], c_hot).then_inc(ld["hot"], 16)
            act.dma_start(relt[0:32, :], a["rel_bias_2"].rearrange("h b -> b h"), allow_slow_non_contiguous=True).then_inc(ld["rel"], 16)
            linear("wout", 1, 4)
            enter("n3", "mlp", q_end("wout"), early=True)
            square_sums(2)

            c0, q0, _ = seg["mlp"]

            def up_rows(g, i=None):
                more = 0 if i is None else i
                q = q0 + 8 if g == 0 else q0 + 16 + 16 * (g - 1)
                act.wait_ge(pe_half, q + more * 16)
                if g or i is not None:
                    act.wait_ge(u_tps, g + more)
                else:
                    act.wait_ge(n_rstd, 3)
                for b in range(SB):
                    nc.scalar.activation(g_row[:, b], bank(b), ACT.Relu, scale=s_rstd[:, b:b + 1]).then_inc(silu_done, 1)
                for b in range(SB):
                    act.wait_ge(silu_done, 2 * g + b + 1 + (0 if i is None else i * 2))
                    ins = nc.scalar.activation(u_row[:, b], g_row[:, b], ACT.Square)
                ins.then_inc(u_row_done, 1)

            def up_hi(g, i=None, base_=0):
                more = 0 if i is None else i
                act.wait_ge(u_tps, base_ + g + 1 + more)
                copy(uhi[:].rearrange("p k (b n) -> p b k n", b=SB),
                     ps_b[:, 1024:2048].rearrange("p (b k n) -> p b k n", b=SB, k=4)).then_inc(u_hi, 1)

            for k in range(8, 16):
                hi(q0 + k, chunk=c0 + k // 2)
                if k == 10:
                    up_rows(0)
                if k == 14:
                    up_hi(0)
            ng = D_FF // NT
            with act.Fori(0, ng - 2) as i:
                for k in range(16):
                    hi(q0 + 16 + k, i=i, halves=16, chunk=c0 + 8 + k // 2)
                    if k == 2:
                        up_rows(1, i)
                    if k == 12:
                        up_hi(1, i)
            k0 = 16 + 16 * (ng - 2)
            for k in range(16):
                hi(q0 + k0 + k, chunk=c0 + (k0 + k) // 2)
                if k == 2:
                    up_rows(ng - 1)
                if k == 10:
                    up_hi(ng - 1)

            enter("n4", "in2", q_end("mlp"), early=True)
            square_sums(3)
            looped("in2", T2 // 2)
            linear("in2", T2 - 1, T2)
            act.wait_ge(evicted, seg["in2"][2] + 6)
            for kv in range(2):
                for b in range(SB):
                    ins = copy(kdup[:, b, kv], kv_rows(b, kv).unsqueeze(2).to_broadcast([P, NSA_G, 2, HD2]))
            ins.then_inc(ns["dup"], 1)
            tail("tail2", TAIL2)

            act.wait_ge(pe_half, q_end("tail2"))
            for kv in range(2):
                for t in range(2):
                    act.dma_start(pet[t * HD2:(t + 1) * HD2, kv], a["cmp_pe_2"][0, kv].rearrange("(l t) d -> t d l", t=2)[t],
                                  allow_slow_non_contiguous=True).then_inc(ld["cmp"], 16)
            for n, kv in enumerate((0, 0, 1)):
                act.dma_start(cw2[:, n], a["cmp_w2_2"][0, kv]).then_inc(ld["cmp"], 16)
            act.wait_ge(ns["t1"], 1)
            for n in range(2):
                nc.scalar.activation(nqt[:, 4 * n:4 * n + 4].rearrange("p x s -> p (x s)"), ps_b[:, n * 1024:(n + 1) * 1024], ACT.Copy,
                                     scale=HD2 ** -0.5).then_inc(ns["t1s"], 1)
            act.wait_ge(ns["t2"], 1)
            copy(nkt[:, 0:2].rearrange("p g r s -> p (g r s)"), ps_b[:, 0:1024]).then_inc(ns["t2_act"], 1)
            for r in range(2):
                for b in range(SB):
                    ins = copy(vdup[:, b, r], kv_rows(b, 3 + 2 * r).unsqueeze(2).to_broadcast([P, NSA_G, 2, HD2]))
            ins.then_inc(ns["vdup"], 1)
            act.wait_ge(evicted, seg["special"][2])
            nc.scalar.activation(gates, gates, ACT.Sigmoid).then_inc(ns["gate"], 1)
            for n in range(2):
                c = slice(NM + n * D, NM + (n + 1) * D)
                nc.scalar.activation(proj2[:, :, c], proj2[:, :, c], ACT.Sigmoid).then_inc(merge_gate, 1)
            act.wait_ge(ns["hid"], 1)
            act.wait_ge(ns["hidr"], 1)
            for kv in range(2):
                nc.scalar.activation(hid[:, kv, :, 0:N_CMP], bank(4 + kv)[:, 0:NSA_G * N_CMP].rearrange("p (g n) -> p g n", n=N_CMP),
                                     ACT.Gelu_apprx_tanh).then_inc(ns["gelu"], 1)
            act.wait_ge(ns["yps"], 1)
            copy(yt[:, 0:4].rearrange("p x s -> p (x s)"), ps_a[:, 0:1024]).then_inc(ns["ysb"], 1)
            act.wait_ge(ns["sub"], 1)
            nc.scalar.activation(pc[:], pc[:], ACT.Exp).then_inc(ns["exp"], 1)
            act.wait_ge(ns["pooled"], 1)
            copy(xhi[:, 8:16], yt[:]).then_inc(ns["pool_hi"], 1)

            def branch_exps(x, t):
                act.wait_ge(nb["max"], 2 * x + t + 1)
                for r in range(2):
                    for b in range(SB):
                        y = branch_row(x, t, r, b)
                        p = branch_prob(x, t, r, b)
                        ins = nc.scalar.activation(p, p, ACT.Exp, bias=s_bneg[:, y:y + 1], accum_out=s_bsum[:, y:y + 1])
                ins.then_inc(nb["exp"], 1)

            for t in range(2):
                branch_exps(0, t)
            c0, q0, _ = seg["br"]
            for x in range(8):
                for r in range(2):
                    if x < 7:
                        branch_exps(x + 1, r)
                    act.wait_ge(nb["pt"], 2 * x + r + 1)
                    copy(probt[:, x % 2, r * 768:r * 768 + 512], pair_bank(x)[:, r * 512:(r + 1) * 512]).then_inc(nb["pt_act"], 1)
                if x == 7:
                    act.wait_ge(nb["pv"], 7)
                    for k in range(4):
                        hi(q0 + k, chunk=c0 + k // 2)
                act.wait_ge(nb["y"], x + 1)
                copy(xhi[:, x], stage_t[:, x % 2, 0:S]).then_inc(nb["hi"], 1)
            linear("br", 0, 2, kchunks=2, opened=4)
            linear("br", 2, 8, kchunks=2)
            enter("y1", "mixo", q_end("br"), early=True)
            load_post_gain("ln_mix_post_2")
            m2 = {20 + 2 * j: (lambda j=j: hi_group("m2", j, x2hi)) for j in range(4)}
            m2[28] = lambda: square_sums(4)
            rest = linear("mixo", 0, 4, lambda t, tile, q: post_squares(tile, q), opened=8, behind=m2)

            def some(name, first, last):
                c0, q0, _ = seg[name]
                for k in range(first, last):
                    hi(q0 + k, chunk=c0 + k // 2)

            some("xk", 0, 3)
            rest()
            post_norm(0)
            some("xk", 3, 6)
            hi_group("n5", 0, xhi)
            some("xk", 6, 7)
            hi_group("n5", 1, xhi)
            some("xk", 7, 8)
            hi_group("n5", 2, xhi)
            some("xq", 0, 1)
            hi_group("n5", 3, xhi)
            some("xq", 1, 3)
            evict(seg["xk"][2], q_end("xk"), lambda b: xkv[:, b, 0:512], 4)
            act.wait_ge(post_done, 8)
            load_post_gain("ln_x_post_2")
            some("xq", 3, 6)
            square_sums(5)
            some("xq", 6, 8)
            some("xv", 0, 2)
            evict(seg["xq"][2], q_end("xq"), lambda b: qx[:, b], 5)
            some("xv", 2, 4)
            attn_rows(2, ps_b, HD ** -0.5, 1.0)
            some("xv", 4, 8)
            exps(2, False, ps_b)
            ahead_of("xo")
            evict(seg["xv"][2], q_end("xv"), lambda b: xkv[:, b, 512:1024], 4)
            probs(2, ps_b)
            load_sqrt()
            enter("xo", "xo", q_end("xv"), halves=2)
            rest_xo = linear("xo", 0, 4, lambda t, tile, q: post_squares(tile, q), kchunks=1, opened=2)

            enter("n6", "ffn", q_end("xo"), first=lambda: (rest_xo(), post_norm(1)))
            square_sums(6)
            act.wait_ge(post_done, 16)
            load_post_gain("ln_ffn_post_2")
            c0, q0, _ = seg["ffn"]
            ng = D_FF2 // NT
            gbase, sbase = D_FF // NT, 2 * (D_FF // NT)

            def gate_rows(g, i=None):
                more = 0 if i is None else i
                q = q0 + 8 if g == 0 else q0 + 24 + 24 * (g - 1)
                act.wait_ge(pe_half, q + more * 24)
                if g or i is not None:
                    act.wait_ge(u_row_done, gbase + g + more)
                else:
                    act.wait_ge(n_rstd, 7)
                for b in range(SB):
                    nc.scalar.activation(g_row[:, b], bank(b), ACT.Silu, scale=s_rstd[:, b:b + 1]).then_inc(silu_done, 1)

            for k in range(8, 16):
                hi(q0 + k, chunk=c0 + k // 2)
                if k == 10:
                    gate_rows(0)
            for k in range(16, 32):
                hi(q0 + k, chunk=c0 + k // 2)
                if k == 26:
                    gate_rows(1)
                    up_hi(0, base_=gbase)
            with act.Fori(0, ng - 2) as i:
                for k in range(24):
                    hi(q0 + 32 + k, i=i, halves=24, chunk=c0 + 16 + k // 2)
                    if k == 18:
                        gate_rows(2, i)
                        up_hi(1, i, gbase)
            k0 = 32 + 24 * (ng - 2)
            for k in range(16):
                hi(q0 + k0 + k, chunk=c0 + (k0 + k) // 2)
                if k == 10:
                    up_hi(ng - 1, base_=gbase)
            load_sqrt()
            for t in range(4):
                act.wait_ge(d_add, 4 * gbase + 4 * (ng - 1) + t + 1)
                act.wait_ge(post_sq, SB * (8 + t))
                for b in range(SB):
                    nc.scalar.activation(junk2[:, b * NT:(b + 1) * NT], ybuf[:, b, t * NT:(t + 1) * NT], ACT.Square,
                                               accum_out=s_pp[:, 4 * b + t:4 * b + t + 1]).then_inc(post_sq, 1)
            post_norm(2)

        @block.gpsimd
        def _(pool):
            def load_rows(n, rows_, src):
                for j in range(4):
                    if n == 0 and j == 2:
                        pool.wait_ge(ld["gains"], 16 * 8)
                        pool.wait_ge(ld["gains2"], 16 * 6)
                    c = slice(j * NT, (j + 1) * NT)
                    pool.dma_start(rows_[:, :, c], a[src][0].rearrange("(b p) d -> p b d", p=P)[:, :, c]).then_inc(norm_loaded[n][j], 16)

            load_rows(0, mem_rows, "mem")
            pool.wait_ge(pe_half, 1)
            load_rows(1, h, "x")
            pool.wait_ge(pe_half, 8)
            pool.dma_start(base[:, P:], c_base[:, P:]).then_inc(ld["base"], 16)

            G = nc.gpsimd

            normed = (proj1[:, :, FQ:FQ + 512], proj1[:, :, FK:FK + 512], mkv[:, :, 0:512], proj1[:, :, MQ:MQ + 512])
            pool.wait_ge(hn["rstd"], 1)
            for n, v in enumerate(normed):
                for b in range(SB):
                    rows_ = v[:, b].rearrange("p (h d) -> p h d", d=HD)
                    ins = G.tensor_tensor(rows_, rows_, s_hrstd[:, 8 * n + 4 * b:8 * n + 4 * b + 4].unsqueeze(2).to_broadcast([P, 4, HD]), ALU.mult)
                if n % 2:
                    ins.then_inc(hn["rows"], 1)
            pool.wait_ge(pe_half, seg["wout"][1])

            def distance(l):
                w = LEVELS_ALL[l]
                if l >= 2:
                    pool.wait_ge(gla["q"], l - 1)
                    pool.wait_ge(gla["k"], l - 1)
                else:
                    pool.wait_ge(gla["b"], 1)
                v = gbt[:].rearrange("p x (m t) -> p (x m) t", t=2 * w)
                G.tensor_tensor(ge[:, l % 2].rearrange("p x (m t) -> p (x m) t", t=2 * w), v,
                                v[:, :, w - 1:w].to_broadcast([P, 4 * S // (2 * w), 2 * w]), ALU.subtract).then_inc(gla["d"], 1)

            distance(0)
            G.memset(gke[:], 0.0).then_inc(gla["zero"], 1)
            pool.wait_ge(gla["zero"], 1)
            for l in range(8):
                w = LEVELS_ALL[l]
                if l < 7:
                    distance(l + 1)
                pool.wait_ge(gla["e"], l + 1)
                if l >= 2:
                    pool.wait_ge(gla["s"], l - 1)
                first = [t.rearrange("p x (m t) -> p (x m) t", t=2 * w)[:, :, 0:w] for t in (gke[:, l % 2], gkt[:], ge[:, l % 2])]
                G.tensor_tensor(*first, ALU.mult).then_inc(gla["k"], 1)

            pool.wait_ge(fx["rstd"], 1)
            pool.wait_ge(gate_done, 2)
            fox_mix = mix[:, :, FOX_AT:FOX_AT + 512]
            for b in range(SB):
                G.tensor_tensor(fox_mix[:, b].rearrange("p (h d) -> p h d", d=HD), fox_o[:, b].rearrange("p (h d) -> p h d", d=HD),
                                s_orstd[:, 16 * b + 8:16 * b + 12].unsqueeze(2).to_broadcast([P, 4, HD]), ALU.mult).then_inc(fx["over"], 1)
            for b in range(SB):
                pool.wait_ge(fx["over"], b + 1)
                ins = G.tensor_tensor(fox_mix[:, b], fox_mix[:, b], proj1[:, b, FG:FG + 512], ALU.mult)
            ins.then_inc(fx["mixed"], 1)

            pool.wait_ge(ns["tpsb"], 1)
            pool.dma_start(toep_dram, toep[:]).then_inc(ld["toep"], 16)
            pool.wait_ge(ld["toep"], 16)
            for hh in range(NSA_H):
                pool.dma_start(flip[:, hh], bass.AP(toep_dram.tensor, hh * 512, [[1, P], [1, S]])).then_inc(ld["flip"], 16)

            pool.wait_ge(t_ps, sum(QUADS["y1"]))
            load_rows(2, mix, "mem_2")

        @block.vector
        def _(dve):
            order = [0]
            V = nc.vector

            def link(ins):
                order[0] += 1
                ins.then_inc(dve_order, 1)
                dve.wait_ge(dve_order, order[0])

            def lo(q, i=None, halves=0, chunk=None, kn_=None):
                more = 0 if i is None else i
                dve.wait_ge(hi_done, q + 1 + more * halves)
                j, c = q % 2, chunk
                if kn_ is None:
                    return V.tensor_tensor(wlo[:, q % 4], raw[:, c % SLOTS, 2 * j:2 * j + 2], whi[:, q % 4].bitcast(F32),
                                           ALU.subtract).then_inc(lo_done, 1)
                n = kn_ * KB // 2
                return V.tensor_tensor(wlo[:, q % 4].rearrange("p k n -> p (k n)")[:, 0:n],
                                       raw[:, c % SLOTS].rearrange("p k n -> p (k n)")[:, j * n:(j + 1) * n],
                                       whi[:, q % 4].rearrange("p k n -> p (k n)")[:, 0:n].bitcast(F32),
                                       ALU.subtract).then_inc(lo_done, 1)

            def q_end(name):
                names = list(seg)
                return seg[names[names.index(name) + 1]][1]

            def linear(name, first, last, evict=None, kchunks=4, opened=0, behind={}):
                c0, q0, t0 = seg[name]
                n = 2 * kchunks
                pend = []
                for k in range(first * n, last * n):
                    if k >= opened:
                        lo(q0 + k, chunk=c0 + k // 2)
                    if k in behind:
                        behind[k]()
                    if evict is not None:
                        if (k + 1) % n == 0:
                            pend.append((k + 3, k // n))
                        if pend and pend[0][0] <= k:
                            _, t = pend.pop(0)
                            dve.wait_ge(pe_half, q0 + (t + 1) * n)
                            evict(t, t0 + t)

                def rest():
                    for _, t in pend:
                        dve.wait_ge(pe_half, q0 + (t + 1) * n)
                        evict(t, t0 + t)
                return rest

            def looped(name, pairs, odd, proj):
                c0, q0, t0 = seg[name]

                def out_of(t, col):
                    for b in range(SB):
                        ins = V.tensor_scalar(proj[:, b, col], bank(2 * ((t0 + t) % 2) + b), s_rstd[:, b:b + 1], None, ALU.mult)
                    ins.then_inc(evicted, 1)

                for k in range(8, 16):
                    lo(q0 + k, chunk=c0 + k // 2)
                    if k == 10:
                        dve.wait_ge(pe_half, q0 + 8)
                        out_of(0, slice(0, NT))
                with dve.Fori(1, pairs) as i:
                    for k in range(16):
                        lo(q0 + k, i, 16, chunk=c0 + k // 2)
                        if k == 2:
                            dve.wait_ge(pe_half, q0 + i * 16)
                            out_of(1, bass.ds(i * (2 * NT) - NT, NT))
                        if k == 10:
                            dve.wait_ge(pe_half, q0 + 8 + i * 16)
                            out_of(0, bass.ds(i * (2 * NT), NT))
                last = 2 * pairs - 1
                if odd:
                    for k in range(8):
                        lo(q0 + 16 * pairs + k, chunk=c0 + 8 * pairs + k // 2)
                        if k == 2:
                            dve.wait_ge(pe_half, q0 + 16 * pairs)
                            out_of(last, slice(last * NT, (last + 1) * NT))
                    last += 1
                return q0 + 8 * (last + 1), lambda: out_of(last, slice(last * NT, (last + 1) * NT))

            def tail(nth, name, n, before, proj, c1, ahead=None):
                c0, q0, t0 = seg[name]
                for k in range(2):
                    lo(q0 + k, chunk=c0, kn_=n)
                q, out_of = before
                if ahead is not None:
                    ahead()
                dve.wait_ge(pe_half, q)
                out_of()
                dve.wait_ge(pe_half, q0 + 2)
                V.tensor_copy(stage_t[0:n, 0, 0:S], bank(2 * (t0 % 2))[0:n, 0:S]).then_inc(tail_sb, 1)
                dve.wait_ge(tail_ps, nth)
                for b in range(SB):
                    ins = V.tensor_scalar(proj[:, b, c1:c1 + n], bank(2 * (t0 % 2) + 1)[:, b * n:(b + 1) * n], s_rstd[:, b:b + 1], None, ALU.mult)
                ins.then_inc(evicted, 1)

            def row_scale(n):
                dve.wait_ge(n_sq, n + 1)
                V.tensor_scalar(s_var, s_sq, 1.0 / D, EPS, ALU.mult, ALU.add).then_inc(n_var, 1)
                dve.wait_ge(n_std, n + 1)
                V.reciprocal(s_rstd2 if n == 4 else s_rstd, s_std).then_inc(n_rstd, 1)
                dve.wait_ge(n_rstd, n + 1)

            def ahead_of(name):
                c0, q0, _ = seg[name]
                for k in range(2):
                    lo(q0 + k, chunk=c0)

            def turned_rows(quads, j, gain):
                t0 = QUADS[quads][0]
                for k in range(2 * j, 2 * j + 2):
                    b, kb = quad_dst(quads, k)
                    dve.wait_ge(t_ps, t0 + k + 1)
                    if t0 + k >= 2:
                        dve.wait_ge(t_lo, t0 + k - 1)
                    ps = bank(4 + (t0 + k + 2) % 4)
                    if gain is None:
                        ins = V.tensor_copy(stage_t[:, (t0 + k) % 2], ps)
                    else:
                        ins = V.tensor_tensor(stage_t[:, (t0 + k) % 2].rearrange("p (k n) -> p k n", n=P),
                                              ps.rearrange("p (k n) -> p k n", n=P),
                                              gain[:, kb:kb + 4].unsqueeze(2).to_broadcast([P, 4, P]), ALU.mult)
                    ins.then_inc(t_y, 1)

            def lo_group(quads, j, x, low):
                t0 = QUADS[quads][0]
                for k in range(2 * j, 2 * j + 2):
                    b, kb = quad_dst(quads, k)
                    dve.wait_ge(t_hi, t0 + k + 1)
                    V.tensor_tensor(low[:, kb:kb + 4, b * P:(b + 1) * P],
                                    stage_t[:, (t0 + k) % 2].rearrange("p (k n) -> p k n", n=P),
                                    x[:, kb:kb + 4, b * P:(b + 1) * P].bitcast(F32), ALU.subtract).then_inc(t_lo, 1)

            def enter(quads, name, gain=None, halves=8, first=None, rows_of=None, late=False,
                      early=False, ahead_=3):
                c0, q0, _ = seg[name]
                t0, n = QUADS[quads]

                def group_rows(j):
                    turned_rows(quads, j, gain)

                def group(j):
                    if j or not early:
                        group_rows(j)
                    if j == 0 and early and first is not None:
                        first()
                    if rows_of is not None and j + 1 < n // 2:
                        rows_of(j + 1)
                    lo_group(quads, j, xhi, xlo)

                def ahead(k):
                    if k + 4 < halves:
                        lo(q0 + k + 4, chunk=c0 + (k + 4) // 2)

                def begin(j):
                    if j == 0 and first is not None and not early:
                        first()
                    group(j)
                    if j == 0 and late:
                        for k in range(4):
                            lo(q0 + k, chunk=c0 + k // 2)
                    elif j == 0 and halves > 2:
                        for k in range(ahead_, 4):
                            lo(q0 + k, chunk=c0 + k // 2)

                if halves > 2 and not late:
                    for k in range(ahead_):
                        lo(q0 + k, chunk=c0 + k // 2)
                if early:
                    group_rows(0)
                opening(n // 2, halves, begin, ahead)

            def post_gained(n):
                def evict(t, tile):
                    dve.wait_ge(ld["gain"], 16 * (n + 1))
                    for b in range(SB):
                        dve.wait_ge(post_sq, SB * (4 * n + t) + b + 1)
                        ins = V.tensor_tensor(ybuf[:, b, t * NT:(t + 1) * NT], bank(2 * (tile % 2) + b),
                                              post_gain[:, t * NT:(t + 1) * NT], ALU.mult)
                    ins.then_inc(evicted, 1)
                return evict

            def post_rows(pairs):
                for t, b in pairs:
                    c = slice(t * NT, (t + 1) * NT)
                    V.scalar_tensor_tensor(h[:, b, c], ybuf[:, b, c], s_prstd[:, b:b + 1], h[:, b, c], ALU.mult,
                                           ALU.add).then_inc(post_done, 1)

            def post_group(j):
                post_rows([(j, b) for b in range(SB)])

            def post_norm(n):
                dve.wait_ge(post_sq, SB * 4 * (n + 1))
                link(V.reduce_sum(s_psq, s_pp.rearrange("p (b t) -> p b t", t=4), axis=AX))
                V.tensor_scalar(s_pvar, s_psq, 1.0 / D, EPS, ALU.mult, ALU.add).then_inc(post_var, 1)
                dve.wait_ge(post_std, n + 1)
                link(V.reciprocal(s_prstd, s_pstd))

            dve.wait_ge(gain_ps, 2)
            link(V.tensor_copy(gain_t[:], bank(7)[:, 0:P]))
            link(V.tensor_copy(gain2_t[:], bank(7)[:, P:P + 16]))
            V.tensor_scalar(gain2_t[:, G_FQ:G_FQ + 3:2], gain2_t[:, G_FQ:G_FQ + 3:2], HD ** -0.5, None, ALU.mult).then_inc(gain_sb, 1)
            dve.wait_ge(gain_sb, 1)

            enter("n0", "memkv", gain_t[:, G_MEM:G_MEM + 16], ahead_=2)
            row_scale(0)
            linear("memkv", 0, 2, opened=8)
            enter("n2", "in1", gain_t[:, G_ATTN:G_ATTN + 16], early=True)
            row_scale(1)
            c0, q0, t0 = seg["in1"]

            def in1_out(pos, col):
                for b in range(SB):
                    ins = V.tensor_scalar(proj1[:, b, col], bank(2 * ((t0 + pos) % 2) + b), s_rstd[:, b:b + 1], None, ALU.mult)
                ins.then_inc(evicted, 1)

            def cols(t):
                return slice(t * NT, (t + 1) * NT)

            for k in range(8, 32):
                lo(q0 + k, chunk=c0 + k // 2)
                if k % 8 == 2:
                    dve.wait_ge(pe_half, q0 + k - 2)
                    in1_out(k // 8 - 1, cols(IN1_FIRST[k // 8 - 1]))
            for k in range(32, 48):
                lo(q0 + k, chunk=c0 + k // 2)
                if k % 8 == 2:
                    dve.wait_ge(pe_half, q0 + k - 2)
                    in1_out(k // 8 - 1, cols(IN1_FIRST[-1] if k == 34 else IN1_LOOP[0]))
            with dve.Fori(3, T1 // 2 - 1) as i:
                for k in range(16):
                    lo(q0 + k, i, 16, chunk=c0 + k // 2)
                    if k % 8 == 2:
                        dve.wait_ge(pe_half, q0 + k - 2 + i * 16)
                        in1_out(k // 8 + 1, bass.ds(i * (2 * NT) + (IN1_LOOP[0] - 5 + k // 8) * NT, NT))
            dve.wait_ge(ld["gw2"], 32)
            link(V.memset(g_ones[:], 1.0))

            def products(x, y, width, out_):
                for b in range(SB):
                    for hh in range(512 // width):
                        c = slice(hh * width, (hh + 1) * width)
                        ins = V.tensor_tensor_reduce(squares[:, b, c], x[:, b, c], y[:, b, c], 1.0, 0.0, ALU.mult, ALU.add,
                                                     accum_out=out_[:, b * (512 // width) + hh:b * (512 // width) + hh + 1])
                link(ins)

            fq, fk, mq, gq, gk = (proj1[:, :, c:c + 512] for c in (FQ, FK, MQ, GQ, GK))
            mk = mkv[:, :, 0:512]
            sums = {0: (fq, fq, HD, s_hss[:, 0:8]), 1: (fk, fk, HD, s_hss[:, 8:16]), 3: (mk, mk, HD, s_hss[:, 16:24]),
                    6: (mq, mq, HD, s_hss[:, 24:32]), 13: (gq, gk, GLA_DK, s_diag)}
            for k in range(16):
                kk = 8 * (T1 - 2) + k
                lo(q0 + kk, chunk=c0 + kk // 2)
                if k in sums:
                    products(*sums[k])
                if k % 8 == 2:
                    dve.wait_ge(pe_half, q0 + kk - 2)
                    in1_out(kk // 8 - 1, cols(IN1_LAST[0] if k == 10 else IN1_LOOP[1] - 1))
                if k == 4:
                    dve.wait_ge(gla["tps"], 1)
                    V.tensor_scalar(gqt[:].rearrange("p x s -> p (x s)"), ps_b[:, 0:1024], GLA_DK ** -0.5, None, ALU.mult)
                if k == 5:
                    V.tensor_copy(gkt[:].rearrange("p x s -> p (x s)"), ps_b[:, 1024:2048]).then_inc(gla["tsb"], 1)
                if k == 7:
                    V.tensor_scalar(s_hss, s_hss, 1.0 / HD, EPS, ALU.mult, ALU.add).then_inc(hn["var"], 1)
                    dve.wait_ge(gla["gaps"], 1)
                    V.tensor_copy(gat[:], bank(4)[0:GLA_RANK, 0:S]).then_inc(gla["gat"], 1)
                    V.tensor_scalar(fct[:, 0], bank(5)[0:4, 0:S], fbias[:, 0:1], None, ALU.add).then_inc(fx["z"], 1)
                if k == 10:
                    dve.wait_ge(hn["std"], 1)
                    V.reciprocal(s_hrstd, s_hstd).then_inc(hn["rstd"], 1)
                if k == 11:
                    dve.wait_ge(gla["zps"], 1)
                    link(V.tensor_tensor(gl[:], ps_b[:, 1024:2048].rearrange("p (x s) -> p x s", s=S),
                                         gain2_t[:, B_GLA:B_GLA + 4].unsqueeze(2).to_broadcast([P, 4, S]), ALU.add))
                    V.scalar_tensor_tensor(gz[:], gl[:], -1.0, gl[:], ALU.mult, ALU.max).then_inc(gla["z"], 1)
                    dve.wait_ge(fx["z"], 1)
                    V.scalar_tensor_tensor(fct[:, 1], fct[:, 0], -1.0, fct[:, 0], ALU.mult, ALU.max).then_inc(fx["z"], 1)

            def log_decays():
                dve.wait_ge(gla["ln"], 1)
                link(V.scalar_tensor_tensor(gl[:], gl[:], 0.0, gz[:], ALU.min, ALU.subtract))
                for x in range(4):
                    ins = V.tensor_tensor_scan(gbt[:, x], g_ones[:], gl[:, x], 0.0, ALU.mult, ALU.add)
                ins.then_inc(gla["b"], 1)
                dve.wait_ge(fx["ln"], 1)
                link(V.scalar_tensor_tensor(fct[:, 0], fct[:, 0], 0.0, fct[:, 1], ALU.min, ALU.subtract))
                link(V.tensor_tensor_scan(fct[:, 2], g_ones[0:4, :], fct[:, 0], 0.0, ALU.mult, ALU.add))
                link(V.tensor_copy(fc_parts[:, 0], fct[:, 2]))
                link(V.tensor_tensor(fct[:, 3], fct[:, 2], fc_parts[:, 0], ALU.subtract))
                link(V.tensor_copy(fc_parts[:, 1], fct[:, 3]))
                link(V.tensor_tensor(fct[:, 2], fct[:, 3], fc_parts[:, 1], ALU.subtract))
                V.tensor_copy(fc_parts[:, 2], fct[:, 2]).then_inc(fx["c"], 1)

            def last_out():
                in1_out(T1 - 1, cols(IN1_LAST[1]))

            tail(1, "tail1", TAIL1, (q0 + 8 * T1, last_out), proj1, T1 * NT, ahead=log_decays)

            dve.wait_ge(pe_half, q_end("tail1"))
            dve.wait_ge(ld["base"], 16)
            link(V.tensor_scalar(s_diag, s_diag, GLA_DK ** -0.5, None, ALU.mult))
            for b in range(SB):
                ins = V.tensor_tensor(att[:].rearrange("p (x b t) n -> p x b t n", b=SB, t=2)[:, :, b],
                                      ident.unsqueeze(1).unsqueeze(1).to_broadcast([P, 4, 2, P]),
                                      s_diag[:, 8 * b:8 * b + 8].rearrange("p (x t) -> p x t", t=2).unsqueeze(3).to_broadcast([P, 4, 2, P]),
                                      ALU.mult)
            V.memset(gqe[:], 0.0).then_inc(gla["att0"], 1)
            dve.wait_ge(gla["att0"], 1)

            def decayed_q(l):
                dve.wait_ge(gla["e"], l + 1)
                if l >= 2:
                    dve.wait_ge(gla["s"], l - 1)
                w = LEVELS_ALL[l]
                for t in range(2):
                    r = slice(t * GLA_DK, (t + 1) * GLA_DK)
                    q, e = (v.rearrange("p x (m t) -> p x m t", t=2 * w)[r, :, :, w:] for v in (gqt[:], ge[:, l % 2]))
                    ins = V.tensor_tensor(gqe[r, l % 2, :, t].rearrange("p x (m t) -> p x m t", t=w), q, e, ALU.mult)
                ins.then_inc(gla["q"], 1)

            def scores(l):
                dve.wait_ge(gla["s"], l + 1)
                ps = ps_b[:, (l % 2) * 1024:(l % 2 + 1) * 1024]
                if l == 7:
                    V.tensor_copy(att10[:], ps.rearrange("p (y n) -> p y n", n=P)).then_inc(gla["att"], 1)
                    return
                w = LEVELS[l]
                m = base[:, C_MASK + l * P:C_MASK + (l + 1) * P].bitcast(U32)
                if l:
                    dve.wait_ge(gla["att"], l)
                V.copy_predicated(att[:].rearrange("p y (m t) -> p y m t", t=2 * w)[:, :, :, w:],
                                  m.rearrange("p (m t) -> p m t", t=2 * w)[:, :, w:].unsqueeze(1).to_broadcast([P, 16, P // (2 * w), w]),
                                  ps.rearrange("p (y m t) -> p y m t", y=16, t=w)).then_inc(gla["att"], 1)

            def maxima(n, ps, causal):
                dve.wait_ge(a_log, n + 1)
                for half_ in range(2):
                    c = slice(4 * half_, 4 * half_ + 4)
                    if causal:
                        for y in range(4 * half_, 4 * half_ + 4):
                            b = y % 2
                            keys = S if b else P
                            ins = V.tensor_tensor_reduce(pr[:, y, 0:keys], ps[:, y * S:y * S + keys],
                                                         base[:, C_CAUSAL + b * S:C_CAUSAL + b * S + keys], 1.0, 3 * NEG, ALU.add, ALU.max,
                                                         accum_out=s_max[:, y:y + 1])
                    else:
                        ins = V.reduce_max(s_max[:, c], ps[:, half_ * 1024:(half_ + 1) * 1024].rearrange("p (y k) -> p y k", k=S), axis=AX)
                    link(ins)
                    V.tensor_scalar(s_neg[:, c], s_max[:, c], -1.0, None, ALU.mult).then_inc(a_max, 1)

            def probs(n, ps):
                dve.wait_ge(a_pps, n + 1)
                V.tensor_copy(pt[:, 4:8], ps[:, 1024:2048].rearrange("p (x k n) -> p x k n", k=2, n=P)).then_inc(a_psb, 1)
                dve.wait_ge(a_exp, n + 1)
                link(V.reciprocal(s_co, s_sum))

            def head_weights(n):
                dve.wait_ge(a_exp, n + 1)
                co = s_oco.rearrange("p (b h) -> p h b", b=SB)[:, 8 + 4 * n:12 + 4 * n]
                return V.reciprocal(co, s_sum.rearrange("p (h b) -> p h b", b=SB))

            def head_var(n):
                ss, co = (by_head(v)[:, :, O_PARTS[n]] for v in (s_oss, s_oco))
                link(V.tensor_tensor(ss, ss, co, ALU.mult))
                link(V.tensor_tensor(ss, ss, co, ALU.mult))
                V.tensor_scalar(ss, ss, 1.0 / HD, EPS, ALU.mult, ALU.add).then_inc(o_var, 1)

            def head_rstd(n):
                std, rstd, co = (by_head(v)[:, :, O_PARTS[n]] for v in (s_ostd, s_orstd, s_oco))
                dve.wait_ge(o_std, n + 1)
                link(V.reciprocal(rstd, std))
                return V.tensor_tensor(rstd, rstd, co, ALU.mult)

            V.memset(s_oco, 1.0)

            def turned_probs(n, ps):
                dve.wait_ge(a_pps, n + 1)
                V.tensor_copy(pt[:, 4:8], ps[:, 1024:2048].rearrange("p (x k n) -> p x k n", k=2, n=P)).then_inc(a_psb, 1)

            maxima(0, ps_a, True)
            for l in range(8):
                decayed_q(l)
                if l:
                    scores(l - 1)
                if l == 2:
                    link(head_weights(0))
                    turned_probs(0, ps_a)
                if l == 3:
                    dve.wait_ge(a_o, 1)
                    dve.wait_ge(o_sq, 1)
                    V.tensor_copy(fox_o[:].rearrange("p b (h d) -> p h b d", d=HD),
                                  ps_a[:, 0:1024].rearrange("p (h b d) -> p h b d", b=SB, d=HD)).then_inc(a_out, 1)
                    head_var(0)
                if l == 5:
                    maxima(1, ps_a, False)
            scores(7)
            turned_probs(1, ps_a)
            head_rstd(0).then_inc(fx["rstd"], 1)
            link(head_weights(1))
            dve.wait_ge(gla["o"], 2)
            second = head_junk[:, 8:16]
            link(V.tensor_copy(second.rearrange("p h d -> p (h d)"), ps_b[:, 1024:2048]))
            for hh in range(GLA_H):
                o = second[:, hh]
                ins = V.tensor_tensor_reduce(o, o, ps_b[:, 1024 + hh * HD:1024 + (hh + 1) * HD], 1.0, 0.0, ALU.mult, ALU.add, accum_out=s_oss[:, 16 + hh:17 + hh])
            link(ins)
            dve.wait_ge(o_sq, 2)
            head_var(1)

            def head_out(n):
                for b in range(SB):
                    if n < 8:
                        src, g = ps_b[:, b * 1024 + n * HD:b * 1024 + (n + 1) * HD], GG + n * HD
                    else:
                        src, g = ps_a[:, (2 * (n - 12) + b) * HD:(2 * (n - 12) + b + 1) * HD], MG + (n - 12) * HD
                    y = 16 * b + n
                    ins = V.scalar_tensor_tensor(mix[:, b, n * HD:(n + 1) * HD], src, s_orstd[:, y:y + 1], proj1[:, b, g:g + HD],
                                                 ALU.mult, ALU.mult)
                if n % 4 == 3:
                    ins.then_inc(o_rows, 1)

            dve.wait_ge(gate_done, 3)
            link(head_rstd(1))
            for n in range(8):
                head_out(n)
            dve.wait_ge(a_o, 2)
            dve.wait_ge(o_sq, 3)
            head_var(2)
            link(head_rstd(2))
            for n in range(12, 16):
                head_out(n)
            dve.wait_ge(o_rows, 3)
            dve.wait_ge(fx["mixed"], 1)
            enter("o", "wout", gain_t[:, G_OUT:G_OUT + 16], late=True)

            def add_to(dst, sem_):
                def evict(t, tile):
                    for b in range(SB):
                        ins = V.tensor_tensor(dst[:, b, t * NT:(t + 1) * NT], dst[:, b, t * NT:(t + 1) * NT],
                                              bank(2 * (tile % 2) + b), ALU.add)
                    ins.then_inc(sem_, 1)
                return evict

            dve.wait_ge(t_ps, sum(QUADS["o"]))

            def table_row():
                dve.wait_ge(ld["rel"], 16)
                V.memset(relt[32:33, :], 1.0).then_inc(ns["rel"], 1)

            def table_done():
                dve.wait_ge(ns["tp"], 1)
                V.tensor_copy(toep[:], bank(4)[0:16, :]).then_inc(ns["tpsb"], 1)

            linear("wout", 0, 3, add_to(h, evicted), opened=8, behind={11: table_row, 14: table_done})()
            for n in range(8):
                dve.wait_ge(ns["flip"], n + 1)
                V.tensor_copy(bias[:, 2 * n:2 * n + 2].rearrange("p h k -> p (h k)"), bank(4 + n % 4)).then_inc(ns["bias"], 1)
            rest_wout = linear("wout", 3, 4, add_to(h, evicted))
            enter("n3", "mlp", gain_t[:, G_MLP:G_MLP + 16], first=rest_wout, early=True)
            row_scale(2)

            def up_lo(g, i=None, base_=0):
                more = 0 if i is None else i
                dve.wait_ge(u_hi, base_ + g + 1 + more)
                V.tensor_tensor(ulo[:].rearrange("p k (b n) -> p b k n", b=SB),
                                ps_b[:, 1024:2048].rearrange("p (b k n) -> p b k n", b=SB, k=4),
                                uhi[:].rearrange("p k (b n) -> p b k n", b=SB).bitcast(F32), ALU.subtract).then_inc(u_lo, 1)

            def down_add(dst, t, q, i=None, per=16, first=False, n0=0, banks=2):
                dve.wait_ge(pe_half, q + (0 if i is None else i * per))
                if n0 or i is not None:
                    dve.wait_ge(d_add, n0 + (0 if i is None else i * 4))
                for b in range(SB):
                    ps = bank(banks + 2 * (t % 2) + b)
                    d = dst[:, b, t * NT:(t + 1) * NT]
                    ins = V.tensor_copy(d, ps) if first else V.tensor_tensor(d, d, ps, ALU.add)
                ins.then_inc(d_add, 1)

            c0, q0, _ = seg["mlp"]
            ng = D_FF // NT
            for k in range(8, 16):
                lo(q0 + k, chunk=c0 + k // 2)
                if k == 14:
                    up_lo(0)
            for k in range(16):
                lo(q0 + 16 + k, chunk=c0 + 8 + k // 2)
                if k in (4, 6, 8, 10):
                    down_add(h, k // 2 - 2, q0 + 16 + k - 2)
                if k == 12:
                    up_lo(1)
            with dve.Fori(1, ng - 2) as i:
                for k in range(16):
                    lo(q0 + 16 + k, i, 16, chunk=c0 + 8 + k // 2)
                    if k in (4, 6, 8, 10):
                        t = k // 2 - 2
                        down_add(h, t, q0 + 16 + k - 2, i, n0=t - 3)
                    if k == 12:
                        up_lo(1, i)
            k0 = 16 + 16 * (ng - 2)
            for k in range(16):
                lo(q0 + k0 + k, chunk=c0 + (k0 + k) // 2)
                if k in (4, 6, 8):
                    t = k // 2 - 2
                    down_add(h, t, q0 + k0 + k - 2, n0=4 * (ng - 2) + t - 3)
                if k == 10:
                    down_add(h, 3, q0 + k0 + 8, n0=4 * (ng - 2))
                    up_lo(ng - 1)
                if k in (12, 14):
                    t = k // 2 - 6
                    down_add(h, t, q0 + k0 + 10 + 2 * t, n0=4 * (ng - 1) + t - 3)
            def last_downs():
                for t in (2, 3):
                    down_add(h, t, q0_mlp + k0_mlp + 10 + 2 * t, n0=4 * (D_FF // NT - 1) + t - 3)

            q0_mlp, k0_mlp = q0, k0
            enter("n4", "in2", gain_t[:, G_MIX:G_MIX + 16], first=last_downs, early=True)
            row_scale(3)
            before = looped("in2", T2 // 2, True, proj2)
            for r in range(2):
                for b in range(SB):
                    ins = V.tensor_copy(kdup[:, b, 2 + r], kv_rows(b, 2 + 2 * r).unsqueeze(2).to_broadcast([P, NSA_G, 2, HD2]))
            ins.then_inc(ns["dup"], 1)
            tail(2, "tail2", TAIL2, before, proj2, T2 * NT)

            dve.wait_ge(pe_half, q_end("tail2"))
            V.memset(hid[:], 0.0)
            V.memset(kcbd[:], 0.0)
            V.memset(pc[:, 0, :, 7:16], NEG)
            V.memset(pc[:, 1, :, 15:16], NEG).then_inc(ns["hidr"], 1)
            dve.wait_ge(ns["hidr"], 1)
            dve.wait_ge(ns["tk"], 1)
            dve.wait_ge(ld["cmp"], 16 * 7)
            for kv in range(2):
                rawt = ps_a[:, kv * 1024:(kv + 1) * 1024].rearrange("p (g s) -> p g s", s=S)
                for t in range(2):
                    r = slice(t * HD2, (t + 1) * HD2)
                    for g in range(NSA_G):
                        v = rawt[r, g, t:t + 1]
                        win = bass.AP(v.tensor, v.offset, [list(v.ap[0]), [2, CMP_LEN // 2], [CMP_STRIDE, N_CMP]])
                        ins = V.tensor_tensor(xpe[r, kv, :, g], win, pet[r, kv].unsqueeze(2).to_broadcast([HD2, CMP_LEN // 2, N_CMP]),
                                              ALU.add)
                ins.then_inc(ns["xpe"], 1)
            dve.wait_ge(ns["t2"], 1)
            V.tensor_copy(nkt[:, 2:4].rearrange("p g r s -> p (g r s)"), ps_b[:, 1024:2048]).then_inc(ns["t2_dve"], 1)
            dve.wait_ge(ns["gelu"], 2)
            for g2 in range(2):
                for x in range(2):
                    ins = V.tensor_copy(hidr[:, g2, 4 * x:4 * x + 4], hid[:, 1, 2 * g2 + x].unsqueeze(1).to_broadcast([P, 4, 16]))
            ins.then_inc(ns["hidr"], 1)
            dve.wait_ge(ns["yps"], 1)
            V.tensor_copy(yt[:, 4:8].rearrange("p x s -> p (x s)"), ps_a[:, 1024:2048]).then_inc(ns["ysb"], 1)
            dve.wait_ge(ns["kv"], 1)
            for t in range(2):
                V.tensor_copy(kcbd[t * HD2:(t + 1) * HD2, :, t], bank(6)[t * HD2:(t + 1) * HD2, 0:64].rearrange("p (g n) -> p g n", n=16))
            for g2 in range(2):
                ins = V.tensor_tensor(vbd[:, g2], bank(7)[:, g2 * HD2:(g2 + 1) * HD2].unsqueeze(1).to_broadcast([P, 8, HD2]),
                                      blkmask.unsqueeze(2).to_broadcast([P, 8, HD2]), ALU.mult)
            ins.then_inc(ns["kvs"], 1)
            dve.wait_ge(ns["log"], 1)
            lg = bank(4).rearrange("p (b h n) -> p b h n", b=SB, n=16)
            for b in range(SB):
                n = N_CMP if b else 7
                off = 31 if b else 159
                link(V.tensor_tensor(pc[:, b, :, 0:n], lg[:, b, :, 0:n], bias[:, :, off:off + 16 * (n - 1) + 1:16], ALU.add))
            cview = pc[:].rearrange("p b h n -> p (b h) n")
            V.tensor_scalar(cmask[:], cview, NEG / 2, None, ALU.is_gt)
            link(V.reduce_max(s_cmax, cview, axis=AX))
            V.tensor_tensor(cview, cview, s_cmax.unsqueeze(2).to_broadcast([P, 32, 16]), ALU.subtract).then_inc(ns["sub"], 1)
            dve.wait_ge(ns["exp"], 1)
            link(V.tensor_tensor(cview, cview, cmask[:], ALU.mult))
            link(V.reduce_sum(s_csum, cview, axis=AX))
            link(V.tensor_scalar(s_csum, s_csum, 1.0, None, ALU.max))
            link(V.reciprocal(s_cinv, s_csum))
            dve.wait_ge(ns["gate"], 1)
            cinv = s_cinv.rearrange("p (b h) -> p b h", b=SB)
            link(V.tensor_tensor(cinv, cinv, gates.rearrange("p b (h c) -> p b h c", c=3)[:, :, :, 0], ALU.mult))
            V.tensor_tensor(cview, cview, s_cinv.unsqueeze(2).to_broadcast([P, 32, 16]), ALU.mult).then_inc(ns["p"], 1)
            dve.wait_ge(ns["pps"], 1)
            V.tensor_copy(pct[:].rearrange("p b x n -> p (b x n)"), bank(5)).then_inc(ns["psb"], 1)
            dve.wait_ge(ns["pool"], 1)
            V.tensor_tensor(yt[:], ps_a[:, :].rearrange("p (x s) -> p x s", s=S),
                            gain2_t[:, G_POOL:G_POOL + 8].unsqueeze(2).to_broadcast([P, 8, S]), ALU.mult).then_inc(ns["pooled"], 1)
            def branch_maxima(x):
                if x >= 2:
                    dve.wait_ge(nb["pt"], 2 * (x - 1))
                for t in range(2):
                    dve.wait_ge(nb["logits"], 2 * x + t + 1)
                    for r in range(2):
                        for b in range(SB):
                            y = branch_row(x, t, r, b)
                            ins = V.tensor_tensor_reduce(branch_prob(x, t, r, b), branch_logits(x, t, r, b),
                                                         bias[:, 2 * x + t, (0 if b else P):S], 1.0, 3 * NEG, ALU.add, ALU.max,
                                                         accum_out=s_bmax[:, y:y + 1])
                    link(ins)
                    y = branch_row(x, t, 0, 0)
                    V.tensor_scalar(s_bneg[:, y:y + 4], s_bmax[:, y:y + 4], -1.0, None, ALU.mult).then_inc(nb["max"], 1)

            def weights(x):
                dve.wait_ge(nb["exp"], 2 * x + 2)
                y = branch_row(x, 0, 0, 0)
                link(V.reciprocal(s_bco[:, y:y + 8], s_bsum[:, y:y + 8]))
                for t in range(2):
                    gv = gates[:, :, 3 * (2 * x + t) + 1:3 * (2 * x + t) + 3].rearrange("p b r -> p r b")
                    co = s_bco[:, y + 4 * t:y + 4 * t + 4].rearrange("p (r b) -> p r b", r=2)
                    ins = V.tensor_tensor(co, co, gv, ALU.mult)
                link(ins)
                V.tensor_tensor(diag[:, x % 2], ident.unsqueeze(1).to_broadcast([P, 8, P]),
                                s_bco[:, y:y + 8].unsqueeze(2).to_broadcast([P, 8, P]), ALU.mult).then_inc(nb["diag"], 1)

            def turned(x):
                for r in range(2):
                    dve.wait_ge(nb["pt"], 2 * x + r + 1)
                    V.tensor_copy(probt[:, x % 2, r * 768 + 512:(r + 1) * 768], pair_bank(x)[:, 1024 + r * 512:1280 + r * 512]
                                  ).then_inc(nb["pt_dve"], 1)

            def outputs(x):
                dve.wait_ge(nb["pv"], x + 1)
                if x >= 2:
                    dve.wait_ge(nb["lo"], x - 1)
                for t in range(2):
                    r = slice(t * HD2, (t + 1) * HD2)
                    ins = V.tensor_tensor(stage_t[r, x % 2, 0:S], pair_bank(x)[r, t * S:(t + 1) * S], cmp_o[r, x], ALU.add)
                ins.then_inc(nb["y"], 1)

            def outputs_lo(x):
                dve.wait_ge(nb["hi"], x + 1)
                V.tensor_tensor(xlo[:, x], stage_t[:, x % 2, 0:S], xhi[:, x].bitcast(F32), ALU.subtract).then_inc(nb["lo"], 1)

            branch_maxima(0)
            dve.wait_ge(ns["oc"], 1)
            V.tensor_copy(cmp_o[:].rearrange("p x s -> p (x s)"), ps_a[:, :]).then_inc(ns["cmp"], 1)
            weights(0)
            c0, q0, _ = seg["br"]
            for x in range(8):
                if x < 7:
                    branch_maxima(x + 1)
                turned(x)
                if x < 7:
                    weights(x + 1)
                outputs(x)
                if x:
                    outputs_lo(x - 1)
            lo(q0, chunk=c0)
            outputs_lo(7)
            for k in range(1, 4):
                lo(q0 + k, chunk=c0 + k // 2)

            dve.wait_ge(ns["pool_hi"], 1)
            V.tensor_tensor(xlo[:, 8:16], yt[:], xhi[:, 8:16].bitcast(F32), ALU.subtract).then_inc(nb["lo"], 1)
            dve.wait_ge(nb["lo"], 9)

            dve.wait_ge(merge_gate, 2)

            def merge(t, tile):
                br, n = t % 2, t // 2
                for b in range(SB):
                    dst = mix[:, b, n * NT:(n + 1) * NT]
                    gv = proj2[:, b, NM + br * D + n * NT:NM + br * D + (n + 1) * NT]
                    if br == 0:
                        ins = V.tensor_tensor(dst, bank(2 * (tile % 2) + b), gv, ALU.mult)
                    else:
                        ins = V.tensor_tensor(gv, bank(2 * (tile % 2) + b), gv, ALU.mult)
                ins.then_inc(evicted, 1)
                if br == 1:
                    dve.wait_ge(evicted, tile + 1)
                    for b in range(SB):
                        dst = mix[:, b, n * NT:(n + 1) * NT]
                        ins = V.tensor_tensor(dst, dst, proj2[:, b, NM + D + n * NT:NM + D + (n + 1) * NT], ALU.add)
                    ins.then_inc(y1_done, 1)

            rest_br = linear("br", 0, 8, merge, kchunks=2, opened=4)
            enter("y1", "mixo", first=rest_br, early=True)
            m2 = {19 + 2 * j: (lambda j=j: turned_rows("m2", j, gain_t[:, G_MEM2:G_MEM2 + 16])) for j in range(4)}
            m2.update({20 + 2 * j: (lambda j=j: lo_group("m2", j, x2hi, x2lo)) for j in range(4)})
            m2[28] = lambda: row_scale(4)
            rest = linear("mixo", 0, 4, post_gained(0), opened=8, behind=m2)

            def residual(n, rest):
                rest()
                post_norm(n)
                post_group(0)

            def some(name, first, last):
                c0, q0, _ = seg[name]
                for k in range(first, last):
                    lo(q0 + k, chunk=c0 + k // 2)

            def split(j):
                turned_rows("n5", j, gain_t[:, G_X:G_X + 16])
                lo_group("n5", j, xhi, xlo)

            some("xk", 0, 3)
            residual(0, rest)
            some("xk", 3, 4)
            post_group(1)
            some("xk", 4, 5)
            post_group(2)
            some("xk", 5, 6)
            post_group(3)
            split(0)
            some("xk", 6, 7)
            split(1)
            some("xk", 7, 8)
            split(2)
            some("xq", 0, 1)
            split(3)
            some("xq", 1, 6)
            row_scale(5)
            some("xq", 6, 8)
            some("xv", 0, 8)
            maxima(2, ps_b, False)
            ahead_of("xo")
            probs(2, ps_b)
            dve.wait_ge(a_o, 3)
            for b in range(SB):
                ins = V.tensor_tensor(mix[:, b, 0:512].rearrange("p (h d) -> p h d", d=HD),
                                      ps_b[:, 0:1024].rearrange("p (h b d) -> p h b d", b=SB, d=HD)[:, :, b],
                                      s_co.rearrange("p (h b) -> p h b", b=SB)[:, :, b].unsqueeze(2).to_broadcast([P, 4, HD]), ALU.mult)
            ins.then_inc(a_out, 1)
            enter("xo", "xo", halves=2)
            rest_xo = linear("xo", 0, 4, post_gained(1), kchunks=1, opened=2)
            enter("n6", "ffn", gain_t[:, G_FFN:G_FFN + 16], first=lambda: residual(1, rest_xo), rows_of=post_group)
            row_scale(6)
            c0, q0, _ = seg["ffn"]
            gbase, sbase, dbase = D_FF // NT, 2 * (D_FF // NT), 4 * (D_FF // NT)
            ng = D_FF2 // NT

            def up_rows(g, i=None):
                more = 0 if i is None else i
                q = q0 + 16 if g == 0 else q0 + 32 + 24 * (g - 1)
                dve.wait_ge(pe_half, q + more * 24)
                dve.wait_ge(silu_done, sbase + 2 * g + 2 + more * 2)
                dve.wait_ge(u_tps, gbase + g + more)
                for b in range(SB):
                    ins = V.scalar_tensor_tensor(u_row[:, b], bank(2 + b), s_rstd[:, b:b + 1], g_row[:, b], ALU.mult, ALU.mult)
                ins.then_inc(u_row_done, 1)

            for k in range(8, 32):
                lo(q0 + k, chunk=c0 + k // 2)
                if k == 18:
                    up_rows(0)
                if k == 26:
                    up_lo(0, base_=gbase)
            for k in range(24):
                lo(q0 + 32 + k, chunk=c0 + 16 + k // 2)
                if k == 2:
                    up_rows(1)
                if k in (4, 6, 8, 10):
                    down_add(ybuf, k // 2 - 2, q0 + 32 + k - 2, first=True, banks=4)
                if k == 18:
                    up_lo(1, base_=gbase)
            with dve.Fori(1, ng - 2) as i:
                for k in range(24):
                    lo(q0 + 32 + k, i, 24, chunk=c0 + 16 + k // 2)
                    if k == 2:
                        up_rows(1, i)
                    if k in (4, 6, 8, 10):
                        t = k // 2 - 2
                        down_add(ybuf, t, q0 + 32 + k - 2, i, 24, n0=dbase + t - 3, banks=4)
                    if k == 18:
                        up_lo(1, i, gbase)
            k0 = 32 + 24 * (ng - 2)
            for k in range(16):
                lo(q0 + k0 + k, chunk=c0 + (k0 + k) // 2)
                if k == 2:
                    up_rows(ng - 1)
                if k in (4, 6, 8):
                    t = k // 2 - 2
                    down_add(ybuf, t, q0 + k0 + k - 2, n0=dbase + 4 * (ng - 2) + t - 3, banks=4)
                if k == 10:
                    down_add(ybuf, 3, q0 + k0 + 8, n0=dbase + 4 * (ng - 2), banks=4)
                    up_lo(ng - 1, base_=gbase)
                if k in (12, 14):
                    t = k // 2 - 6
                    down_add(ybuf, t, q0 + k0 + 10 + 2 * t, n0=dbase + 4 * (ng - 1) + t - 3, banks=4)
            dve.wait_ge(ld["gain"], 16 * 3)

            def times_gain(t):
                dve.wait_ge(post_sq, SB * (8 + t + 1))
                for b in range(SB):
                    c = slice(t * NT, (t + 1) * NT)
                    ins = V.tensor_tensor(ybuf[:, b, c], ybuf[:, b, c], post_gain[:, c], ALU.mult)
                return ins

            times_gain(0)
            down_add(ybuf, 2, q0 + k0 + 14, n0=dbase + 4 * (ng - 1) - 1, banks=4)
            times_gain(1)
            down_add(ybuf, 3, q0 + k0 + 16, n0=dbase + 4 * (ng - 1), banks=4)
            times_gain(2)
            link(times_gain(3))
            post_norm(2)
            post_rows([(t, b) for b in range(SB) for t in range(4)])

        @block.tensor
        def _(pe):
            mm = nc.tensor.matmul

            def half(q, banks, kbs, first, last, i=None, halves=0, xh=None, xl=None):
                xh, xl = (xhi, xlo) if xh is None else (xh, xl)
                more = 0 if i is None else i
                pe.wait_ge(lo_done, q + 1 + more * halves)
                w0, w1_ = whi[:, q % 4], wlo[:, q % 4]
                for j, kb in enumerate(kbs):
                    for b in range(SB):
                        o = bank(banks[b])
                        x0, x1 = xh[:, kb, b * P:(b + 1) * P], xl[:, kb, b * P:(b + 1) * P]
                        mm(o, x0, w0[:, j], start=first and j == 0, stop=False)
                        mm(o, x0, w1_[:, j], start=False, stop=False)
                        ins = mm(o, x1, w0[:, j], start=False, stop=last and j == len(kbs) - 1)
                ins.then_inc(pe_half, 1)

            def free(t, i=None, tiles=0):
                if t >= 2:
                    pe.wait_ge(evicted, t - 1 + (0 if i is None else i * tiles))

            def tile(name, t, kchunks=4, kb0=0, i=None, tiles=0, halves=0, ahead=None, behind={}, x=(None, None)):
                c0, q0, t0 = seg[name]
                g = t0 + t
                free(g, i, tiles)
                n = 2 * kchunks
                for k in range(n):
                    if k == n - 2 and ahead is not None:
                        ahead()
                    half(q0 + t * n + k, (2 * (g % 2), 2 * (g % 2) + 1), (kb0 + 2 * k, kb0 + 2 * k + 1), k == 0, k == n - 1,
                         i=i, halves=halves, xh=x[0], xl=x[1])
                    if k in behind:
                        behind[k]()

            def looped(name, pairs):
                tile(name, 1)
                with pe.Fori(1, pairs) as i:
                    tile(name, 0, i=i, tiles=2, halves=16)
                    tile(name, 1, i=i, tiles=2, halves=16)

            def tail(name, n):
                c0, q0, t0 = seg[name]
                free(t0)
                o = bank(2 * (t0 % 2))[0:n, 0:S]
                for k in range(2):
                    q = q0 + k
                    pe.wait_ge(lo_done, q + 1)
                    w0, w1_ = (w[:, q % 4].rearrange("p k n -> p (k n)")[:, 0:8 * n].rearrange("p (k n) -> p k n", n=n) for w in (whi, wlo))
                    for j in range(8):
                        x0, x1 = xhi[:, 8 * k + j], xlo[:, 8 * k + j]
                        mm(o, w0[:, j], x0, start=k == 0 and j == 0, stop=False)
                        mm(o, w1_[:, j], x0, start=False, stop=False)
                        ins = mm(o, w0[:, j], x1, start=False, stop=k == 1 and j == 7)
                    ins.then_inc(pe_half, 1)

            def turn_tail(nth, name, n):
                pe.wait_ge(tail_sb, nth)
                rows_ = bank(2 * (seg[name][2] % 2) + 1)
                for b in range(SB):
                    ins = nc.tensor.transpose(rows_[:, b * n:(b + 1) * n], stage_t[0:n, 0, b * P:(b + 1) * P], base[0:n, C_ID:C_ID + n])
                ins.then_inc(tail_ps, 1)

            def turn_group(quads, src, ready, j):
                t0 = QUADS[quads][0]
                ready(j)
                for k in range(2 * j, 2 * j + 2):
                    b, kb = quad_dst(quads, k)
                    if t0 + k >= 4:
                        pe.wait_ge(t_y, t0 + k - 3)
                    o = bank(4 + (t0 + k + 2) % 4)
                    for m in range(4):
                        ins = nc.tensor.transpose(o[:, m * P:(m + 1) * P], src[:, b, (kb + m) * P:(kb + m + 1) * P], ident)
                    ins.then_inc(t_ps, 1)

            def enter(quads, name, src, ready, halves=8, early=False):
                c0, q0, tile0 = seg[name]
                t0, n = QUADS[quads]

                def group(j):
                    if j or not early:
                        turn_group(quads, src, ready, j)

                def first_half(k):
                    g, per = (tile0 + k // 4, 4) if name == "br" else (tile0, halves)
                    if k % per == 0 and name not in ("mlp", "ffn"):
                        free(g)
                    elif k == 0:
                        pe.wait_ge(evicted, tile0)
                    if k % 2 == 0:
                        pe.wait_ge(t_lo, t0 + k + 2)
                    bk = (0, 1) if name in ("mlp", "ffn") else (2 * (g % 2), 2 * (g % 2) + 1)
                    half(q0 + k, bk, (2 * k, 2 * k + 1), k % per == 0, k % per == per - 1)

                opening(n // 2, halves, group, first_half)

            pe.wait_ge(ld["ident"], 16)
            pe.wait_ge(ld["gains"], 16 * 8)
            nc.tensor.transpose(bank(7)[:, 0:P], gains[:], ident).then_inc(gain_ps, 1)
            pe.wait_ge(ld["gains2"], 16 * 6)
            nc.tensor.transpose(bank(7)[:, P:P + 16], gains2[:], base[0:16, C_ID:C_ID + 16]).then_inc(gain_ps, 1)
            pe.wait_ge(gain_sb, 1)

            def loaded(n):
                return lambda j: pe.wait_ge(norm_loaded[n][j], 16)

            enter("n0", "memkv", mem_rows, loaded(0))
            tile("memkv", 1, ahead=lambda: turn_group("n2", h, loaded(1), 0))
            enter("n2", "in1", h, loaded(1), early=True)
            c0, q0, _ = seg["in1"]
            for t in range(1, 4):
                tile("in1", t)
            with pe.Fori(2, T1 // 2 - 1) as i:
                tile("in1", 0, i=i, tiles=2, halves=16)
                tile("in1", 1, i=i, tiles=2, halves=16)
            t0 = seg["in1"][2]

            def gla_rows():
                for n, col in enumerate((GQ, GK)):
                    for x in range(4):
                        for b in range(SB):
                            ins = nc.tensor.transpose(ps_b[:, n * 1024 + x * S + b * P:n * 1024 + x * S + (b + 1) * P],
                                                      proj1[:, b, col + x * P:col + (x + 1) * P], ident)
                ins.then_inc(gla["tps"], 1)

            def decay_rows():
                pe.wait_ge(gla["tsb"], 1)
                for n, (col, rank) in enumerate(((GA, GLA_RANK), (FF, 4))):
                    for b in range(SB):
                        ins = nc.tensor.transpose(bank(4 + n)[0:rank, b * P:(b + 1) * P], proj1[:, b, col:col + rank], ident)
                ins.then_inc(gla["gaps"], 1)

            def decays():
                pe.wait_ge(gla["gat"], 1)
                pe.wait_ge(ld["gw2"], 32)
                for x in range(4):
                    ins = mm(ps_b[:, 1024 + x * S:1024 + (x + 1) * S], gw2[:, x * P:(x + 1) * P], gat[:], start=True, stop=True)
                ins.then_inc(gla["zps"], 1)

            def transposes_of(ps, qs, ks):
                for n, src in enumerate((qs, ks)):
                    for x in range(4):
                        for b in range(SB):
                            ins = nc.tensor.transpose(ps[:, n * 1024 + x * S + b * P:n * 1024 + x * S + (b + 1) * P],
                                                      src[:, b, x * P:(x + 1) * P], ident)
                ins.then_inc(a_tps, 1)

            def fox_rows():
                pe.wait_ge(hn["rows"], 1)
                pe.wait_ge(gla["z"], 1)
                transposes_of(ps_b, proj1[:, :, FQ:FQ + 512], proj1[:, :, FK:FK + 512])

            between = {3: gla_rows, 6: decay_rows, 9: decays, 14: fox_rows}
            for t in range(T1 - 2, T1):
                free(t0 + t)
                for k in range(8):
                    half(q0 + 8 * t + k, (2 * ((t0 + t) % 2), 2 * ((t0 + t) % 2) + 1), (2 * k, 2 * k + 1), k == 0, k == 7)
                    if 8 * (t - T1 + 2) + k in between:
                        between[8 * (t - T1 + 2) + k]()
            tail("tail1", TAIL1)


            def level(l):
                pe.wait_ge(gla["q"], l + 1)
                pe.wait_ge(gla["k"], l + 1)
                if l >= 2:
                    pe.wait_ge(gla["att"], l - 1)
                q, k = gqe[:, l % 2], gke[:, l % 2]
                for x in range(4):
                    c = (l % 2) * 1024 + x * S
                    if l == 7:
                        ins = mm(ps_b[:, c:c + S], k[:, x, 0:P], q[:, x].rearrange("p t n -> p (t n)"), start=True, stop=True)
                        continue
                    for b in range(SB):
                        ins = mm(ps_b[:, c + b * P:c + (b + 1) * P], k[:, x, b * P:(b + 1) * P], q[:, x, :, b * 64:(b + 1) * 64],
                                 start=True, stop=True)
                ins.then_inc(gla["s"], 1)

            def gla_out():
                for b in range(SB):
                    pe.wait_ge(gla["att"], 7 + b)
                    for hh in range(GLA_H):
                        x, t = hh // 2, hh % 2
                        o = ps_b[:, b * 1024 + hh * P:b * 1024 + (hh + 1) * P]
                        ins = mm(o, att[:, (x * SB + b) * 2 + t], proj1[:, b, GV + hh * P:GV + (hh + 1) * P], start=True, stop=b == 0)
                        if b:
                            ins = mm(o, att10[:, hh], proj1[:, 0, GV + hh * P:GV + (hh + 1) * P], start=False, stop=True)
                    ins.then_inc(gla["o"], 1)

            def logits(ps, n, forget, heads=range(4)):
                pe.wait_ge(a_tsb, n + 1)
                for hh in heads:
                    for b in range(SB):
                        y = 2 * hh + b
                        keys = P if forget and b == 0 else S
                        o = ps[:, y * S:y * S + keys]
                        q, k = (qt1, kt1) if n < 2 else (qt, kt)
                        ins = mm(o, q[:, hh, b * P:(b + 1) * P], k[:, hh, 0:keys], start=True, stop=not forget)
                        if forget:
                            one = base[0:4, C_SEL:C_ALL].bitcast(BF16)[:, hh * (S + P):(hh + 1) * (S + P)]
                            for part in range(3):
                                c = fc_parts[:, part]
                                mm(o, c[:, b * P:(b + 1) * P], one[:, 0:keys], start=False, stop=False)
                                ins = mm(o, one[:, S:S + P], c[:, 0:keys], start=False, stop=part == 2)
                return ins

            def turn(ps, n, causal):
                pe.wait_ge(a_exp, n + 1)
                for y in range(8):
                    for k in range(1 if causal and y % 2 == 0 else 2):
                        ins = nc.tensor.transpose(ps[:, y * S + k * P:y * S + (k + 1) * P], pr[:, y, k * P:(k + 1) * P], ident)
                ins.then_inc(a_pps, 1)

            def weigh(ps, n, v, causal):
                pe.wait_ge(a_psb, 2 * (n + 1))
                for y in range(8):
                    last = 0 if causal and y % 2 == 0 else 1
                    for k in range(last + 1):
                        ins = mm(ps[:, y * HD:(y + 1) * HD], pt[:, y, k], v(y // 2, k), start=k == 0, stop=k == last)
                ins.then_inc(a_o, 1)

            pe.wait_ge(fx["c"], 1)
            pe.wait_ge(ld["base"], 16)
            assert seg["tail1"][2] % 2 == 0
            pe.wait_ge(evicted, seg["tail1"][2])
            logits(ps_a, 0, True, (2, 3))
            turn_tail(1, "tail1", TAIL1)
            pe.wait_ge(evicted, seg["wout"][2])
            logits(ps_a, 0, True, (0, 1)).then_inc(a_log, 1)
            level(0)
            level(1)
            turn(ps_a, 0, True)
            level(2)
            weigh(ps_a, 0, lambda hh, k: proj1[:, k, FV + hh * HD:FV + (hh + 1) * HD], True)
            level(3)
            pe.wait_ge(a_out, 1)
            pe.wait_ge(hn["rows"], 2)
            transposes_of(ps_a, proj1[:, :, MQ:MQ + 512], mkv)
            level(4)
            logits(ps_a, 1, False).then_inc(a_log, 1)
            level(5)
            level(6)
            level(7)
            turn(ps_a, 1, False)
            gla_out()
            weigh(ps_a, 1, lambda hh, k: mkv[:, k, 512 + hh * HD:512 + (hh + 1) * HD], False)

            def heads_mixed(j):
                if j == 2:
                    pe.wait_ge(fx["mixed"], 1)
                else:
                    pe.wait_ge(o_rows, 3 if j == 3 else 2)

            enter("o", "wout", mix, heads_mixed)

            def table():
                pe.wait_ge(ld["hot"], 16)
                pe.wait_ge(ns["rel"], 1)
                pe.wait_ge(t_y, sum(QUADS["o"]))
                mm(bank(4)[0:16, :], relt[0:33, :], hot[0:33, 0:512], start=True, stop=True).then_inc(ns["tp"], 1)

            tile("wout", 1, behind={3: table})
            tile("wout", 2)
            pe.wait_ge(ns["tpsb"], 1)
            pe.wait_ge(ld["flip"], 16 * NSA_H)
            for n in range(8):
                if n >= 4:
                    pe.wait_ge(ns["bias"], n - 3)
                mm(bank(4 + n % 4), hot[:, 512:512 + P], flip[:, 2 * n:2 * n + 2].rearrange("p h k -> p (h k)"),
                   start=True, stop=True).then_inc(ns["flip"], 1)

            def added(j):
                pe.wait_ge(ns["bias"], 8)
                pe.wait_ge(evicted, seg["wout"][2] + j + 1)

            tile("wout", 3, ahead=lambda: turn_group("n3", h, added, 0))
            enter("n3", "mlp", h, added, early=True)

            c0, q0, _ = seg["mlp"]

            def up_tile(q, i=None, per=0, banks=(0, 1), between=None):
                for k in range(8):
                    half(q + k, banks, (2 * k, 2 * k + 1), k == 0, k == 7, i=i, halves=per)
                    if k == 2 and between is not None:
                        between()

            def u_transposes(g, i=None, base_=0):
                more = 0 if i is None else i
                pe.wait_ge(u_row_done, base_ + g + 1 + more)
                if base_ or g or i is not None:
                    pe.wait_ge(u_lo, base_ + g + more)
                for b in range(SB):
                    for j in range(4):
                        ins = nc.tensor.transpose(ps_b[:, 1024 + (b * 4 + j) * P:1024 + (b * 4 + j + 1) * P],
                                                  u_row[:, b, j * P:(j + 1) * P], ident)
                ins.then_inc(u_tps, 1)

            def down_tile(q, t, added, i=None, per=0, banks=2, add_step=4):
                if added is not None:
                    pe.wait_ge(d_add, added + (0 if i is None else i * add_step))
                for k in range(2):
                    half(q + k, (banks + 2 * (t % 2), banks + 2 * (t % 2) + 1), (2 * k, 2 * k + 1), k == 0, k == 1, i=i, halves=per,
                         xh=uhi, xl=ulo)

            def mlp_downs(q, g, i=None, ahead=None):
                more = 0 if i is None else i
                pe.wait_ge(u_lo, g + 1 + more)
                for t in range(4):
                    if t == 3 and ahead is not None:
                        ahead()
                    added = 4 * g + t - 1
                    down_tile(q + 2 * t, t, added if added > 0 else None, i, 16)

            ng = D_FF // NT
            pe.wait_ge(u_row_done, 1)
            up_tile(q0 + 8, between=lambda: u_transposes(0))
            mlp_downs(q0 + 16, 0)
            pe.wait_ge(u_row_done, 2)
            up_tile(q0 + 24, between=lambda: u_transposes(1))
            with pe.Fori(1, ng - 2) as i:
                pe.wait_ge(u_lo, i + 1)
                for t in range(4):
                    down_tile(q0 + 16 + 2 * t, t, t - 1, i, 16)
                pe.wait_ge(u_row_done, i + 2)
                up_tile(q0 + 24, i, 16, between=lambda: u_transposes(1, i))
            k0 = 16 + 16 * (ng - 2)
            mlp_downs(q0 + k0, ng - 2)
            pe.wait_ge(d_add, 4 * (ng - 1))
            u_transposes(ng - 1)

            def downs_added(j):
                pe.wait_ge(d_add, 4 * ng if j else 4 * (ng - 1) + 1)

            mlp_downs(q0 + k0 + 8, ng - 1, ahead=lambda: turn_group("n4", h, downs_added, 0))

            enter("n4", "in2", h, downs_added, early=True)
            looped("in2", T2 // 2)
            tile("in2", T2 - 1)
            tail("tail2", TAIL2)

            for x in range(8):
                for b in range(SB):
                    ins = nc.tensor.transpose(ps_b[:, x * S + b * P:x * S + (b + 1) * P],
                                              proj2[:, b, NQ + x * P:NQ + (x + 1) * P], ident)
            ins.then_inc(ns["t1"], 1)
            turn_tail(2, "tail2", TAIL2)
            pe.wait_ge(evicted, seg["special"][2])

            def dup_transposes(ps, kinds, swap):
                for n, kind in enumerate(kinds):
                    for g in range(NSA_G):
                        for b in range(SB):
                            c = ((2 * g + n) if swap else (4 * n + g)) * S + b * P
                            ins = nc.tensor.transpose(ps[:, c:c + P], kdup[:, b, kind, g].rearrange("p x d -> p (x d)"), ident)
                return ins

            pe.wait_ge(ns["dup"], 2)
            dup_transposes(ps_a, (0, 1), False).then_inc(ns["tk"], 1)
            pe.wait_ge(ns["t1s"], 2)
            dup_transposes(ps_b, (2, 3), True).then_inc(ns["t2"], 1)
            pe.wait_ge(ns["t2_act"], 1)
            for kv in range(2):
                pe.wait_ge(ns["xpe"], kv + 1)
                pe.wait_ge(sp_loaded[kv], 16)
                for l in range(CMP_LEN // 2):
                    w = raw[:, (special0 + kv) % SLOTS].rearrange("p k n -> p (k n)")[:, l * P:(l + 1) * P]
                    ins = mm(bank(4 + kv)[:, 0:NSA_G * N_CMP], w, xpe[:, kv, l].rearrange("p g n -> p (g n)"),
                             start=l == 0, stop=l == CMP_LEN // 2 - 1)
            ins.then_inc(ns["hid"], 1)
            pe.wait_ge(sp_loaded[2], 16)
            band = raw[:, (special0 + 2) % SLOTS].rearrange("p k n -> p (k n)").rearrange("p (b w s) -> p b w s", b=SB, w=4)
            for x in range(8):
                for b in range(SB):
                    ins = mm(ps_a[:, x * S:(x + 1) * S], proj2[:, b, NU + x * P:NU + (x + 1) * P], band[:, b, x // 2],
                             start=b == 0, stop=b == SB - 1)
            ins.then_inc(ns["yps"], 1)
            pe.wait_ge(ns["hidr"], 2)
            pe.wait_ge(ns["t2_dve"], 1)
            mm(bank(6)[:, 0:64], cw2[:, 0:2].rearrange("p x d -> p (x d)"), hid[:, 0].rearrange("p g n -> p (g n)"), start=True, stop=True)
            for g2 in range(2):
                ins = mm(bank(7)[:, g2 * HD2:(g2 + 1) * HD2], hidr[:, g2].rearrange("p x n -> p (x n)"), cw2[:, 2],
                         start=True, stop=True)
            ins.then_inc(ns["kv"], 1)
            pe.wait_ge(ns["kvs"], 1)
            for b in range(SB):
                for x in range(8):
                    ins = mm(bank(4)[:, (b * 8 + x) * 32:(b * 8 + x + 1) * 32], nqt[:, x, b * P:(b + 1) * P],
                             kcbd[:, x // 2].rearrange("p t n -> p (t n)"), start=True, stop=True)
            ins.then_inc(ns["log"], 1)
            pe.wait_ge(ns["ysb"], 2)
            pe.wait_ge(sp_loaded[3], 16)
            wp = raw[:, (special0 + 3) % SLOTS].rearrange("p k n -> p (k n)").rearrange("p (g k n) -> p g k n", g=4, k=2)
            for x in range(8):
                g = x // 2
                for k in range(2):
                    ins = mm(ps_a[:, x * S:(x + 1) * S], wp[:, g, k, (x % 2) * P:(x % 2 + 1) * P], yt[:, 2 * g + k],
                             start=k == 0, stop=k == 1)
            ins.then_inc(ns["pool"], 1)
            pe.wait_ge(ns["p"], 1)
            for b in range(SB):
                for g2 in range(2):
                    ins = nc.tensor.transpose(bank(5)[:, (b * 2 + g2) * P:(b * 2 + g2 + 1) * P],
                                              pc[:, b, 8 * g2:8 * g2 + 8].rearrange("p h n -> p (h n)"), ident)
            ins.then_inc(ns["pps"], 1)
            def branch_qk(x):
                if x == 1:
                    pe.wait_ge(ns["cmp"], 1)
                if x >= 2:
                    pe.wait_ge(nb["y"], x - 1)
                for t in range(2):
                    r = slice(t * HD2, (t + 1) * HD2)
                    c = t * 1024
                    mm(pair_bank(x)[:, c:c + 2 * S], nqt[r, x, P:S], nkt[r, x // 2].rearrange("p r s -> p (r s)"), start=True, stop=True)
                    mm(pair_bank(x)[:, c + 2 * S:c + 3 * S], nqt[r, x, 0:P], nkt[r, x // 2, :, 0:P], start=True, stop=True
                       ).then_inc(nb["logits"], 1)

            pe.wait_ge(ns["psb"], 1)
            branch_qk(0)
            pe.wait_ge(ns["pooled"], 1)
            for x in range(8):
                ins = mm(ps_a[:, x * S:(x + 1) * S], vbd[:, x // 4, 2 * (x % 4):2 * (x % 4) + 2].rearrange("p h d -> p (h d)"),
                         pct[:, :, x // 4], start=True, stop=True)
            ins.then_inc(ns["oc"], 1)
            for x in range(8):
                if x < 7:
                    branch_qk(x + 1)
                ps = pair_bank(x)
                pe.wait_ge(nb["diag"], x + 1)
                for r in range(2):
                    for t in range(2):
                        for b in range(SB):
                            for k in range(b + 1):
                                c = r * 512 + t * S + b * P if k == 0 else 1024 + r * 512 + t * P
                                ins = mm(ps[:, c:c + P], branch_prob(x, t, r, b)[:, k * P:(k + 1) * P],
                                         diag[:, x % 2, 4 * t + 2 * r + b], start=True, stop=True)
                    ins.then_inc(nb["pt"], 1)
                if x == 0:
                    pe.wait_ge(ns["vdup"], 1)
                o = ps[:, 0:512]
                for r in range(2):
                    pe.wait_ge(nb["pt_act"], 2 * x + r + 1)
                    pe.wait_ge(nb["pt_dve"], 2 * x + r + 1)
                    v0, v1 = (vdup[:, k, r, x // 2].rearrange("p x d -> p (x d)") for k in range(2))
                    mm(o, v0, probt[:, x % 2, r * 768:r * 768 + 512], start=r == 0, stop=False)
                    ins = mm(o.rearrange("p (t s) -> p t s", t=2)[:, :, P:S], v1,
                             probt[:, x % 2, r * 768 + 512:(r + 1) * 768].rearrange("p (t s) -> p t s", t=2),
                             start=False, stop=r == 1)
                ins.then_inc(nb["pv"], 1)

            pe.wait_ge(nb["lo"], 8)
            tile("br", 0, 2, 0)
            pe.wait_ge(nb["lo"], 9)
            def merged(j):
                pe.wait_ge(y1_done, j + 1)

            for t in range(1, 7):
                tile("br", t, 2, 8 * (t % 2))
            tile("br", 7, 2, 8, ahead=lambda: turn_group("y1", mix, merged, 0))
            enter("y1", "mixo", mix, merged, early=True)
            tile("mixo", 1)
            tile("mixo", 2, behind={2 * j + 1: (lambda j=j: turn_group("m2", mix, loaded(2), j)) for j in range(4)})
            tile("mixo", 3)

            def residual_rows(j):
                pe.wait_ge(post_done, 2 * (j + 1))

            pe.wait_ge(t_lo, sum(QUADS["m2"]))
            tile("xk", 0, x=(x2hi, x2lo), behind={4 + j: (lambda j=j: turn_group("n5", h, residual_rows, j)) for j in range(4)})
            c0, q0, t0 = seg["xq"]
            free(t0)
            for k in range(8):
                if k % 2 == 0:
                    pe.wait_ge(t_lo, QUADS["n5"][0] + k + 2)
                half(q0 + k, (2 * (t0 % 2), 2 * (t0 % 2) + 1), (2 * k, 2 * k + 1), k == 0, k == 7)

            def rows_turned():
                pe.wait_ge(evicted, seg["xv"][2])
                transposes_of(ps_b, qx, xkv)

            tile("xv", 0, x=(x2hi, x2lo), behind={1: rows_turned, 3: lambda: logits(ps_b, 2, False).then_inc(a_log, 1)})
            turn(ps_b, 2, False)
            pe.wait_ge(evicted, seg["xo"][2])
            weigh(ps_b, 2, lambda hh, k: xkv[:, k, 512 + hh * HD:512 + (hh + 1) * HD], False)
            enter("xo", "xo", mix, lambda j: pe.wait_ge(a_out, 2), halves=2)
            for t in range(1, 4):
                tile("xo", t, 1)
            enter("n6", "ffn", h, lambda j: pe.wait_ge(post_done, 8 + 2 * (j + 1)))

            c0, q0, _ = seg["ffn"]
            gbase, sbase, dbase = D_FF // NT, 2 * (D_FF // NT), 4 * (D_FF // NT)
            ng = D_FF2 // NT
            up_tile(q0 + 8, banks=(2, 3))
            pe.wait_ge(silu_done, sbase + 2)
            up_tile(q0 + 16, between=None)
            pe.wait_ge(u_row_done, gbase + 1)
            u_transposes(0, base_=gbase)
            up_tile(q0 + 24, banks=(2, 3))

            def ffn_downs(q, g, i=None):
                pe.wait_ge(u_lo, gbase + g + 1 + (0 if i is None else i))
                for t in range(4):
                    down_tile(q + 2 * t, t, dbase + 4 * g + t - 1, i, 24, banks=4)

            def ffn_group(g, i=None):
                more = 0 if i is None else i
                ffn_downs(q0 + 32 + 24 * g, g, i)
                pe.wait_ge(silu_done, sbase + 2 * g + 4 + more * 2)
                up_tile(q0 + 40 + 24 * g, i, 24)
                u_tr(g, i)
                up_tile(q0 + 48 + 24 * g, i, 24, banks=(2, 3))

            def u_tr(g, i=None):
                pe.wait_ge(d_add, dbase + 4 * g + 4 + (0 if i is None else i * 4))
                u_transposes(g + 1, i, gbase)

            ffn_group(0)
            with pe.Fori(1, ng - 2) as i:
                ffn_group(0, i)
            k0 = 32 + 24 * (ng - 2)
            ffn_downs(q0 + k0, ng - 2)
            u_tr(ng - 2)
            ffn_downs(q0 + k0 + 8, ng - 1)


_INS = ["x", "mem", "attn_norm_g", "w_in", "gla_a_w2", "gla_a_b", "fox_f_b", "fox_q_norm_g", "fox_k_norm_g", "mem_norm_g",
        "w_mem_kv", "mem_q_norm_g", "mem_k_norm_g", "out_norm_g", "w_out", "mlp_norm_g", "w_up", "w_down", "mem_2", "rel_bias_2",
        "ln_mix_pre_2", "ln_mix_post_2", "ln_x_pre_2", "ln_x_post_2", "ln_mem_2", "ln_ffn_pre_2", "ln_ffn_post_2", "w_in_2",
        "cmp_pe_2", "cmp_w1_2", "cmp_w2_2", "w_pool_2", "pool_scale_2", "w_br_attn_2", "w_br_pool_2", "w_mix_out_2", "w_xq_2",
        "w_xkv_2", "w_xo_2", "w_gate_2", "w_up_2", "w_down_2"]


def kernel(**inputs):
    import concourse.bacc as _bacc
    from concourse.bass_utils import run_bass_kernel_spmd as _run

    nc = _bacc.Bacc("TRN2", target_bir_lowering=False, num_devices=1, dynamic_dma_scratch_size=1024)
    arrays, args = {}, {}
    for name in _INS:
        v = np.ascontiguousarray(inputs[name])
        arrays[f"in_{name}"] = v
        args[name] = nc.dram_tensor(f"in_{name}", v.shape, mybir.dt.from_np(v.dtype), kind="ExternalInput").ap()
    consts = []
    for name, v in zip(("base", "bands", "hot"), shape_constants()):
        arrays[f"const_{name}"] = v
        consts.append(nc.dram_tensor(f"const_{name}", v.shape, F32, kind="ExternalInput").ap())
    out = nc.dram_tensor("out", (1, S, D), F32, kind="ExternalOutput").ap()
    hybrid_blocks_kernel(nc, args, *consts, out)
    r = _run(nc, [arrays], core_ids=[0])
    return r.results[0]["out"]
```
